# Optimizing a Trainium2 kernel written in Bass

```python
import jax
import jax.numpy as jnp
from jax import lax
import numpy as np

D_MODEL = 1024
BATCH = 1
SEQ = 256
DEPTH = 2

HEAD_DIM = 64
ROPE_DIM = HEAD_DIM // 4
ROPE_THETA = 500000.0
NORM_EPS = 1e-6
NEG_INF = -1e30
FORCE_SCORE = 1e6

NSA_HEADS = 8
NSA_KV_GROUPS = 2
NSA_HPG = NSA_HEADS // NSA_KV_GROUPS
CMP_LEN = 32
CMP_STRIDE = 16
SLC_BLOCK = 64
SLC_TOPK = 16
WINDOW = 512

FOX_HEADS = 8

Q_BLOCK = 128
SLC_SUB = 32

NSA_Q = NSA_HEADS * HEAD_DIM
NSA_KV = NSA_KV_GROUPS * HEAD_DIM
NSA_GATES = 3 * NSA_HEADS
FOX_W = FOX_HEADS * HEAD_DIM
A_SPLITS = (NSA_Q, NSA_KV, NSA_KV, NSA_KV, NSA_KV, NSA_KV, NSA_KV, NSA_GATES, FOX_W, FOX_W, FOX_W, FOX_HEADS)
IN_A_WIDTH = sum(A_SPLITS)
MIX_A_WIDTH = NSA_Q + FOX_W

GLA_HEADS = 4
GLA_DK = D_MODEL // 2
GLA_DV = D_MODEL
GLA_DK_HEAD = GLA_DK // GLA_HEADS
GLA_DV_HEAD = GLA_DV // GLA_HEADS
GLA_RANK = 16
GLA_TAU = 16.0
GLA_CHUNK = 64
C_SPLITS = (GLA_DK, GLA_DK, GLA_DV, GLA_DV, GLA_RANK)
IN_C_WIDTH = sum(C_SPLITS)

D_FF = ((8 * D_MODEL // 3 + 127) // 128) * 128
N_EXPERTS = 8
TOP_K = 2

N_EVEN = (DEPTH + 1) // 2
N_ODD = DEPTH // 2

kernel_name = 'hybrid_nsa_fox_gla_moe_block'

def _split(t, sizes):
    return jnp.split(t, np.cumsum(sizes)[:-1].tolist(), axis=-1)

def rmsnorm(x, g):
    xf = x.astype(jnp.float32)
    y = xf * lax.rsqrt(jnp.mean(xf * xf, axis=-1, keepdims=True) + NORM_EPS)
    return (y * g.astype(jnp.float32)).astype(x.dtype)

def rope_tables(pos):
    inv = ROPE_THETA ** (-jnp.arange(0, ROPE_DIM, 2, dtype=jnp.float32) / ROPE_DIM)
    ang = pos.astype(jnp.float32)[:, None] * inv[None, :]
    return jnp.cos(ang), jnp.sin(ang)

def partial_rope(x, cos, sin):
    r = x[..., :ROPE_DIM].astype(jnp.float32)
    half = ROPE_DIM // 2
    x1, x2 = r[..., :half], r[..., half:]
    c, s = cos[None, :, None, :], sin[None, :, None, :]
    rot = jnp.concatenate([x1 * c - x2 * s, x1 * s + x2 * c], axis=-1).astype(x.dtype)
    return jnp.concatenate([rot, x[..., ROPE_DIM:]], axis=-1)

def masked_softmax(s, mask):
    s = jnp.where(mask, s.astype(jnp.float32), NEG_INF)
    p = jax.nn.softmax(s, axis=-1)
    return jnp.where(mask, p, 0.0)

def swiglu(x, w_gate, w_up, w_down):
    return (jax.nn.silu(x @ w_gate) * (x @ w_up)) @ w_down

def nsa_fox_mixer(h, w_in, nsa_q_norm, nsa_k_norm, pe_k, pe_v, ck1, ck2, cv1, cv2,
                  gate_bias, fox_q_norm, fox_k_norm, fox_f_bias, w_out):
    B, S, _ = h.shape
    G, R, dh = NSA_KV_GROUPS, NSA_HPG, HEAD_DIM
    n_blk = S // Q_BLOCK
    scale = dh ** -0.5
    proj = h @ w_in
    qa, kc, vc, ksl, vsl, kwn, vwn, ga, qb, kb, vb, fb = _split(proj, A_SPLITS)

    def heads(t, n):
        return t.reshape(B, S, n, dh)

    pos = jnp.arange(S)
    cos, sin = rope_tables(pos)

    qa = partial_rope(rmsnorm(heads(qa, NSA_HEADS), nsa_q_norm), cos, sin)
    ksl = partial_rope(rmsnorm(heads(ksl, G), nsa_k_norm), cos, sin)
    kwn = partial_rope(rmsnorm(heads(kwn, G), nsa_k_norm), cos, sin)
    vsl, vwn = heads(vsl, G), heads(vwn, G)

    n_cmp = (S - CMP_LEN) // CMP_STRIDE + 1
    cmp_idx = jnp.arange(n_cmp)[:, None] * CMP_STRIDE + jnp.arange(CMP_LEN)[None, :]

    def compress(tok, pe, w1, w2):
        blk = heads(tok, G)[:, cmp_idx] + pe[None, None, :, None, :]
        blk = blk.transpose(0, 1, 3, 2, 4).reshape(B, n_cmp, G, CMP_LEN * dh)
        return jax.nn.gelu(blk @ w1) @ w2

    cmp_end = jnp.arange(n_cmp) * CMP_STRIDE + CMP_LEN - 1
    ccos, csin = rope_tables(cmp_end)
    k_cmp = partial_rope(rmsnorm(compress(kc, pe_k, ck1, ck2), nsa_k_norm), ccos, csin)
    v_cmp = compress(vc, pe_v, cv1, cv2)

    n_slc = S // SLC_BLOCK
    k_sel = min(SLC_TOPK, n_slc)
    c_start = jnp.arange(n_cmp) * CMP_STRIDE
    s_start = jnp.arange(n_slc) * SLC_BLOCK
    overlap = jnp.maximum(
        jnp.minimum(c_start[:, None] + CMP_LEN, s_start[None, :] + SLC_BLOCK)
        - jnp.maximum(c_start[:, None], s_start[None, :]), 0).astype(jnp.float32) / CMP_LEN

    ks_blocks = ksl.reshape(B, n_slc, SLC_BLOCK, G, dh).transpose(0, 3, 1, 2, 4)
    vs_blocks = vsl.reshape(B, n_slc, SLC_BLOCK, G, dh).transpose(0, 3, 1, 2, 4)
    gather_blocks = jax.vmap(jax.vmap(lambda kbk, ix: kbk[ix]))

    k_pad = jnp.pad(kwn, ((0, 0), (WINDOW, 0), (0, 0), (0, 0)))
    v_pad = jnp.pad(vwn, ((0, 0), (WINDOW, 0), (0, 0), (0, 0)))
    blk_ids = jnp.arange(n_slc)

    def nsa_block(i):
        q0 = i * Q_BLOCK
        qg = lax.dynamic_slice_in_dim(qa, q0, Q_BLOCK, axis=1).reshape(B, Q_BLOCK, G, R, dh)
        tq = q0 + jnp.arange(Q_BLOCK)
        s_c = jnp.einsum('bqgrd,bngd->bgrqn', qg, k_cmp) * scale
        p_c = masked_softmax(s_c, cmp_end[None, :] <= tq[:, None])
        o_c = jnp.einsum('bgrqn,bngd->bqgrd', p_c.astype(v_cmp.dtype), v_cmp)
        imp = jnp.einsum('bgrqn,ns->bgqs', p_c, overlap)
        cur = tq // SLC_BLOCK
        forced = (blk_ids[None, :] == 0) | (blk_ids[None, :] == cur[:, None]) | (blk_ids[None, :] == cur[:, None] - 1)
        future = blk_ids[None, :] > cur[:, None]
        imp = jnp.where(forced, FORCE_SCORE, jnp.where(future, -FORCE_SCORE, imp))
        _, sel = lax.top_k(imp, k_sel)

        def slc_sub(j):
            qs = lax.dynamic_slice_in_dim(qg, j * SLC_SUB, SLC_SUB, axis=1)
            idx = lax.dynamic_slice_in_dim(sel, j * SLC_SUB, SLC_SUB, axis=2)
            ts = lax.dynamic_slice_in_dim(tq, j * SLC_SUB, SLC_SUB)
            kg = gather_blocks(ks_blocks, idx).reshape(B, G, SLC_SUB, k_sel * SLC_BLOCK, dh)
            vg = gather_blocks(vs_blocks, idx).reshape(B, G, SLC_SUB, k_sel * SLC_BLOCK, dh)
            kpos = (idx[..., None] * SLC_BLOCK + jnp.arange(SLC_BLOCK)).reshape(B, G, SLC_SUB, k_sel * SLC_BLOCK)
            m = kpos <= ts[None, None, :, None]
            s_s = jnp.einsum('bqgrd,bgqkd->bgrqk', qs, kg) * scale
            p_s = masked_softmax(s_s, m[:, :, None])
            return jnp.einsum('bgrqk,bgqkd->bqgrd', p_s.astype(vg.dtype), vg)

        o_s = lax.map(slc_sub, jnp.arange(Q_BLOCK // SLC_SUB))
        o_s = o_s.transpose(1, 0, 2, 3, 4, 5).reshape(B, Q_BLOCK, G, R, dh)

        kw = lax.dynamic_slice_in_dim(k_pad, q0, WINDOW + Q_BLOCK, axis=1)
        vw = lax.dynamic_slice_in_dim(v_pad, q0, WINDOW + Q_BLOCK, axis=1)
        kpos_w = q0 - WINDOW + jnp.arange(WINDOW + Q_BLOCK)
        dist = tq[:, None] - kpos_w[None, :]
        m_w = (dist >= 0) & (dist < WINDOW) & (kpos_w[None, :] >= 0)
        s_w = jnp.einsum('bqgrd,bkgd->bgrqk', qg, kw) * scale
        p_w = masked_softmax(s_w, m_w)
        o_w = jnp.einsum('bgrqk,bkgd->bqgrd', p_w.astype(vw.dtype), vw)
        return o_c, o_s, o_w

    o_c, o_s, o_w = lax.map(nsa_block, jnp.arange(n_blk))

    def unblock_a(o):
        return o.transpose(1, 0, 2, 3, 4, 5).reshape(B, S, NSA_HEADS, dh)

    gates = jax.nn.sigmoid((ga + gate_bias).astype(jnp.float32)).reshape(B, S, NSA_HEADS, 3)
    o_a = (gates[..., 0:1] * unblock_a(o_c) + gates[..., 1:2] * unblock_a(o_s)
           + gates[..., 2:3] * unblock_a(o_w)).astype(h.dtype).reshape(B, S, NSA_Q)

    qb = rmsnorm(heads(qb, FOX_HEADS), fox_q_norm)
    kb = rmsnorm(heads(kb, FOX_HEADS), fox_k_norm)
    vb = heads(vb, FOX_HEADS)
    log_f = jax.nn.log_sigmoid(fb.astype(jnp.float32) + fox_f_bias.astype(jnp.float32))
    cum_t = jnp.cumsum(log_f, axis=1).transpose(0, 2, 1)

    def fox_block(i):
        q0 = i * Q_BLOCK
        q = lax.dynamic_slice_in_dim(qb, q0, Q_BLOCK, axis=1)
        cq = lax.dynamic_slice_in_dim(cum_t, q0, Q_BLOCK, axis=2)
        tq = q0 + jnp.arange(Q_BLOCK)
        s_f = (jnp.einsum('bqhd,bkhd->bhqk', q, kb).astype(jnp.float32) * scale
               + cq[..., None] - cum_t[:, :, None, :])
        p_f = masked_softmax(s_f, pos[None, :] <= tq[:, None])
        return jnp.einsum('bhqk,bkhd->bqhd', p_f.astype(vb.dtype), vb)

    o_b = lax.map(fox_block, jnp.arange(n_blk)).transpose(1, 0, 2, 3, 4).reshape(B, S, FOX_W)

    return jnp.concatenate([o_a, o_b], axis=-1) @ w_out

def gla_mixer(h, w_in, w_a2, b_a, o_norm, w_out):
    B, S, _ = h.shape
    H, dk, dv, C = GLA_HEADS, GLA_DK_HEAD, GLA_DV_HEAD, GLA_CHUNK
    n_ch = S // C
    q, k, v, r, a1 = _split(h @ w_in, C_SPLITS)
    q = q.reshape(B, S, H, dk) * (dk ** -0.5)
    k = k.reshape(B, S, H, dk)
    v = v.reshape(B, S, H, dv)
    log_a = (jax.nn.log_sigmoid((a1 @ w_a2 + b_a).astype(jnp.float32)) / GLA_TAU).reshape(B, S, H, dk)

    def chunks(t):
        return t.astype(jnp.float32).reshape(B, n_ch, C, H, t.shape[-1]).transpose(1, 0, 3, 2, 4)

    causal = jnp.tril(jnp.ones((C, C), dtype=bool))[None, None, :, :, None]

    def step(state, inp):
        qc, kc, vc, gc = inp
        b = jnp.cumsum(gc, axis=2)
        o_inter = jnp.einsum('bhcd,bhde->bhce', qc * jnp.exp(b), state)
        dlt = b[:, :, :, None, :] - b[:, :, None, :, :]
        decay = jnp.where(causal, jnp.exp(jnp.where(causal, dlt, 0.0)), 0.0)
        att = jnp.einsum('bhid,bhjd,bhijd->bhij', qc, kc, decay)
        o_intra = jnp.einsum('bhij,bhje->bhie', att, vc)
        b_last = b[:, :, -1:, :]
        state = (jnp.exp(b_last[:, :, 0, :, None]) * state
                 + jnp.einsum('bhcd,bhce->bhde', kc * jnp.exp(b_last - b), vc))
        return state, o_inter + o_intra

    state0 = jnp.zeros((B, H, dk, dv), jnp.float32)
    _, o = lax.scan(step, state0, (chunks(q), chunks(k), chunks(v), chunks(log_a)))
    o = o.transpose(1, 0, 3, 2, 4).reshape(B, S, H, dv)
    o = rmsnorm(o, o_norm).astype(h.dtype).reshape(B, S, GLA_DV) * jax.nn.silu(r)
    return o @ w_out

def moe_ffn(h, router, w_gate, w_up, w_down):
    B, S, D = h.shape
    xt = h.reshape(B * S, D)
    logits = (xt @ router).astype(jnp.float32)
    top_v, top_i = lax.top_k(logits, TOP_K)
    top_w = jax.nn.softmax(top_v, axis=-1)
    gates = jnp.sum(jax.nn.one_hot(top_i, N_EXPERTS, dtype=jnp.float32) * top_w[..., None], axis=1)
    out = jnp.zeros((B * S, D), jnp.float32)
    for e in range(N_EXPERTS):
        out = out + gates[:, e:e + 1] * swiglu(xt, w_gate[e], w_up[e], w_down[e]).astype(jnp.float32)
    return out.astype(h.dtype).reshape(B, S, D)

def setup_inputs(seed: int = 0) -> dict:
    key = jax.random.key(seed)
    keys = iter(jax.random.split(key, 40))

    def w(shape, fan_in):
        return jax.random.normal(next(keys), shape, jnp.float32) * (fan_in ** -0.5)

    def gain(shape):
        return 1.0 + 0.05 * jax.random.normal(next(keys), shape, jnp.float32)

    def small(shape, s=0.02):
        return s * jax.random.normal(next(keys), shape, jnp.float32)

    NE, NO = N_EVEN, N_ODD
    return {
        'x': jax.random.normal(next(keys), (BATCH, SEQ, D_MODEL), jnp.float32),
        'a_norm': gain((NE, D_MODEL)),
        'a_w_in': w((NE, D_MODEL, IN_A_WIDTH), D_MODEL),
        'a_q_norm': gain((NE, HEAD_DIM)),
        'a_k_norm': gain((NE, HEAD_DIM)),
        'a_pe_k': small((NE, CMP_LEN, HEAD_DIM), 0.1),
        'a_pe_v': small((NE, CMP_LEN, HEAD_DIM), 0.1),
        'a_cmp_k_w1': w((NE, CMP_LEN * HEAD_DIM, HEAD_DIM), CMP_LEN * HEAD_DIM),
        'a_cmp_k_w2': w((NE, HEAD_DIM, HEAD_DIM), HEAD_DIM),
        'a_cmp_v_w1': w((NE, CMP_LEN * HEAD_DIM, HEAD_DIM), CMP_LEN * HEAD_DIM),
        'a_cmp_v_w2': w((NE, HEAD_DIM, HEAD_DIM), HEAD_DIM),
        'a_gate_bias': small((NE, NSA_GATES), 0.1),
        'a_fox_q_norm': gain((NE, HEAD_DIM)),
        'a_fox_k_norm': gain((NE, HEAD_DIM)),
        'a_fox_f_bias': 2.0 + small((NE, FOX_HEADS), 0.5),
        'a_w_out': w((NE, MIX_A_WIDTH, D_MODEL), MIX_A_WIDTH),
        'f_norm': gain((NE, D_MODEL)),
        'f_w_gate': w((NE, D_MODEL, D_FF), D_MODEL),
        'f_w_up': w((NE, D_MODEL, D_FF), D_MODEL),
        'f_w_down': w((NE, D_FF, D_MODEL), D_FF),
        'c_norm': gain((NO, D_MODEL)),
        'c_w_in': w((NO, D_MODEL, IN_C_WIDTH), D_MODEL),
        'c_w_a2': w((NO, GLA_RANK, GLA_DK), GLA_RANK),
        'c_b_a': small((NO, GLA_DK), 0.1),
        'c_o_norm': gain((NO, GLA_DV_HEAD)),
        'c_w_out': w((NO, GLA_DV, D_MODEL), GLA_DV),
        'm_norm': gain((NO, D_MODEL)),
        'm_router': w((NO, D_MODEL, N_EXPERTS), D_MODEL),
        'm_w_gate': w((NO, N_EXPERTS, D_MODEL, D_FF), D_MODEL),
        'm_w_up': w((NO, N_EXPERTS, D_MODEL, D_FF), D_MODEL),
        'm_w_down': w((NO, N_EXPERTS, D_FF, D_MODEL), D_FF),
    }

def reference(x, a_norm, a_w_in, a_q_norm, a_k_norm, a_pe_k, a_pe_v, a_cmp_k_w1, a_cmp_k_w2,
              a_cmp_v_w1, a_cmp_v_w2, a_gate_bias, a_fox_q_norm, a_fox_k_norm, a_fox_f_bias, a_w_out,
              f_norm, f_w_gate, f_w_up, f_w_down,
              c_norm, c_w_in, c_w_a2, c_b_a, c_o_norm, c_w_out,
              m_norm, m_router, m_w_gate, m_w_up, m_w_down):
    for layer in range(DEPTH):
        i = layer // 2
        if layer % 2 == 0:
            x = x + nsa_fox_mixer(rmsnorm(x, a_norm[i]), a_w_in[i], a_q_norm[i], a_k_norm[i],
                                  a_pe_k[i], a_pe_v[i], a_cmp_k_w1[i], a_cmp_k_w2[i],
                                  a_cmp_v_w1[i], a_cmp_v_w2[i], a_gate_bias[i],
                                  a_fox_q_norm[i], a_fox_k_norm[i], a_fox_f_bias[i], a_w_out[i])
            x = x + swiglu(rmsnorm(x, f_norm[i]), f_w_gate[i], f_w_up[i], f_w_down[i])
        else:
            x = x + gla_mixer(rmsnorm(x, c_norm[i]), c_w_in[i], c_w_a2[i], c_b_a[i], c_o_norm[i], c_w_out[i])
            x = x + moe_ffn(rmsnorm(x, m_norm[i]), m_router[i], m_w_gate[i], m_w_up[i], m_w_down[i])
    return x


_drawn_inputs = setup_inputs


def setup_inputs(seed=0):
    import zlib

    import numpy as np

    out = dict(_drawn_inputs(seed))
    spreads = {}
    factors = {}
    for name, (base, spread) in spreads.items():
        noise = np.random.default_rng([zlib.crc32(name.encode()), seed]).standard_normal(out[name].shape)
        drawn = base * np.exp(spread * noise) if base else spread * noise
        out[name] = jnp.asarray(drawn.astype(out[name].dtype))
    for name, factor in factors.items():
        out[name] = (out[name] * factor).astype(out[name].dtype)
    return out
```

```python
from contextlib import ExitStack

import concourse.bass as bass
import numpy as np
from concourse import mybir

F32 = mybir.dt.float32
BF16 = mybir.dt.bfloat16
I32 = mybir.dt.int32
U32 = mybir.dt.uint32
ALU = mybir.AluOpType
ACT = mybir.ActivationFunctionType
AX = mybir.AxisListType

P = 128
SEQ, DM = 256, 1024
NT = SEQ // P
NK = DM // P
HD = 64
NH = 8
NG = 2
NCMP = 15
EPS = 1e-6
NEG = -1e30
DFF = 2816
CH = 256
NCH = DFF // CH
BLK = 512
UB = 4
RING = 11
NE = 8
CAP = 128
OVER_ROUNDS = 3
GH = 4
GB = 8
NGB = P // GB

A_IN_CG, C_IN_CG = 6, 6
U_A_IN = 0
U_A_OUT = U_A_IN + A_IN_CG * NK // UB
U_FFN = U_A_OUT + 2 * NK // UB
CHUNK_UNITS = (NK + 4) // UB
U_C_IN = U_FFN + NCH * CHUNK_UNITS
U_C_OUT = U_C_IN + C_IN_CG * NK // UB
U_MOE = U_C_OUT + 2 * NK // UB
EXP_UNITS = NCH * CHUNK_UNITS
U_END = U_MOE + NE * EXP_UNITS
FRONT_WIDTH = {1: 288}

C_ID, C_TRI, C_ONES, C_IOTA, C_BD = 0, 128, 256, 384, 512
C_SEL = 640
C_ROPE = C_SEL + GB + P
C_CROPE = C_ROPE + NT * 32
C_CBIAS = C_CROPE + 32
C_CMASK = C_CBIAS + NT * 16
C_HMASK = C_CMASK + NT * 16
C_REP = C_HMASK + 8
C_END = C_REP + 2 * P
R_QN, R_KN, R_FQ, R_FK, R_ON, R_GB, R_FB = 0, 64, 128, 192, 256, 512, 536
R_NORM = 544
R_BA = R_NORM + 4 * NK
R_ROUTER = R_BA + GH
R_A1 = R_ROUTER + NK * NE
R_PE = R_A1 + NK * 16
R_END = R_PE + 2 * 16


def constants():
    c = np.zeros((P, C_END), np.float32)
    i = np.arange(P)
    c[:, C_ID:C_ID + P] = np.eye(P)
    c[:, C_TRI:C_TRI + P] = i[:, None] <= i[None, :]
    c[:, C_ONES:C_ONES + P] = 1.0
    c[:, C_IOTA:C_IOTA + P] = i[None, :]
    c[:, C_BD:C_BD + P] = (i[:, None] <= i[None, :]) & (i[:, None] // GB == i[None, :] // GB)
    c[:, C_SEL:C_SEL + GB + P] = np.arange(GB + P)[None, :] % GB == 0
    inv = np.float32(500000.0) ** (-np.arange(0, 16, 2, dtype=np.float32) / np.float32(16))

    def rope(pos):
        ang = pos.astype(np.float32)[:, None] * inv[None, :].astype(np.float32)
        co, si = np.cos(ang), np.sin(ang)
        return np.concatenate([co, co, -si, si], axis=1).astype(np.float32)

    for t in range(NT):
        c[:, C_ROPE + 32 * t:C_ROPE + 32 * (t + 1)] = rope(t * P + i)
    ends = np.arange(NCMP) * 16 + 31
    c[0:NCMP, C_CROPE:C_CROPE + 32] = rope(ends)
    c[NCMP:2 * NCMP, C_CROPE:C_CROPE + 32] = rope(ends)
    for t in range(NT):
        seen = (ends[None, :] <= (t * P + i)[:, None])
        c[:, C_CBIAS + 16 * t:C_CBIAS + 16 * t + NCMP] = np.where(seen, 0.0, NEG)
        c[:, C_CMASK + 16 * t:C_CMASK + 16 * t + NCMP] = seen
    c[:, C_HMASK:C_HMASK + 8] = i[:, None] // 16 == np.arange(8)[None, :]
    for g in range(NG):
        rep = (i[:, None] == i[None, :] % 16) & (i[None, :] // 64 == g) & (i[:, None] < NCMP)
        c[:, C_REP + g * P:C_REP + (g + 1) * P] = rep
    return c


def masks():
    i = np.arange(P)
    m = np.zeros((P, 1024 + P), np.float32)
    late = np.where(i[:, None] >= i[None, :], 0.0, NEG)
    for h in range(4):
        m[:, h * P:(h + 1) * P] = late
    m[:, 512 + 128:512 + 256] = late
    m[:, 512 + 384:512 + 512] = late
    m[:, 1024:1024 + P] = np.eye(P)
    return (m.view(np.uint32) >> 16).astype(np.uint16)


def trunk(nc, x_d, w_d, const_d, mask_d, small_d, comp_d, wa2_d, out_d, stop=99):
    ctx = ExitStack()
    with ctx:
        def sb(name, shape, dt=F32):
            return ctx.enter_context(nc.sbuf_tensor(name, shape, dt))

        def sem(name):
            return ctx.enter_context(nc.semaphore(name))

        ring = sb("ring", [P, RING, UB, BLK])
        x = sb("x", [P, NT, DM])
        hn = sb("hn", [P, NT, DM])
        hT = sb("hT", [P, NK, SEQ])
        cst = sb("cst", [P, C_END])
        msk_bits = sb("msk_bits", [P, 1024 + P], mybir.dt.uint16)
        msk = msk_bits[:, :].bitcast(BF16)
        sml = sb("sml", [P, R_END])
        wa2 = sb("wa2", [16, 512])
        ss = sb("ss", [P, NT])
        rstd = sb("rstd", [P, NT])
        mhalf = sb("mhalf", [P, 32])
        arena = sb("arena", [P, ARENA])
        esc = sb("esc", [P, 2, 512])

        class Carve:
            def __init__(self):
                self.at = 0

            def __call__(self, n, dt=F32):
                a = arena[:, self.at:self.at + n]
                self.at += n
                assert self.at <= ARENA, self.at
                return a

        ident = cst[:, C_ID:C_ID + P]
        tri = cst[:, C_TRI:C_TRI + P]
        ones = cst[:, C_ONES:C_ONES + P]
        iota = cst[:, C_IOTA:C_IOTA + P]
        mbd = cst[:, C_BD:C_BD + P]
        mident = msk[:, 1024:1024 + P]

        bank = [ctx.enter_context(nc.psum_tensor(f"bank{i}", [P, 512], F32)) for i in range(8)]

        c0 = Carve()
        front = c0(A_IN_CG * NT * BLK)
        proj4 = front.rearrange("p (c t n) -> p c t n", c=A_IN_CG, t=NT)
        proj = [proj4[:, i, :, :] for i in (5, 0, 2, 3, 4, 1)]
        qT = hT[:, :, :]
        keyT = c0(4 * SEQ).rearrange("p (h n) -> p h n", h=4)
        fqT = front[:, 2048:4096].rearrange("p (h n) -> p h n", h=NH)
        fkT = front[:, 4096:6144].rearrange("p (h n) -> p h n", h=NH)
        scr0 = c0.at
        cw1 = c0(2 * 16 * HD).rearrange("p (v j d) -> p v j d", v=2, j=16)
        cw2 = c0(2 * HD).rearrange("p (v d) -> p v d", v=2)
        kc2 = esc[:, :, :].rearrange("p b n -> p (b n)").rearrange("p (v g n) -> p v g n", v=2, g=NG)
        blkT = c0(2 * 16 * 30).rearrange("p (v j g n) -> p v j g n", v=2, j=16, g=NG)
        assert c0.at - scr0 >= 2560
        pbuf = arena[:, scr0:scr0 + 1024].rearrange("p (b n) -> p b n", b=2)
        ptb = arena[:, scr0 + 1024:scr0 + 2048].rearrange("p (b n) -> p b n", b=2)
        tmpo = arena[:, scr0 + 2048:scr0 + 2560]
        sq = hn[:, :, :].rearrange("p t n -> p (t n)")
        faug = arena[:, scr0:scr0 + 2 * NT * NH * 66].rearrange("p (w t h n) -> p w t h n", w=2, t=NT, h=NH)
        hss = c0(6 * 32).rearrange("p (w n) -> p w n", w=6)
        hrs = c0(6 * 32).rearrange("p (w n) -> p w n", w=6)
        rA = c0(256)
        rB = c0(256)
        gel = c0(4 * 64).rearrange("p (w n) -> p w n", w=4)
        kcm = c0(4 * 64).rearrange("p (w n) -> p w n", w=4)
        kcmpT = c0(32)
        vcmp = c0(2 * 64).rearrange("p (g d) -> p g d", g=2)
        vbd = c0(512)
        fz = c0(5 * 16).rearrange("p (w n) -> p w n", w=5)
        gat = c0(48)
        sc = c0(2 * 128).rearrange("p (t n) -> p t n", t=2)
        mc = c0(16)
        sumc = c0(16)
        facc = c0(16)
        pcT = c0(256).rearrange("p (t n) -> p t n", t=2)
        negm = c0(6 * 8).rearrange("p (s h) -> p s h", s=6)
        sums = c0(6 * 8).rearrange("p (s h) -> p s h", s=6)
        fac = c0(6 * 8).rearrange("p (s h) -> p s h", s=6)
        oacc = hn

        cf = Carve()
        sg = cf(2 * CH).rearrange("p (b n) -> p b n", b=2)
        hact = cf(2 * CH).rearrange("p (b n) -> p b n", b=2)
        h2T = cf(2 * CH).rearrange("p (b n) -> p b n", b=2)
        xgT = cf(DM).rearrange("p (k n) -> p k n", k=NK)
        ysb = cf(DM)
        disp = cf(2 * P).rearrange("p (t n) -> p t n", t=2)
        dispg = cf(2 * P).rearrange("p (t n) -> p t n", t=2)
        combT = cf(2 * P).rearrange("p (t n) -> p t n", t=2)
        lg = cf(16).rearrange("p (t n) -> p t n", t=2)
        mx = cf(16).rearrange("p (t n) -> p t n", t=2)
        mxi = sb("mxi", [P, 2, 8], U32)
        idf = cf(16).rearrange("p (t n) -> p t n", t=2)
        ee = cf(2)
        w12 = cf(4).rearrange("p (t n) -> p t n", t=2)
        oh = cf(2 * 16).rearrange("p (w t n) -> p w t n", w=2, t=2)
        gate = cf(24).rearrange("p (t n) -> p t n", t=2)
        slot = cf(24).rearrange("p (t n) -> p t n", t=2)
        picked = cf(16).rearrange("p (t n) -> p t n", t=2)
        cur = cf(4).rearrange("p (w t) -> p w t", w=2)
        over = cf(8 * 8).rearrange("p (w n) -> p w n", w=8)
        ovt = cf(16).rearrange("p (t n) -> p t n", t=2)
        ovf = cf(4)
        ovi = sb("ovi", [1, 4], I32)

        cg_ = Carve()
        gq = cg_(NT * 512).rearrange("p (t n) -> p t n", t=NT)
        gk = cg_(NT * 512).rearrange("p (t n) -> p t n", t=NT)
        gb = cg_(NT * 512).rearrange("p (t n) -> p t n", t=NT)
        gv = cg_(NT * DM).rearrange("p (t n) -> p t n", t=NT)
        prod = cg_(GB * 512).rearrange("p (s n) -> p s n", s=GB)
        kt = cg_((NGB - 1) * 512).rearrange("p (i n) -> p i n", i=NGB - 1)
        gr = kt[:, 0:4, :].rearrange("p i n -> p (i n)").rearrange("p (t n) -> p t n", t=NT)
        gqt = cg_(512)
        att = prod[:, 0:2, :]
        kbar, qbar, far = prod[:, 2, :], prod[:, 3, :], prod[:, 4, :]
        a1T = cg_(SEQ)
        gz = prod[:, 0:2, :].rearrange("p s n -> p (s n)")
        ge = prod[:, 2:4, :].rearrange("p s n -> p (s n)")
        rmask = prod[:, 4:6, :].rearrange("p s n -> p (s n)")
        oss = sb("oss", [P, NT * GH])
        ors = sb("ors", [P, NT * GH])

        NAMES = """x_in const_in late_in units_used x_ready ss rstd hn hT_psum hT dve_chain act_chain pool_chain
            proj kc_psum kc blk hid hid_in tanh gelu cmp2 cmp2_sb kcmp_ss kcmp_rstd kcmp kcmpT_psum kcmpT
            vrep vbd head_ss head_rstd head_done gate_z gate_e fox_z fox_l fox_lf cum aug
            headT_psum headT foxT_psum foxT cmp_s cmp_d cmp_e cmp_p cmp_pT_psum cmp_pT cmp_o
            scores rowmax probs probsT_psum probsT pv o_done
            gu silu hact h2T_psum h2T
            a1 a1_sb z zb absz soft decay gla_qk gla_vr prod_zero kt_zero diag_arg diag_exp prod diag
            k_arg k_exp kt q_arg q_exp qt cross att far_arg far_exp far_ops far_psum far_sb
            gla_o gla_ss gla_rstd mixed
            logits top gap gap_exp picked rank route disp dispg combT_psum combT xg_psum xg
            cur m_silu m_hact m_h2T_psum m_h2T ysb scat out""".split()
        S = {n: sem(n) for n in NAMES}
        s_loaded = [sem(f"loaded{i}") for i in range(RING)]

        def loaded(eng, u):
            eng.wait_ge(s_loaded[u % RING], 16 * (u // RING + 1))

        att_units = []
        for br in range(3):
            for t in range(NT):
                n = 4 if t == 0 else 2
                att_units += [(br, t, h0, n) for h0 in range(0, NH, n)]
        AU = len(att_units)

        def seq_of(u):
            return att_units[u][0] * NT + att_units[u][1]

        ends_seq = [u for u in range(AU) if u == AU - 1 or seq_of(u + 1) != seq_of(u)]
        steps = [(c, t) for c in range(NCH) for t in range(NT)]
        X_MOE = 12

        def pos_g(c, half):
            return half if c == 0 else 3 * c - 1 + half

        def pos_d(c):
            return 4 + 3 * c if c < NCH - 1 else EXP_UNITS - 1

        block = ctx.enter_context(nc.Block())

        @block.sync
        def _(sp):
            def fetch(u, slot_):
                sp.dma_start(ring[:, slot_, :, :], w_d[u, :, :].rearrange("p (b n) -> p b n", b=UB))\
                  .then_inc(s_loaded[slot_], 16)

            sp.dma_start(x[:, :, :], x_d.rearrange("(t p) n -> p t n", p=P)).then_inc(S["x_in"], 16)
            for dst, src in ((cst[:, :], const_d[:, :]), (sml[:, :], small_d[:, :])):
                sp.dma_start(dst, src).then_inc(S["const_in"], 16)
            fetch(0, 0)
            fetch(1, 1)
            for dst, src in ((arena[:, scr0:scr0 + 2176], comp_d[:, :]), (msk_bits[:, :], mask_d[:, :]),
                             (wa2[:, :], wa2_d[:, :])):
                sp.dma_start(dst, src).then_inc(S["late_in"], 16)
            for u in range(2, RING):
                fetch(u, u)
            limit = LIMITS[stop]
            full = limit // RING
            if stop < 5:
                full = 1
            else:
                with sp.Fori(1, full) as it:
                    for s_ in range(RING):
                        sp.wait_ge(S["units_used"], (it - 1) * RING + s_ + 1)
                        sp.dma_start(ring[:, s_, :, :],
                                     w_d[bass.ds(it * RING + s_, 1), :, :].rearrange("a p (b n) -> p (a b) n", b=UB))\
                          .then_inc(s_loaded[s_], 16)
            for u in range(full * RING, limit):
                sp.wait_ge(S["units_used"], u - RING + 1)
                fetch(u, u % RING)
            if stop < 5:
                sp.wait_ge(S["x_ready"], 4 * (stop - 1))
            else:
                sp.wait_ge(S["route"], 1)
                n_over = sp.value_load(ovi[0:1, 0:1], min_val=0, max_val=OVER_ROUNDS)
                with sp.Fori(0, OVER_ROUNDS) as r:
                    with sp.If(n_over > r):
                        who = sp.value_load(ovi[0:1, bass.ds(r + 1, 1)], min_val=0, max_val=NE - 1)
                        for i in range(EXP_UNITS):
                            sp.wait_ge(S["units_used"], r * EXP_UNITS + (U_END + i - RING + 1))
                            sl = (U_END + i) % RING
                            sp.dma_start(ring[:, sl, :, :],
                                         w_d[bass.ds(who * EXP_UNITS + (U_MOE + i), 1), :, :]
                                         .rearrange("a p (b n) -> p (a b) n", b=UB)).then_inc(s_loaded[sl], 16)
                sp.wait_ge(S["x_ready"], n_over * 4 + (X_MOE + 4 * NE))
            sp.dma_start(out_d.rearrange("(t p) n -> p t n", p=P), x[:, :, :]).then_inc(S["out"], 16)
            sp.wait_ge(S["out"], 16)

        @block.gpsimd
        def _(pool):
            chain = [0]

            def link(ins):
                chain[0] += 1
                ins.then_inc(S["pool_chain"], 1)
                pool.wait_ge(S["pool_chain"], chain[0])

            def inv_root(out, in_, width, n, done):
                r = in_.shape[0]
                link(nc.gpsimd.tensor_scalar(in_, in_, 1.0 / width, EPS, ALU.mult, ALU.add))
                nc.gpsimd.tensor_tensor(out, in_, mhalf[0:r, 0:n], ALU.pow).then_inc(S[done], 1)

            link(nc.gpsimd.memset(mhalf[:], -0.5))

            def norm(n):
                pool.wait_ge(S["ss"], NT * (n + 1))
                inv_root(rstd[:], ss[:], DM, NT, "rstd")

            norm(0)
            for i, n in enumerate((8, 16, 16, 16)):
                pool.wait_ge(S["head_ss"], i + 1)
                inv_root(hrs[:, i, 0:n], hss[:, i, 0:n], HD, n, "head_rstd")
                if i == 1:
                    pool.wait_ge(S["kcmp_ss"], 1)
                    inv_root(hrs[0:30, 4, 0:1], hss[0:30, 4, 0:1], HD, 1, "kcmp_rstd")
            if stop >= 3:
                norm(1)
            if stop >= 4:
                norm(2)
                pool.wait_ge(S["x_ready"], 8)
                nc.gpsimd.memset(kt, 0.0).then_inc(S["kt_zero"], 1)
                pool.wait_ge(S["decay"], 1)
                nc.gpsimd.memset(prod, 0.0).then_inc(S["prod_zero"], 1)
                pool.wait_ge(S["gla_ss"], NT * GH)
                inv_root(ors[:], oss[:], 256, NT * GH, "gla_rstd")
            if stop >= 5:
                norm(3)

        @block.tensor
        def _(pe):
            mm = nc.tensor.matmul

            def transposes(g, ready):
                for i in range(4):
                    t, half = i // 2, i % 2
                    ready(t)
                    for j in range(4):
                        k = half * 4 + j
                        last = nc.tensor.transpose(bank[i][:, j * P:(j + 1) * P], hn[:, t, k * P:(k + 1) * P], ident)
                    last.then_inc(S["hT_psum"], 1)

            def normed(n):
                return lambda t: pe.wait_ge(S["hn"], NT * n + t + 1)

            def group(u0, cg, banks, width=BLK):
                for k in range(NK):
                    b = cg * NK + k
                    if b % UB == 0:
                        loaded(pe, u0 + b // UB)
                    w = block_at(u0, b)
                    for t in range(NT):
                        last = mm(bank[banks[t]][:, 0:width], hT[:, k, t * P:(t + 1) * P], w[:, 0:width],
                                  start=(k == 0), stop=(k == NK - 1))
                    if b % UB == UB - 1:
                        last.then_inc(S["units_used"], 1)

            def block_at(u0, b):
                u = u0 + b // UB
                return ring[:, u % RING, b % UB, :]

            pe.wait_ge(S["const_in"], CONST_DMAS * 16)
            transposes(0, normed(0))
            pe.wait_ge(S["hT"], 4)

            def in_group(cg):
                if cg >= 2:
                    pe.wait_ge(S["proj"], 2 * (cg - 1))
                b = 4 + 2 * (cg % 2)
                group(U_A_IN, cg, (b, b + 1), FRONT_WIDTH.get(cg, BLK))

            in_group(0)
            in_group(1)
            pe.wait_ge(S["proj"], 2)
            for v in range(2):
                for g in range(NG):
                    for t in range(NT):
                        last = nc.tensor.transpose(bank[v][0:HD, (g * NT + t) * P:(g * NT + t + 1) * P],
                                                   proj[0][:, t, v * P + g * HD:v * P + (g + 1) * HD], ident)
                last.then_inc(S["kc_psum"], 1)
            in_group(2)
            pe.wait_ge(S["late_in"], 48)
            pe.wait_ge(S["blk"], 4)
            for v in range(2):
                for j in range(16):
                    last = mm(bank[2][0:HD, v * 32:v * 32 + 30], cw1[:, v, j, :],
                              blkT[:, v, j, :, :].rearrange("p g n -> p (g n)"), start=(j == 0), stop=(j == 15))
            last.then_inc(S["hid"], 1)
            pe.wait_ge(S["head_done"], 1)
            pe.wait_ge(S["kc"], 4)
            for t in range(NT):
                for kk in range(4):
                    last = nc.tensor.transpose(bank[t][0:HD, kk * P:(kk + 1) * P],
                                               proj[0][:, t, 256 + kk * HD:256 + (kk + 1) * HD], ident)
                last.then_inc(S["headT_psum"], 1)
            pe.wait_ge(S["gelu"], 1)
            mm(bank[3][0:30, 0:HD], gel[0:HD, 3, 0:30], cw2[0:HD, 0, :], start=True, stop=True)
            for g in range(NG):
                last = mm(bank[3][0:NCMP, (g + 1) * HD:(g + 2) * HD], gel[0:HD, 3, 30 + NCMP * g:30 + NCMP * (g + 1)],
                          cw2[0:HD, 1, :], start=True, stop=True)
            last.then_inc(S["cmp2"], 1)
            in_group(3)
            pe.wait_ge(S["cmp2_sb"], 1)
            for g in range(NG):
                last = mm(bank[2][:, 0:HD], cst[0:NCMP, C_REP + g * P:C_REP + (g + 1) * P], vcmp[0:NCMP, g, :],
                          start=(g == 0), stop=(g == NG - 1))
            last.then_inc(S["vrep"], 1)
            pe.wait_ge(S["kcmp"], 1)
            nc.tensor.transpose(bank[3][0:HD, 256:286], kcm[0:30, 3, :], ident[0:30, 0:30]).then_inc(S["kcmpT_psum"], 1)
            in_group(4)
            in_group(5)
            pe.wait_ge(S["head_done"], 2)
            pe.wait_ge(S["vbd"], 1)
            pe.wait_ge(S["kcmpT"], 1)
            for i in range(4):
                t, half = i // 2, i % 2
                if i < 2:
                    pe.wait_ge(S["headT"], i + 1)
                for j in range(4):
                    h = half * 4 + j
                    last = nc.tensor.transpose(bank[i][0:HD, j * P:(j + 1) * P],
                                               proj[2][:, t, h * HD:(h + 1) * HD], ident)
                last.then_inc(S["headT_psum"], 1)
            pe.wait_ge(S["headT"], 3)
            pe.wait_ge(S["fox_lf"], 1)
            mm(bank[0][:, 0:8], tri, fz[:, 4, 0:8], start=True, stop=True)
            mm(bank[0][:, 8:16], ones, fz[:, 4, 0:8], start=True, stop=False)
            mm(bank[0][:, 8:16], tri, fz[:, 4, 8:16], start=False, stop=True).then_inc(S["cum"], 1)
            pe.wait_ge(S["proj"], 12)
            pe.wait_ge(S["headT"], 6)
            for t in range(NT):
                for h in range(NH):
                    g = h // 4
                    last = mm(bank[6][:, t * P + h * 16:t * P + h * 16 + NCMP], qT[0:HD, h, t * P:(t + 1) * P],
                              kcmpT[0:HD, g * NCMP:(g + 1) * NCMP], start=True, stop=True)
            last.then_inc(S["cmp_s"], 1)
            pe.wait_ge(S["aug"], 1)
            for i in range(8):
                w, t, half = i // 4, i // 2 % 2, i % 2
                if i % 4 == 0:
                    pe.wait_ge(S["head_done"], 3 + w)
                if i >= 4:
                    pe.wait_ge(S["foxT"], i - 3)
                for j in range(4):
                    h = half * 4 + j
                    last = nc.tensor.transpose(bank[i % 4][0:66, j * P:(j + 1) * P], faug[:, w, t, h, :], ident)
                last.then_inc(S["foxT_psum"], 1)
            pe.wait_ge(S["cmp_p"], 1)
            for t in range(NT):
                last = nc.tensor.transpose(bank[7][:, t * P:(t + 1) * P], sc[:, t, :], ident)
            last.then_inc(S["cmp_pT_psum"], 1)
            pe.wait_ge(S["cmp_pT"], 1)
            for t in range(NT):
                mm(bank[4 + t][:, :], pcT[:, t, :], vbd, start=True, stop=True).then_inc(S["cmp_o"], 1)

            def qk(u):
                br, t, h0, n = att_units[u]
                kw = (t + 1) * P
                if u >= 2:
                    pe.wait_ge(S["probs"], u - 1)
                mm(bank[u % 2][:, :], mident, msk[:, 512 * t:512 * t + 512], start=True, stop=False)
                for j in range(n):
                    h = h0 + j
                    if br < 2:
                        q, k = qT[0:HD, h, t * P:(t + 1) * P], keyT[0:HD, br * 2 + h // 4, 0:kw]
                    else:
                        q, k = fqT[0:66, h, t * P:(t + 1) * P], fkT[0:66, h, 0:kw]
                    last = mm(bank[u % 2][:, j * kw:(j + 1) * kw], q, k, start=False, stop=(j == n - 1))
                last.then_inc(S["scores"], 1)

            def turn(u):
                pe.wait_ge(S["probs"], u + 1)
                if u >= 2:
                    pe.wait_ge(S["probsT"], u - 1)
                for j in range(4):
                    last = nc.tensor.transpose(bank[2 + u % 2][:, j * P:(j + 1) * P],
                                               pbuf[:, u % 2, j * P:(j + 1) * P], ident)
                last.then_inc(S["probsT_psum"], 1)

            def pv(u):
                br, t, h0, n = att_units[u]
                sq_ = seq_of(u)
                pe.wait_ge(S["probsT"], u + 1)
                if u == 0 or seq_of(u - 1) != sq_:
                    pe.wait_ge(S["o_done"], sq_ + 1)
                for j in range(n):
                    h = h0 + j
                    for kt_ in range(t + 1):
                        if br < 2:
                            v = proj[1][:, kt_, br * P + (h // 4) * HD:br * P + (h // 4 + 1) * HD]
                        else:
                            v = proj[5][:, kt_, h * HD:(h + 1) * HD]
                        m = j * (t + 1) + kt_
                        last = mm(bank[4 + sq_ % 2][:, h * HD:(h + 1) * HD], ptb[:, u % 2, m * P:(m + 1) * P], v,
                                  start=(kt_ == 0), stop=(kt_ == t))
                last.then_inc(S["pv"], 1)

            pe.wait_ge(S["foxT"], 8)
            qk(0)
            for u in range(AU):
                if u + 1 < AU:
                    qk(u + 1)
                turn(u)
                if u >= 1:
                    pv(u - 1)
            pv(AU - 1)
            transposes(1, lambda t: pe.wait_ge(S["o_done"], 8))
            if stop < 2:
                return
            pe.wait_ge(S["hT"], 8)
            group(U_A_OUT, 0, (4, 5))
            group(U_A_OUT, 1, (6, 7))
            if stop < 3:
                return
            transposes(2, normed(1))
            pe.wait_ge(S["hT"], 12)

            def gate_up(i, half):
                c, t = steps[i]
                if t == 0:
                    loaded(pe, U_FFN + 3 * c + half)
                if half == 0 and i >= 2:
                    pe.wait_ge(S["hact"], i - 1)
                for k in range(4 * half, 4 * half + 4):
                    last = mm(bank[i % 2][:, :], hT[:, k, t * P:(t + 1) * P], block_at(U_FFN + 3 * c, k),
                              start=(k == 0), stop=(k == NK - 1))
                if t == 1:
                    last.then_inc(S["units_used"], 1)
                elif half:
                    last.then_inc(S["gu"], 1)

            def hidden_T(i):
                pe.wait_ge(S["hact"], i + 1)
                for j in range(2):
                    last = nc.tensor.transpose(bank[2][:, j * P:(j + 1) * P], hact[:, i % 2, j * P:(j + 1) * P], ident)
                last.then_inc(S["h2T_psum"], 1)

            def down(i):
                c, t = steps[i]
                if t == 0:
                    loaded(pe, U_FFN + 3 * c + 2)
                pe.wait_ge(S["h2T"], i + 1)
                for j in range(2):
                    for half in range(2):
                        last = mm(bank[4 + 2 * t + half][:, :], h2T[:, i % 2, j * P:(j + 1) * P],
                                  block_at(U_FFN + 3 * c, NK + 2 * j + half),
                                  start=(c == 0 and j == 0), stop=(c == NCH - 1 and j == 1))
                if t == 1:
                    last.then_inc(S["units_used"], 1)

            n = len(steps)
            for i in range(n):
                gate_up(i, 0)
                if i:
                    hidden_T(i - 1)
                gate_up(i, 1)
                if i:
                    down(i - 1)
            hidden_T(n - 1)
            down(n - 1)
            if stop < 4:
                return

            transposes(3, normed(2))
            pe.wait_ge(S["hT"], 16)
            for k in range(NK):
                last = mm(bank[6][0:16, 0:SEQ], sml[:, R_A1 + 16 * k:R_A1 + 16 * (k + 1)], hT[:, k, :],
                          start=(k == 0), stop=(k == NK - 1))
            last.then_inc(S["a1"], 1)

            def channels(cg, b0):
                for k in range(NK):
                    b = cg * NK + k
                    if b % UB == 0:
                        loaded(pe, U_C_IN + b // UB)
                    w = block_at(U_C_IN, b)
                    for m in range(GH):
                        last = mm(bank[b0 + m][:, 0:SEQ], w[:, m * P:(m + 1) * P], hT[:, k, :],
                                  start=(k == 0), stop=(k == NK - 1))
                    if b % UB == UB - 1:
                        last.then_inc(S["units_used"], 1)

            channels(0, 0)
            pe.wait_ge(S["a1_sb"], 1)
            for h in range(GH):
                last = mm(bank[4 + h // 2][:, h % 2 * SEQ:(h % 2 + 1) * SEQ], wa2[:, h * P:(h + 1) * P], a1T[0:16, :],
                          start=True, stop=True)
            last.then_inc(S["z"], 1)
            pe.wait_ge(S["zb"], 1)
            channels(1, 4)
            pe.wait_ge(S["gla_qk"], 4)
            group(U_C_IN, 2, (0, 1))
            group(U_C_IN, 3, (2, 3))
            pe.wait_ge(S["gla_qk"], 8)
            group(U_C_IN, 4, (4, 5))
            group(U_C_IN, 5, (6, 7))

            def diagonal(t):
                pe.wait_ge(S["prod"], GB * (t + 1))
                for s_ in range(GB):
                    last = mm(bank[t][:, :], cst[:, C_SEL + GB - s_:C_SEL + GB - s_ + P], prod[:, s_, :],
                              start=(s_ == 0), stop=(s_ == GB - 1))
                last.then_inc(S["diag"], 1)

            def cross(t):
                pe.wait_ge(S["kt"], t + 1)
                pe.wait_ge(S["qt"], t + 1)
                for h in range(GH):
                    for i in range(1, NGB):
                        at = h * P + i * GB
                        last = mm(bank[2 + t][:, at:at + GB], kt[:, i - 1, h * P:(h + 1) * P], gqt[:, at:at + GB],
                                  start=True, stop=True)
                last.then_inc(S["cross"], 1)

            pe.wait_ge(S["gla_vr"], 4)
            for t in range(NT):
                cross(t)
                diagonal(t)
            pe.wait_ge(S["far_ops"], 1)
            pe.wait_ge(S["gla_vr"], 8)
            for h in range(GH):
                last = mm(bank[4][:, h * P:(h + 1) * P], kbar[:, h * P:(h + 1) * P], qbar[:, h * P:(h + 1) * P],
                          start=True, stop=True)
            last.then_inc(S["far_psum"], 1)
            pe.wait_ge(S["att"], 2)
            pe.wait_ge(S["far_sb"], 1)
            for t in range(NT):
                for h in range(GH):
                    o = bank[GLA_BANKS[2 * t + h // 2]][:, h % 2 * 256:(h % 2 + 1) * 256]
                    last = mm(o, att[:, t, h * P:(h + 1) * P], gv[:, t, h * 256:(h + 1) * 256],
                              start=True, stop=(t == 0))
                    if t == 1:
                        last = mm(o, far[:, h * P:(h + 1) * P], gv[:, 0, h * 256:(h + 1) * 256],
                                  start=False, stop=True)
                    if h % 2:
                        last.then_inc(S["gla_o"], 1)
            transposes(4, lambda t: pe.wait_ge(S["mixed"], NT * GH))
            pe.wait_ge(S["hT"], 20)
            group(U_C_OUT, 0, (4, 5))
            group(U_C_OUT, 1, (6, 7))
            if stop < 5:
                return

            transposes(5, normed(3))
            pe.wait_ge(S["hT"], 24)
            for t in range(NT):
                for k in range(NK):
                    last = mm(bank[0][:, t * 8:t * 8 + 8], hT[:, k, t * P:(t + 1) * P],
                              sml[:, R_ROUTER + 8 * k:R_ROUTER + 8 * (k + 1)], start=(k == 0), stop=(k == NK - 1))
            last.then_inc(S["logits"], 1)
            pe.wait_ge(S["picked"], 1)
            mm(bank[1][:, 0:8], tri, picked[:, 0, :], start=True, stop=True)
            mm(bank[1][:, 8:16], ones, picked[:, 0, :], start=True, stop=False)
            mm(bank[1][:, 8:16], tri, picked[:, 1, :], start=False, stop=True)
            mm(bank[1][:, 16:24], ones, picked[:, 0, :], start=True, stop=False)
            mm(bank[1][:, 16:24], ones, picked[:, 1, :], start=False, stop=True).then_inc(S["rank"], 1)

            def gather(e, half):
                if half == 0:
                    pe.wait_ge(S["disp"], e + 2)
                else:
                    pe.wait_ge(S["xg"], (e + 1) * 2 + 1)
                for j in range(4):
                    k = half * 4 + j
                    for t in range(NT):
                        last = mm(bank[3][:, j * P:(j + 1) * P], hn[:, t, k * P:(k + 1) * P], disp[:, t, :],
                                  start=(t == 0), stop=(t == NT - 1))
                last.then_inc(S["xg_psum"], 1)

            def expert(e):
                def ring_block(pos, b):
                    return ring[:, (U_MOE + pos) % RING, b, :]

                def arrived(pos):
                    u = U_MOE + pos
                    pe.wait_ge(s_loaded[u % RING], e * (16 * EXP_UNITS // RING) + 16 * (u // RING + 1))

                def m_gate_up(c, half):
                    arrived(pos_g(c, half))
                    for k in range(4 * half, 4 * half + 4):
                        last = mm(bank[c % 2][:, :], xgT[:, k, :], ring_block(pos_g(c, half), k % 4),
                                  start=(k == 0), stop=(k == NK - 1))
                    last.then_inc(S["units_used"], 1)

                def m_hidden_T(c):
                    pe.wait_ge(S["m_hact"], e * NCH + c + 1)
                    for j in range(2):
                        last = nc.tensor.transpose(bank[2][:, j * P:(j + 1) * P],
                                                   hact[:, c % 2, j * P:(j + 1) * P], ident)
                    last.then_inc(S["m_h2T_psum"], 1)

                def m_down(c):
                    arrived(pos_d(c))
                    pe.wait_ge(S["m_h2T"], e * NCH + c + 1)
                    for j in range(2):
                        for half in range(2):
                            last = mm(bank[4 + half][:, :], h2T[:, c % 2, j * P:(j + 1) * P],
                                      ring_block(pos_d(c), 2 * j + half),
                                      start=(c == 0 and j == 0), stop=(c == NCH - 1 and j == 1))
                    last.then_inc(S["units_used"], 1)

                pe.wait_ge(S["xg"], (e + 1) * 2)
                for c in range(NCH):
                    m_gate_up(c, 0)
                    if c:
                        m_hidden_T(c - 1)
                    if c == 1:
                        pe.wait_ge(S["dispg"], e + 1)
                        pe.wait_ge(S["x_ready"], e * 4 + X_MOE)
                        for t in range(NT):
                            last = nc.tensor.transpose(bank[6][:, t * P:(t + 1) * P], dispg[:, t, :], ident)
                        last.then_inc(S["combT_psum"], 1)
                    m_gate_up(c, 1)
                    if c:
                        m_down(c - 1)
                m_hidden_T(NCH - 1)
                gather(e, 0)
                m_down(NCH - 1)
                gather(e, 1)
                pe.wait_ge(S["combT"], e + 1)
                pe.wait_ge(S["ysb"], e * 2 + 2)
                for i in range(4):
                    t, half = i // 2, i % 2
                    if i >= 2:
                        pe.wait_ge(S["x_ready"], e * 4 + (X_MOE + i - 1))
                    mm(bank[6 + i % 2][:, :], combT[:, t, :], ysb[:, half * BLK:(half + 1) * BLK],
                       start=True, stop=True).then_inc(S["scat"], 1)

            gather(-1, 0)
            gather(-1, 1)
            with pe.Fori(0, NE) as e:
                expert(e)
            n_over = pe.value_load(ovi[0:1, 0:1], min_val=0, max_val=OVER_ROUNDS)
            with pe.Fori(NE, NE + OVER_ROUNDS) as e:
                with pe.If(n_over > e - NE):
                    expert(e)

        @block.scalar
        def _(act):
            A = nc.scalar.activation

            def norm(n):
                if n == 0:
                    act.wait_ge(S["x_in"], 16)
                else:
                    act.wait_ge(S["x_ready"], 4 * n)
                junk = hT[:, :, :].rearrange("p k n -> p (k n)")
                for t in range(NT):
                    A(junk[:, t * DM:(t + 1) * DM], x[:, t, :], ACT.Square, accum_out=ss[:, t:t + 1]).then_inc(S["ss"], 1)

            norm(0)
            for cg in range(A_IN_CG):
                w = FRONT_WIDTH.get(cg, BLK)
                act.wait_ge(S["units_used"], 2 * (cg + 1))
                for t in range(NT):
                    nc.scalar.copy(proj[cg][:, t, 0:w], bank[4 + 2 * (cg % 2) + t][:, 0:w]).then_inc(S["proj"], 1)
                if cg == 2:
                    act.wait_ge(S["hid_in"], 1)
                    A(gel[0:HD, 1, 0:60], gel[0:HD, 2, 0:60], ACT.Tanh, scale=0.7978845608028654).then_inc(S["tanh"], 1)
                    act.wait_ge(S["gate_z"], 1)
                    A(gat, gat, ACT.Exp, scale=-1.0).then_inc(S["gate_e"], 1)
                    act.wait_ge(S["fox_z"], 1)
                    A(fz[:, 2, :], fz[:, 1, :], ACT.Exp, scale=-1.0).then_inc(S["act_chain"], 1)
                    act.wait_ge(S["act_chain"], 1)
                    A(fz[:, 3, :], fz[:, 2, :], ACT.Ln, bias=1.0).then_inc(S["fox_l"], 1)
            act.wait_ge(S["cmp_d"], 1)
            A(sc, sc, ACT.Exp, scale=HD ** -0.5).then_inc(S["cmp_e"], 1)
            for i in range(8):
                w, t, half = i // 4, i // 2 % 2, i % 2
                act.wait_ge(S["foxT_psum"], i + 1)
                dst = (fqT, fkT)[w]
                nc.scalar.copy(dst[0:66, half * 4:half * 4 + 4, t * P:(t + 1) * P],
                               bank[i % 4][0:66, :].rearrange("p (h n) -> p h n", h=4)).then_inc(S["foxT"], 1)
            for u in range(AU):
                br, t, h0, n = att_units[u]
                kw = (t + 1) * P
                act.wait_ge(S["rowmax"], u + 1)
                if u >= 2:
                    act.wait_ge(S["probsT_psum"], u - 1)
                for j in range(n):
                    last = A(pbuf[:, u % 2, j * kw:(j + 1) * kw], bank[u % 2][:, j * kw:(j + 1) * kw], ACT.Exp,
                             scale=HD ** -0.5, bias=negm[:, seq_of(u), h0 + j:h0 + j + 1],
                             accum_out=sums[:, seq_of(u), h0 + j:h0 + j + 1])
                last.then_inc(S["probs"], 1)
            if stop < 3:
                return
            norm(1)
            n_steps = len(steps)
            for i in range(n_steps + 1):
                if i >= 1:
                    act.wait_ge(S["h2T_psum"], i)
                    nc.scalar.copy(h2T[:, (i - 1) % 2, :], bank[2][:, 0:CH]).then_inc(S["h2T"], 1)
                if i < n_steps:
                    c, t = steps[i]
                    if t == 0:
                        act.wait_ge(S["gu"], c + 1)
                    else:
                        act.wait_ge(S["units_used"], U_FFN + 3 * c + 2)
                    A(sg[:, i % 2, :], bank[i % 2][:, 0:CH], ACT.Silu).then_inc(S["silu"], 1)
            if stop < 4:
                return
            norm(2)
            act.wait_ge(S["a1"], 1)
            nc.scalar.copy(a1T[0:16, :], bank[6][0:16, 0:SEQ]).then_inc(S["a1_sb"], 1)
            act.wait_ge(S["units_used"], U_C_IN + 2)
            for h in range(GH):
                A(gq[:, :, h * P:(h + 1) * P], bank[h][:, 0:SEQ].rearrange("p (t n) -> p t n", t=NT), ACT.Copy,
                  scale=P ** -0.5).then_inc(S["gla_qk"], 1)
            act.wait_ge(S["absz"], 1)
            A(ge, ge, ACT.Exp, scale=-1.0).then_inc(S["act_chain"], 1)
            act.wait_ge(S["act_chain"], 2)
            A(ge, ge, ACT.Ln, bias=1.0).then_inc(S["soft"], 1)
            act.wait_ge(S["units_used"], U_C_IN + 4)
            for h in range(GH):
                nc.scalar.copy(gk[:, :, h * P:(h + 1) * P], bank[4 + h][:, 0:SEQ].rearrange("p (t n) -> p t n", t=NT))\
                  .then_inc(S["gla_qk"], 1)

            def vr(cg):
                act.wait_ge(S["units_used"], U_C_IN + 2 * (cg + 1))
                half = cg % 2
                for t in range(NT):
                    dst = (gv if cg < 4 else gr)[:, t, half * BLK:(half + 1) * BLK]
                    b = bank[(0, 2, 4, 6)[cg - 2] + t]
                    if cg == 4 and t == 0:
                        act.wait_ge(S["cross"], NT)
                    A(dst, b[:, :], ACT.Copy if cg < 4 else ACT.Silu).then_inc(S["gla_vr"], 1)

            vr(2)
            vr(3)
            for t in range(NT):
                act.wait_ge(S["q_arg"], t + 1)
                qv = gqt.rearrange("p (h i r) -> p h i r", h=GH, r=GB)[:, :, 1:NGB, :]
                A(qv, qv, ACT.Exp).then_inc(S["q_exp"], 1)
                for i in range(1, NGB):
                    act.wait_ge(S["k_arg"], (NGB - 1) * t + i)
                    kv = kt[:, i - 1, :].rearrange("p (h n) -> p h n", h=GH)[:, :, 0:i * GB]
                    A(kv, kv, ACT.Exp).then_inc(S["k_exp"], 1)
                for s_ in range(GB):
                    d = t * GB + s_
                    act.wait_ge(S["diag_arg"], d + 1)
                    e_ = esc[:, d % 2, 0:(GB - s_) * 64]
                    A(e_, e_, ACT.Exp).then_inc(S["diag_exp"], 1)
            act.wait_ge(S["far_arg"], 1)
            A(kbar, kbar, ACT.Exp).then_inc(S["far_exp"], 1)
            A(qbar, gb[:, 1, :], ACT.Exp).then_inc(S["far_exp"], 1)
            vr(4)
            vr(5)
            act.wait_ge(S["far_psum"], 1)
            nc.scalar.copy(far, bank[4][:, :]).then_inc(S["far_sb"], 1)
            act.wait_ge(S["prod"], NT * GB)
            for i in range(NT * GH):
                act.wait_ge(S["gla_o"], i // 2 + 1)
                if i >= 2:
                    act.wait_ge(S["gla_ss"], i - 1)
                b = bank[GLA_BANKS[i // 2]]
                A(esc[:, i % 2, 0:256], b[:, i % 2 * 256:(i % 2 + 1) * 256], ACT.Square,
                  accum_out=oss[:, i:i + 1]).then_inc(S["gla_ss"], 1)
            if stop < 5:
                return
            norm(3)
            act.wait_ge(S["gap"], 1)
            A(ee, ee, ACT.Exp).then_inc(S["gap_exp"], 1)

            def expert(e):
                def turned(c):
                    act.wait_ge(S["m_h2T_psum"], e * NCH + c + 1)
                    nc.scalar.copy(h2T[:, c % 2, :], bank[2][:, 0:CH]).then_inc(S["m_h2T"], 1)

                for c in range(NCH):
                    if c:
                        turned(c - 1)
                    if c == 1:
                        act.wait_ge(S["combT_psum"], e + 1)
                        nc.scalar.copy(combT, bank[6][:, 0:2 * P].rearrange("p (t n) -> p t n", t=NT))\
                          .then_inc(S["combT"], 1)
                    act.wait_ge(S["units_used"], e * EXP_UNITS + (U_MOE + pos_g(c, 1) + 1))
                    A(sg[:, c % 2, :], bank[c % 2][:, 0:CH], ACT.Silu).then_inc(S["m_silu"], 1)
                turned(NCH - 1)
                act.wait_ge(S["units_used"], e * EXP_UNITS + (U_MOE + EXP_UNITS))
                for half in range(2):
                    nc.scalar.copy(ysb[:, half * BLK:(half + 1) * BLK], bank[4 + half][:, :]).then_inc(S["ysb"], 1)

            with act.Fori(0, NE) as e:
                expert(e)
            act.wait_ge(S["route"], 1)
            n_over = act.value_load(ovi[0:1, 0:1], min_val=0, max_val=OVER_ROUNDS)
            with act.Fori(NE, NE + OVER_ROUNDS) as e:
                with act.If(n_over > e - NE):
                    expert(e)

        @block.vector
        def _(dve):
            V = nc.vector
            chain = [0]

            def link(ins):
                chain[0] += 1
                ins.then_inc(S["dve_chain"], 1)
                dve.wait_ge(S["dve_chain"], chain[0])

            def bc(ap, axis, n):
                a = ap.unsqueeze(axis)
                shape = list(a.shape)
                shape[axis] = n
                return a.to_broadcast(shape)

            def norm(n):
                dve.wait_ge(S["rstd"], n + 1)
                for t in range(NT):
                    V.tensor_scalar(hn[:, t, :], x[:, t, :], rstd[:, t:t + 1], None, ALU.mult).then_inc(S["hn"], 1)

            def turned(g, gain=None):
                for i in range(4):
                    t, half = i // 2, i % 2
                    dve.wait_ge(S["hT_psum"], 4 * g + i + 1)
                    dst = hT[:, half * 4:half * 4 + 4, t * P:(t + 1) * P]
                    src = bank[i][:, :].rearrange("p (k n) -> p k n", k=4)
                    if gain is None:
                        V.tensor_copy(dst, src).then_inc(S["hT"], 1)
                    else:
                        gc = R_NORM + NK * gain + 4 * half
                        V.tensor_tensor(dst, src, bc(sml[:, gc:gc + 4], 2, P), ALU.mult).then_inc(S["hT"], 1)

            def residual(u0):
                for cg in range(2):
                    dve.wait_ge(S["units_used"], u0 + 2 * (cg + 1))
                    for t in range(NT):
                        xs = x[:, t, cg * BLK:(cg + 1) * BLK]
                        V.tensor_tensor(xs, xs, bank[4 + 2 * cg + t][:, :], ALU.add).then_inc(S["x_ready"], 1)

            def head_norm(src, nh, which, gain, dst, order):
                n = NT * nh
                dve.wait_ge(S["head_done"], order - 1)
                s3 = sq[:, 0:n * HD].rearrange("p (r d) -> p r d", d=HD).rearrange("p (t h) d -> p t h d", t=NT)
                link(V.tensor_tensor(s3, src, src, ALU.mult))
                V.tensor_reduce(hss[:, which, 0:n], sq[:, 0:n * HD].rearrange("p (r d) -> p r d", d=HD), AX.X, ALU.add)\
                 .then_inc(S["head_ss"], 1)
                dve.wait_ge(S["head_rstd"], order)
                r3 = hrs[:, which, 0:n].rearrange("p (t h) -> p t h", t=NT)
                link(V.tensor_tensor(s3, src, bc(r3, 3, HD), ALU.mult))
                g1 = bc(bc(sml[:, gain:gain + HD], 1, nh), 1, NT)
                return V.tensor_tensor(dst, s3, g1, ALU.mult)

            def rope(v, tab, nh, ra, rb):
                link(V.tensor_tensor(ra, v[:, :, :, 0:16], bc(tab[:, :, 0:16], 2, nh), ALU.mult))
                V.tensor_tensor(rb[:, :, :, 0:8], v[:, :, :, 8:16], bc(tab[:, :, 16:24], 2, nh), ALU.mult)
                link(V.tensor_tensor(rb[:, :, :, 8:16], v[:, :, :, 0:8], bc(tab[:, :, 24:32], 2, nh), ALU.mult))
                return V.tensor_tensor(v[:, :, :, 0:16], ra, rb, ALU.add)

            def four(buf, nh):
                return buf[:, 0:NT * nh * 16].rearrange("p (t h d) -> p t h d", t=NT, h=nh)

            dve.wait_ge(S["x_in"], 16)
            norm(0)
            dve.wait_ge(S["const_in"], CONST_DMAS * 16)
            turned(0, 0)
            for v in range(2):
                dve.wait_ge(S["kc_psum"], v + 1)
                src = bank[v][0:HD, :].rearrange("p (g n) -> p g n", g=NG)
                V.tensor_copy(kc2[0:HD, v, :, :], src).then_inc(S["kc"], 1)
                V.tensor_copy(kc2[HD:P, v, :, 0:SEQ - 1], src[:, :, 1:SEQ]).then_inc(S["kc"], 1)
            dve.wait_ge(S["kc"], 4)
            for v in range(2):
                for g in range(NG):
                    first = kc2[:, v, g, :].rearrange("p (m j w) -> p j m w", j=8, w=2)[:, :, :, 0]
                    pe_ = sml[:, R_PE + 16 * v:R_PE + 16 * (v + 1)]
                    V.tensor_tensor(blkT[:, v, 0:8, g, :], first[:, :, 0:NCMP], bc(pe_[:, 0:8], 2, NCMP), ALU.add)
                    V.tensor_tensor(blkT[:, v, 8:16, g, :], first[:, :, 1:NCMP + 1], bc(pe_[:, 8:16], 2, NCMP),
                                    ALU.add).then_inc(S["blk"], 1)
            tab = cst[:, C_ROPE:C_ROPE + 64].rearrange("p (t n) -> p t n", t=NT)
            keys = proj[0][:, :, 256:512].rearrange("p t (h d) -> p t h d", h=4)
            link(head_norm(keys, 4, 0, R_KN, keys, 1))
            rope(keys, tab, 4, four(rA, 4), four(rB, 4)).then_inc(S["head_done"], 1)
            dve.wait_ge(S["proj"], 4)
            V.tensor_tensor(gat.rearrange("p (t n) -> p t n", t=NT), proj[1][:, :, 256:280],
                            bc(sml[:, R_GB:R_GB + 24], 1, NT), ALU.add).then_inc(S["gate_z"], 1)
            link(V.tensor_tensor(fz[:, 0, :].rearrange("p (t n) -> p t n", t=NT), proj[1][:, :, 280:288],
                                 bc(sml[:, R_FB:R_FB + 8], 1, NT), ALU.add))
            link(V.tensor_scalar(fz[:, 1, :], fz[:, 0, :], -1.0, None, ALU.mult))
            V.tensor_tensor(fz[:, 1, :], fz[:, 1, :], fz[:, 0, :], ALU.max).then_inc(S["fox_z"], 1)
            dve.wait_ge(S["hid"], 1)
            xh = gel[0:HD, 0, 0:60]
            uu = gel[0:HD, 2, 0:60]
            link(V.tensor_copy(xh.rearrange("p (v n) -> p v n", v=2),
                               bank[2][0:HD, 0:64].rearrange("p (v n) -> p v n", v=2)[:, :, 0:30]))
            link(V.tensor_tensor(uu, xh, xh, ALU.mult))
            link(V.tensor_scalar(uu, uu, 0.044715, 1.0, ALU.mult, ALU.add))
            V.tensor_tensor(uu, uu, xh, ALU.mult).then_inc(S["hid_in"], 1)
            for t in range(NT):
                dve.wait_ge(S["headT_psum"], t + 1)
                V.tensor_copy(keyT[0:HD, :, t * P:(t + 1) * P], bank[t][0:HD, :].rearrange("p (h n) -> p h n", h=4))\
                 .then_inc(S["headT"], 1)
            dve.wait_ge(S["tanh"], 1)
            link(V.tensor_scalar(gel[0:HD, 1, 0:60], gel[0:HD, 1, 0:60], 0.5, 0.5, ALU.mult, ALU.add))
            V.tensor_tensor(gel[0:HD, 3, 0:60], gel[0:HD, 1, 0:60], xh, ALU.mult).then_inc(S["gelu"], 1)
            dve.wait_ge(S["proj"], 6)
            qa = proj[2][:, :, :].rearrange("p t (h d) -> p t h d", h=NH)
            link(head_norm(qa, NH, 1, R_QN, qa, 2))
            dve.wait_ge(S["cmp2"], 1)
            V.tensor_copy(vcmp[0:NCMP, :, :], bank[3][0:NCMP, HD:3 * HD].rearrange("p (g d) -> p g d", g=NG))\
             .then_inc(S["cmp2_sb"], 1)
            link(V.tensor_copy(kcm[0:30, 0, :], bank[3][0:30, 0:HD]))
            link(V.tensor_tensor(kcm[0:30, 1, :], kcm[0:30, 0, :], kcm[0:30, 0, :], ALU.mult))
            V.tensor_reduce(hss[0:30, 4, 0:1], kcm[0:30, 1, :], AX.X, ALU.add).then_inc(S["kcmp_ss"], 1)
            rope(qa, tab, NH, four(rA, NH), four(rB, NH)).then_inc(S["head_done"], 1)
            dve.wait_ge(S["kcmp_rstd"], 1)
            link(V.scalar_tensor_tensor(kcm[0:30, 3, :], kcm[0:30, 0, :], hrs[0:30, 4, 0:1], sml[0:30, R_KN:R_KN + HD],
                                        ALU.mult, ALU.mult))
            ct = cst[0:30, C_CROPE:C_CROPE + 32]
            kv = kcm[0:30, 3, :]
            dve.wait_ge(S["head_done"], 2)
            link(V.tensor_tensor(rA[0:30, 0:16], kv[:, 0:16], ct[:, 0:16], ALU.mult))
            V.tensor_tensor(rB[0:30, 0:8], kv[:, 8:16], ct[:, 16:24], ALU.mult)
            link(V.tensor_tensor(rB[0:30, 8:16], kv[:, 0:8], ct[:, 24:32], ALU.mult))
            V.tensor_tensor(kv[:, 0:16], rA[0:30, 0:16], rB[0:30, 0:16], ALU.add).then_inc(S["kcmp"], 1)
            dve.wait_ge(S["vrep"], 1)
            V.tensor_tensor(vbd.rearrange("p (h d) -> p h d", h=NH), bc(bank[2][:, 0:HD], 1, NH),
                            bc(cst[:, C_HMASK:C_HMASK + 8], 2, HD), ALU.mult).then_inc(S["vbd"], 1)
            dve.wait_ge(S["kcmpT_psum"], 1)
            V.tensor_copy(kcmpT[0:HD, 0:30], bank[3][0:HD, 256:286]).then_inc(S["kcmpT"], 1)
            for i in range(4):
                t, half = i // 2, i % 2
                dve.wait_ge(S["headT_psum"], 3 + i)
                V.tensor_copy(qT[0:HD, half * 4:half * 4 + 4, t * P:(t + 1) * P],
                              bank[i][0:HD, :].rearrange("p (h n) -> p h n", h=4)).then_inc(S["headT"], 1)
            dve.wait_ge(S["fox_l"], 1)
            V.scalar_tensor_tensor(fz[:, 4, :], fz[:, 0, :], 0.0, fz[:, 3, :], ALU.min, ALU.subtract)\
             .then_inc(S["fox_lf"], 1)
            dve.wait_ge(S["gate_e"], 1)
            link(V.tensor_scalar(gat, gat, 1.0, None, ALU.add))
            link(V.reciprocal(gat, gat))
            for w, gain in ((0, R_FQ), (1, R_FK)):
                dve.wait_ge(S["proj"], 8 + 2 * w)
                src = proj[3 + w][:, :, :].rearrange("p t (h d) -> p t h d", h=NH)
                head_norm(src, NH, 2 + w, gain, faug[:, w, :, :, 0:HD], 3 + w).then_inc(S["head_done"], 1)
                V.memset(faug[:, w, :, :, HD + 1 - w:HD + 2 - w], 1.0)
            dve.wait_ge(S["cum"], 1)
            cum = bank[0][:, 0:16].rearrange("p (t h) -> p t h", t=NT).unsqueeze(3)
            V.tensor_scalar(faug[:, 0, :, :, HD:HD + 1], cum, HD ** 0.5, None, ALU.mult)
            V.tensor_scalar(faug[:, 1, :, :, HD + 1:HD + 2], cum, -HD ** 0.5, None, ALU.mult).then_inc(S["aug"], 1)
            dve.wait_ge(S["cmp_s"], 1)
            s16 = sc.rearrange("p t (h n) -> p t h n", h=NH)
            s15 = s16[:, :, :, 0:NCMP]
            bias = cst[:, C_CBIAS:C_CBIAS + 32].rearrange("p (t n) -> p t n", t=NT)[:, :, 0:NCMP]
            cm01 = cst[:, C_CMASK:C_CMASK + 32].rearrange("p (t n) -> p t n", t=NT)
            V.memset(s16[:, :, :, NCMP:16], 0.0)
            link(V.tensor_tensor(s15, bank[6][:, 0:2 * P].rearrange("p (t h n) -> p t h n", t=NT, h=NH)[:, :, :, 0:NCMP],
                                 bc(bias, 2, NH), ALU.add))
            m3 = mc.rearrange("p (t h) -> p t h", t=NT)
            link(V.tensor_reduce(m3, s15, AX.X, ALU.max))
            V.tensor_tensor(s15, s15, bc(m3, 3, NCMP), ALU.subtract).then_inc(S["cmp_d"], 1)
            dve.wait_ge(S["cmp_e"], 1)
            link(V.tensor_reduce(sumc.rearrange("p (t h) -> p t h", t=NT), s15, AX.X, ALU.add))
            V.tensor_tensor(s16, s16, bc(cm01, 2, NH), ALU.mult).then_inc(S["cmp_p"], 1)
            link(V.reciprocal(sumc, sumc))
            g4 = gat.rearrange("p (t h w) -> p t h w", t=NT, h=NH)
            V.tensor_tensor(facc.rearrange("p (t h) -> p t h", t=NT), sumc.rearrange("p (t h) -> p t h", t=NT),
                            g4[:, :, :, 0], ALU.mult).then_inc(S["dve_chain"], 1)
            chain[0] += 1
            dve.wait_ge(S["cmp_pT_psum"], 1)
            V.tensor_copy(pcT, bank[7][:, 0:2 * P].rearrange("p (t n) -> p t n", t=NT)).then_inc(S["cmp_pT"], 1)
            dve.wait_ge(S["dve_chain"], chain[0])

            def heads(ap):
                return ap.rearrange("p (h d) -> p h d", h=NH)

            for t in range(NT):
                dve.wait_ge(S["cmp_o"], t + 1)
                V.tensor_tensor(heads(oacc[:, t, 0:512]), heads(bank[4 + t][:, :]), bc(facc[:, t * 8:t * 8 + 8], 2, HD),
                                ALU.mult).then_inc(S["o_done"], 1)

            def rowmax(u):
                br, t, h0, n = att_units[u]
                dve.wait_ge(S["scores"], u + 1)
                m = negm[:, seq_of(u), h0:h0 + n]
                link(V.tensor_reduce(m, bank[u % 2][:, :].rearrange("p (h n) -> p h n", h=n), AX.X, ALU.max))
                V.tensor_scalar(m, m, -HD ** -0.5, None, ALU.mult).then_inc(S["rowmax"], 1)

            def take(q):
                br, t = q // NT, q % NT
                dve.wait_ge(S["pv"], ends_seq[q] + 1)
                o = heads(bank[4 + q % 2][:, :])
                link(V.reciprocal(fac[:, q, :], sums[:, q, :]))
                if br == 2:
                    V.tensor_tensor(heads(oacc[:, t, 512:1024]), o, bc(fac[:, q, :], 2, HD), ALU.mult)\
                     .then_inc(S["o_done"], 1)
                    return
                link(V.tensor_tensor(fac[:, q, :], fac[:, q, :], g4[:, t, :, br + 1], ALU.mult))
                link(V.tensor_tensor(heads(tmpo), o, bc(fac[:, q, :], 2, HD), ALU.mult))
                V.tensor_tensor(oacc[:, t, 0:512], oacc[:, t, 0:512], tmpo, ALU.add).then_inc(S["o_done"], 1)

            rowmax(0)
            for u in range(AU):
                if u + 1 < AU:
                    rowmax(u + 1)
                dve.wait_ge(S["probsT_psum"], u + 1)
                if u >= 2:
                    dve.wait_ge(S["pv"], u - 1)
                V.tensor_copy(ptb[:, u % 2, :], bank[2 + u % 2][:, :]).then_inc(S["probsT"], 1)
                if u - 1 in ends_seq:
                    take(ends_seq.index(u - 1))
            take(2 * 3 - 1)
            turned(1)
            if stop < 2:
                return
            residual(U_A_OUT)
            if stop < 3:
                return
            norm(1)
            turned(2, 1)
            for i in range(len(steps)):
                dve.wait_ge(S["silu"], i + 1)
                V.tensor_tensor(hact[:, i % 2, :], sg[:, i % 2, :], bank[i % 2][:, CH:2 * CH], ALU.mult)\
                 .then_inc(S["hact"], 1)
            dve.wait_ge(S["units_used"], U_C_IN)
            for t in range(NT):
                for half in range(2):
                    xs = x[:, t, half * BLK:(half + 1) * BLK]
                    V.tensor_tensor(xs, xs, bank[4 + 2 * t + half][:, :], ALU.add).then_inc(S["x_ready"], 1)
            if stop < 4:
                return

            norm(2)
            turned(3, 2)
            V.memset(rmask, 1.0).then_inc(S["dve_chain"], 1)
            chain[0] += 1
            dve.wait_ge(S["dve_chain"], chain[0])
            link(V.memset(rmask.rearrange("p (s n) -> p s n", n=P)[:, :, 0:1], 0.0))
            dve.wait_ge(S["z"], 1)
            for h in range(GH):
                last = V.tensor_scalar(gz.rearrange("p (t h n) -> p t h n", t=NT, h=GH)[:, :, h, :],
                                       bank[4 + h // 2][:, h % 2 * SEQ:(h % 2 + 1) * SEQ].rearrange("p (t n) -> p t n", t=NT),
                                       sml[:, R_BA + h:R_BA + h + 1], None, ALU.add)
            last.then_inc(S["zb"], 1)
            dve.wait_ge(S["zb"], 1)
            link(V.tensor_scalar(ge, gz, -1.0, None, ALU.mult))
            V.tensor_tensor(ge, ge, gz, ALU.max).then_inc(S["absz"], 1)
            dve.wait_ge(S["soft"], 1)
            link(V.scalar_tensor_tensor(gz, gz, 0.0, ge, ALU.min, ALU.subtract))
            gbf = gb.rearrange("p t n -> p (t n)")
            link(V.tensor_scalar(gz, gz, 1.0 / 16.0, None, ALU.mult))
            V.tensor_tensor_scan(gbf, rmask, gz, 0.0, ALU.mult, ALU.add).then_inc(S["decay"], 1)
            dve.wait_ge(S["decay"], 1)
            dve.wait_ge(S["kt_zero"], 1)
            dve.wait_ge(S["gla_qk"], 8)

            def q_arg(t):
                b4 = gb[:, t, :].rearrange("p (h i r) -> p h i r", h=GH, r=GB)
                q4 = gqt.rearrange("p (h i r) -> p h i r", h=GH, r=GB)
                prev = b4[:, :, 0:NGB - 1, GB - 1:GB].to_broadcast([P, GH, NGB - 1, GB])
                V.tensor_tensor(q4[:, :, 1:NGB, :], b4[:, :, 1:NGB, :], prev, ALU.subtract).then_inc(S["q_arg"], 1)

            def k_view(t, i):
                kv_ = kt[:, i - 1, :].rearrange("p (h n) -> p h n", h=GH)[:, :, 0:i * GB]
                return kv_, gb[:, t, :].rearrange("p (h n) -> p h n", h=GH), gk[:, t, :].rearrange("p (h n) -> p h n", h=GH)

            def k_arg(t, i):
                kv_, b3, _ = k_view(t, i)
                edge = b3[:, :, i * GB - 1:i * GB].to_broadcast([P, GH, i * GB])
                V.tensor_tensor(kv_, edge, b3[:, :, 0:i * GB], ALU.subtract).then_inc(S["k_arg"], 1)

            def k_mul(t, i):
                kv_, _, k3 = k_view(t, i)
                dve.wait_ge(S["k_exp"], (NGB - 1) * t + i)
                last = V.tensor_tensor(kv_, kv_, k3[:, :, 0:i * GB], ALU.mult)
                if i == NGB - 1:
                    last.then_inc(S["kt"], 1)

            def diag_arg(d):
                t, s_ = d // GB, d % GB
                b3 = gb[:, t, :].rearrange("p (m r) -> p m r", r=GB)
                q3 = gq[:, t, :].rearrange("p (m r) -> p m r", r=GB)
                k3 = gk[:, t, :].rearrange("p (m r) -> p m r", r=GB)
                w = GB - s_
                e3 = esc[:, d % 2, 0:64 * w].rearrange("p (m r) -> p m r", r=w)
                if d >= 2:
                    dve.wait_ge(S["prod"], d - 1)
                V.tensor_tensor(e3, b3[:, :, s_:GB], b3[:, :, s_:s_ + 1].to_broadcast([P, 64, w]), ALU.subtract)\
                 .then_inc(S["diag_arg"], 1)
                p3 = prod[:, s_, :].rearrange("p (m r) -> p m r", r=GB)
                chain[0] += 1
                V.tensor_tensor(p3[:, :, s_:GB], q3[:, :, s_:GB], k3[:, :, s_:s_ + 1].to_broadcast([P, 64, w]), ALU.mult)\
                 .then_inc(S["dve_chain"], 1)
                return chain[0]

            def diag_mul(d, tag):
                s_ = d % GB
                w = GB - s_
                e3 = esc[:, d % 2, 0:64 * w].rearrange("p (m r) -> p m r", r=w)
                p3 = prod[:, s_, :].rearrange("p (m r) -> p m r", r=GB)
                dve.wait_ge(S["diag_exp"], d + 1)
                dve.wait_ge(S["dve_chain"], tag)
                V.tensor_tensor(p3[:, :, s_:GB], p3[:, :, s_:GB], e3, ALU.mult).then_inc(S["prod"], 1)

            for t in range(NT):
                if t:
                    dve.wait_ge(S["cross"], t)
                q_arg(t)
                k_arg(t, 1)
                k_arg(t, 2)
                for i in range(1, NGB):
                    if i + 2 < NGB:
                        k_arg(t, i + 2)
                    k_mul(t, i)
                q4 = gqt.rearrange("p (h i r) -> p h i r", h=GH, r=GB)[:, :, 1:NGB, :]
                dve.wait_ge(S["q_exp"], t + 1)
                V.tensor_tensor(q4, q4, gq[:, t, :].rearrange("p (h i r) -> p h i r", h=GH, r=GB)[:, :, 1:NGB, :],
                                ALU.mult).then_inc(S["qt"], 1)
                if t == 0:
                    dve.wait_ge(S["prod_zero"], 1)
                else:
                    dve.wait_ge(S["diag"], t)
                tag = diag_arg(GB * t)
                for d in range(GB * t, GB * (t + 1)):
                    nxt = diag_arg(d + 1) if d + 1 < GB * (t + 1) else None
                    diag_mul(d, tag)
                    tag = nxt
            dve.wait_ge(S["diag"], NT)
            V.tensor_tensor(kbar.rearrange("p (h n) -> p h n", h=GH),
                            gb[:, 0, :].rearrange("p (h n) -> p h n", h=GH)[:, :, P - 1:P].to_broadcast([P, GH, P]),
                            gb[:, 0, :].rearrange("p (h n) -> p h n", h=GH), ALU.subtract).then_inc(S["far_arg"], 1)
            for t in range(NT):
                dve.wait_ge(S["diag"], t + 1)
                a3 = att[:, t, :].rearrange("p (h n) -> p h n", h=GH)
                link(V.tensor_tensor(a3, bank[t][:, :].rearrange("p (h n) -> p h n", h=GH), bc(mbd, 1, GH), ALU.mult))
                dve.wait_ge(S["cross"], t + 1)
                V.tensor_tensor(a3[:, :, GB:P], a3[:, :, GB:P],
                                bank[2 + t][:, :].rearrange("p (h n) -> p h n", h=GH)[:, :, GB:P], ALU.add)\
                 .then_inc(S["att"], 1)
            dve.wait_ge(S["far_exp"], 2)
            V.tensor_tensor(kbar, kbar, gk[:, 0, :], ALU.mult)
            V.tensor_tensor(qbar, qbar, gq[:, 1, :], ALU.mult).then_inc(S["far_ops"], 1)
            dve.wait_ge(S["gla_vr"], 8)
            r4 = gr.rearrange("p t (h d) -> p t h d", h=GH)
            link(V.tensor_tensor(r4, r4, bc(bc(sml[:, R_ON:R_ON + 256], 1, GH), 1, NT), ALU.mult))
            dve.wait_ge(S["gla_rstd"], 1)
            for i in range(NT * GH):
                t, h = i // GH, i % GH
                b = bank[GLA_BANKS[i // 2]]
                V.scalar_tensor_tensor(hn[:, t, h * 256:(h + 1) * 256], b[:, i % 2 * 256:(i % 2 + 1) * 256],
                                       ors[:, i:i + 1], gr[:, t, h * 256:(h + 1) * 256], ALU.mult, ALU.mult)\
                 .then_inc(S["mixed"], 1)
            turned(4)
            residual(U_C_OUT)
            if stop < 5:
                return

            norm(3)
            turned(5, 3)
            dve.wait_ge(S["logits"], 1)
            link(V.tensor_copy(lg, bank[0][:, 0:16].rearrange("p (t n) -> p t n", t=NT)))
            for t in range(NT):
                link(V.max(mx[:, t, :], lg[:, t, :]))
                link(V.max_index(mxi[:, t, :], mx[:, t, :], lg[:, t, :]))
            link(V.tensor_copy(idf, mxi[:, :, :]))
            V.tensor_tensor(ee, mx[:, :, 1], mx[:, :, 0], ALU.subtract).then_inc(S["gap"], 1)
            for t in range(NT):
                for w in range(2):
                    V.tensor_scalar(oh[:, w, t, :], iota[:, 0:8], idf[:, t, w:w + 1], None, ALU.is_equal)
            link(V.memset(slot[:, :, :], -1.0))
            V.tensor_tensor(picked, oh[:, 0, :, :], oh[:, 1, :, :], ALU.add).then_inc(S["picked"], 1)
            dve.wait_ge(S["gap_exp"], 1)
            link(V.tensor_scalar(w12[:, :, 0], ee, 1.0, None, ALU.add))
            link(V.reciprocal(w12[:, :, 0], w12[:, :, 0]))
            link(V.tensor_tensor(w12[:, :, 1], w12[:, :, 0], ee, ALU.mult))
            link(V.memset(gate[:, :, :], 0.0))
            for t in range(NT):
                link(V.tensor_scalar(gate[:, t, 0:8], oh[:, 0, t, :], w12[:, t, 0:1], None, ALU.mult))
                link(V.scalar_tensor_tensor(gate[:, t, 0:8], oh[:, 1, t, :], w12[:, t, 1:2], gate[:, t, 0:8],
                                            ALU.mult, ALU.add))
            dve.wait_ge(S["rank"], 1)
            dve.wait_ge(S["picked"], 1)
            link(V.tensor_tensor(slot[:, :, 0:8], bank[1][:, 0:16].rearrange("p (t n) -> p t n", t=NT), picked, ALU.mult))
            link(V.tensor_scalar(slot[:, :, 0:8], slot[:, :, 0:8], -1.0, None, ALU.add))
            link(V.tensor_scalar(over[:, 0, :], bank[1][:, 16:24], float(CAP), None, ALU.is_gt))
            link(V.tensor_tensor_scan(over[:, 1, :], ones[:, 0:8], over[:, 0, :], 0.0, ALU.mult, ALU.add))
            V.tensor_copy(ovf[:, 0:1], over[:, 1, 7:8])
            for r in range(OVER_ROUNDS):
                sel = over[:, 2 + r, :]
                link(V.scalar_tensor_tensor(sel, over[:, 1, :], float(r + 1), over[:, 0, :], ALU.is_equal, ALU.mult))
                for col, shift in ((slot, -float(CAP)), (gate, 0.0)):
                    link(V.tensor_tensor(ovt, col[:, :, 0:8], bc(sel, 1, NT), ALU.mult))
                    link(V.tensor_reduce(col[:, :, NE + r], ovt, AX.X, ALU.add))
                    link(V.tensor_scalar(col[:, :, NE + r], col[:, :, NE + r], shift, None, ALU.add))
                link(V.tensor_tensor(ovt[:, 0, :], iota[:, 0:8], sel, ALU.mult))
                link(V.tensor_reduce(ovf[:, 1 + r:2 + r], ovt[:, 0, :], AX.X, ALU.add))
            V.tensor_copy(ovi[:, :], ovf[0:1, :]).then_inc(S["route"], 1)

            ch = [0]

            def prepare(e):
                V.tensor_copy(cur[:, 0, :].unsqueeze(2), slot[:, :, bass.ds(e + 1, 1)]).then_inc(S["cur"], 1)
                V.tensor_copy(cur[:, 1, :].unsqueeze(2), gate[:, :, bass.ds(e + 1, 1)]).then_inc(S["cur"], 1)
                dve.wait_ge(S["cur"], (e + 1) * 2 + 2)
                V.tensor_scalar(disp[:, 0, :], iota, cur[:, 0, 0:1], None, ALU.is_equal)
                V.tensor_scalar(disp[:, 1, :], iota, cur[:, 0, 1:2], None, ALU.is_equal).then_inc(S["disp"], 1)

            def gathered(e, half):
                dve.wait_ge(S["xg_psum"], (e + 1) * 2 + half + 1)
                gc = R_NORM + NK * 3 + 4 * half
                V.tensor_tensor(xgT[:, half * 4:half * 4 + 4, :], bank[3][:, :].rearrange("p (k n) -> p k n", k=4),
                                bc(sml[:, gc:gc + 4], 2, P), ALU.mult).then_inc(S["xg"], 1)

            def expert(e):
                dve.wait_ge(S["disp"], e + 1)
                V.tensor_scalar(dispg[:, 0, :], disp[:, 0, :], cur[:, 1, 0:1], None, ALU.mult)
                V.tensor_scalar(dispg[:, 1, :], disp[:, 1, :], cur[:, 1, 1:2], None, ALU.mult).then_inc(S["dispg"], 1)
                for c in range(NCH):
                    dve.wait_ge(S["m_silu"], e * NCH + c + 1)
                    V.tensor_tensor(hact[:, c % 2, :], sg[:, c % 2, :], bank[c % 2][:, CH:2 * CH], ALU.mult)\
                     .then_inc(S["m_hact"], 1)
                    if c == 4:
                        dve.wait_ge(S["dispg"], e + 1)
                        prepare(e)
                gathered(e, 0)
                gathered(e, 1)
                for i in range(4):
                    t, half = i // 2, i % 2
                    dve.wait_ge(S["scat"], e * 4 + i + 1)
                    xs = x[:, t, half * BLK:(half + 1) * BLK]
                    V.tensor_tensor(xs, xs, bank[6 + i % 2][:, :], ALU.add).then_inc(S["x_ready"], 1)

            prepare(-1)
            gathered(-1, 0)
            gathered(-1, 1)
            with dve.Fori(0, NE) as e:
                expert(e)
            dve.wait_ge(S["route"], 1)
            n_over = dve.value_load(ovi[0:1, 0:1], min_val=0, max_val=OVER_ROUNDS)
            with dve.Fori(NE, NE + OVER_ROUNDS) as e:
                with dve.If(n_over > e - NE):
                    expert(e)


def pack_blocks(w, order=None):
    rows, cols = w.shape
    n = -(-cols // BLK)
    out = np.zeros((n, rows // P, P, BLK), np.float32)
    for c in range(n):
        part = w[:, c * BLK:(c + 1) * BLK]
        out[c, :, :, :part.shape[1]] = part.reshape(rows // P, P, -1)
    return out.reshape(-1, P, BLK)


def pack_ffn(wg, wu, wd):
    g = wg.reshape(NK, P, NCH, CH).transpose(2, 0, 1, 3)
    u = wu.reshape(NK, P, NCH, CH).transpose(2, 0, 1, 3)
    d = wd.reshape(NCH, 2, P, 2, BLK).transpose(0, 1, 3, 2, 4).reshape(NCH, 4, P, BLK)
    return np.concatenate([np.concatenate([g, u], axis=3), d], axis=1)


def layout(inp):
    a = np.asarray
    w = a(inp["a_w_in"])[0]
    cut = np.cumsum([512, 128, 128, 128, 128, 128, 128, 24, 512, 512, 512])
    qa, kc, vc, ksl, vsl, kwn, vwn, ga, qb, kb, vb, fb = np.split(w, cut, axis=1)
    first = pack_blocks(np.concatenate([kc, vc, ksl, kwn], axis=1))
    second = pack_blocks(np.concatenate([vsl, vwn, ga, fb], axis=1))
    a_in = np.concatenate([first, second] + [pack_blocks(m) for m in (qa, qb, kb, vb)])
    cw = a(inp["c_w_in"])[0]
    parts = [a_in, pack_blocks(a(inp["a_w_out"])[0]),
             pack_ffn(a(inp["f_w_gate"])[0], a(inp["f_w_up"])[0], a(inp["f_w_down"])[0]).reshape(-1, P, BLK),
             pack_blocks(cw[:, 0:3072]), pack_blocks(a(inp["c_w_out"])[0])]
    order = []
    for c in range(NCH):
        order += [(c, b) for b in range(8)]
        if c:
            order += [(c - 1, b) for b in range(8, 12)]
    order += [(NCH - 1, b) for b in range(8, 12)]
    ci, bi = np.array([o[0] for o in order]), np.array([o[1] for o in order])
    stream = np.empty((U_END, P, UB * BLK), np.float32)
    front = np.concatenate(parts)
    stream[0:U_MOE] = front.reshape(U_MOE, UB, P, BLK).transpose(0, 2, 1, 3).reshape(U_MOE, P, UB * BLK)
    for e in range(NE):
        blocks = pack_ffn(a(inp["m_w_gate"])[0, e], a(inp["m_w_up"])[0, e], a(inp["m_w_down"])[0, e])[ci, bi]
        at = U_MOE + e * EXP_UNITS
        stream[at:at + EXP_UNITS] = blocks.reshape(EXP_UNITS, UB, P, BLK).transpose(0, 2, 1, 3)\
            .reshape(EXP_UNITS, P, UB * BLK)
    small = np.zeros((P, R_END), np.float32)
    for at, name in ((R_QN, "a_q_norm"), (R_KN, "a_k_norm"), (R_FQ, "a_fox_q_norm"), (R_FK, "a_fox_k_norm"),
                     (R_ON, "c_o_norm"), (R_GB, "a_gate_bias"), (R_FB, "a_fox_f_bias")):
        v = a(inp[name])[0]
        small[:, at:at + v.shape[0]] = v[None, :]
    for i, name in enumerate(("a_norm", "f_norm", "c_norm", "m_norm")):
        small[:, R_NORM + NK * i:R_NORM + NK * (i + 1)] = a(inp[name])[0].reshape(NK, P).T
    small[:, R_BA:R_BA + GH] = a(inp["c_b_a"])[0].reshape(GH, P).T
    small[:, R_ROUTER:R_ROUTER + NK * NE] = a(inp["m_router"])[0].reshape(NK, P, NE).transpose(1, 0, 2).reshape(P, -1)
    small[:, R_A1:R_A1 + NK * 16] = cw[:, 3072:3088].reshape(NK, P, 16).transpose(1, 0, 2).reshape(P, -1)
    for v, name in enumerate(("a_pe_k", "a_pe_v")):
        small[:, R_PE + 16 * v:R_PE + 16 * (v + 1)] = a(inp[name])[0].reshape(16, P).T
    comp = np.zeros((P, 2176), np.float32)
    for v, c in enumerate("kv"):
        comp[:, 1024 * v:1024 * (v + 1)] = a(inp[f"a_cmp_{c}_w1"])[0].reshape(16, P, HD).transpose(1, 0, 2).reshape(P, -1)
        comp[0:HD, 2048 + HD * v:2048 + HD * (v + 1)] = a(inp[f"a_cmp_{c}_w2"])[0]
    return {"x": a(inp["x"])[0], "weights": stream, "constants": constants(), "masks": masks(), "small": small,
            "compress": comp, "w_a2": a(inp["c_w_a2"])[0]}


ARENA = 20000
CONST_DMAS = 2
GLA_BANKS = (5, 6, 7, 0)
LIMITS = {1: U_A_OUT, 2: U_FFN, 3: U_C_IN, 4: U_MOE, 5: U_END}


def kernel(**inputs):
    import concourse.bacc as bacc
    from concourse.bass_utils import run_bass_kernel_spmd

    nc = bacc.Bacc("TRN2", target_bir_lowering=False, num_devices=1)
    arrays = {k: np.ascontiguousarray(v) for k, v in layout(inputs).items()}
    d = {k: nc.dram_tensor("in_" + k, v.shape, mybir.dt.from_np(v.dtype), kind="ExternalInput").ap()
         for k, v in arrays.items()}
    out = nc.dram_tensor("out", (SEQ, DM), F32, kind="ExternalOutput").ap()
    trunk(nc, d["x"], d["weights"], d["constants"], d["masks"], d["small"], d["compress"], d["w_a2"], out, STOP)
    r = run_bass_kernel_spmd(nc, [{"in_" + k: v for k, v in arrays.items()}], core_ids=[0])
    return r.results[0]["out"].reshape(1, SEQ, DM)


STOP = 5
```

```python
from contextlib import ExitStack

import concourse.bass as bass
import numpy as np
from concourse import mybir

F32 = mybir.dt.float32
F32R = mybir.dt.float32r
BF16 = mybir.dt.bfloat16
I32 = mybir.dt.int32
U32 = mybir.dt.uint32
ALU = mybir.AluOpType
ACT = mybir.ActivationFunctionType
AX = mybir.AxisListType

P = 128
SEQ, DM = 256, 1024
NT = SEQ // P
NK = DM // P
HD = 64
NH = 8
NG = 2
NCMP = 15
EPS = 1e-6
NEG = -1e30
DFF = 2816
CH = 256
NCH = DFF // CH
BLK = 512
UB = 4
RAW = 6
SPLIT = 3
NE = 8
CAP = 128
SCATTER, TURN, GATHER = 3, 5, 7
OVER_ROUNDS = 3
GH = 4
GB = 8
NGB = P // GB

A_IN_CG, C_IN_CG = 6, 6
U_A_IN = 0
U_A_OUT = U_A_IN + A_IN_CG * NK // UB
U_FFN = U_A_OUT + 2 * NK // UB
CHUNK_UNITS = (NK + 4) // UB
U_C_IN = U_FFN + NCH * CHUNK_UNITS
U_C_OUT = U_C_IN + C_IN_CG * NK // UB
U_MOE = U_C_OUT + 2 * NK // UB
EXP_UNITS = NCH * CHUNK_UNITS
U_END = U_MOE + NE * EXP_UNITS
W_END = U_END + 6
EXP_ORDER = [0, 1, 3, 4] + [3 * c + i for c in range(2, NCH) for i in (0, 1, 2)] + [3 * NCH + 2, 3 * NCH + 5]
HOLES = (U_MOE + 2, U_MOE + 4, U_END - 2, U_END - 2, U_END - 1, U_END - 1)
FRONT_WIDTH = {1: 288}

C_ID, C_TRI, C_ONES, C_IOTA, C_BD = 0, 128, 256, 384, 512
C_SEL = 640
C_ROPE = C_SEL + GB + P
C_CROPE = C_ROPE + NT * 32
C_CBIAS = C_CROPE + 32
C_CMASK = C_CBIAS + NT * 16
C_HMASK = C_CMASK + NT * 16
C_REP = C_HMASK + 8
C_END = C_REP + 2 * P
R_QN, R_KN, R_FQ, R_FK, R_ON, R_GB, R_FB = 0, 64, 128, 192, 256, 512, 536
R_NORM = 544
R_BA = R_NORM + 4 * NK
R_ROUTER = R_BA + GH
R_A1 = R_ROUTER + NK * NE
R_PE = R_A1 + NK * 16
R_END = R_PE + 2 * 16


def constants():
    c = np.zeros((P, C_END), np.float32)
    i = np.arange(P)
    c[:, C_ID:C_ID + P] = np.eye(P)
    c[:, C_TRI:C_TRI + P] = i[:, None] <= i[None, :]
    c[:, C_ONES:C_ONES + P] = 1.0
    c[:, C_IOTA:C_IOTA + P] = i[None, :]
    c[:, C_BD:C_BD + P] = (i[:, None] <= i[None, :]) & (i[:, None] // GB == i[None, :] // GB)
    c[:, C_SEL:C_SEL + GB + P] = np.arange(GB + P)[None, :] % GB == 0
    inv = np.float32(500000.0) ** (-np.arange(0, 16, 2, dtype=np.float32) / np.float32(16))

    def rope(pos):
        ang = pos.astype(np.float32)[:, None] * inv[None, :].astype(np.float32)
        co, si = np.cos(ang), np.sin(ang)
        return np.concatenate([co, co, -si, si], axis=1).astype(np.float32)

    for t in range(NT):
        c[:, C_ROPE + 32 * t:C_ROPE + 32 * (t + 1)] = rope(t * P + i)
    ends = np.arange(NCMP) * 16 + 31
    c[0:NCMP, C_CROPE:C_CROPE + 32] = rope(ends)
    c[NCMP:2 * NCMP, C_CROPE:C_CROPE + 32] = rope(ends)
    for t in range(NT):
        seen = (ends[None, :] <= (t * P + i)[:, None])
        c[:, C_CBIAS + 16 * t:C_CBIAS + 16 * t + NCMP] = np.where(seen, 0.0, NEG)
        c[:, C_CMASK + 16 * t:C_CMASK + 16 * t + NCMP] = seen
    c[:, C_HMASK:C_HMASK + 8] = i[:, None] // 16 == np.arange(8)[None, :]
    for g in range(NG):
        rep = (i[:, None] == i[None, :] % 16) & (i[None, :] // 64 == g) & (i[:, None] < NCMP)
        c[:, C_REP + g * P:C_REP + (g + 1) * P] = rep
    return c


def masks():
    i = np.arange(P)
    m = np.zeros((P, 1024 + P), np.float32)
    late = np.where(i[:, None] >= i[None, :], 0.0, NEG)
    for h in range(4):
        m[:, h * P:(h + 1) * P] = late
    m[:, 512 + 128:512 + 256] = late
    m[:, 512 + 384:512 + 512] = late
    m[:, 1024:1024 + P] = np.eye(P)
    return (m.view(np.uint32) >> 16).astype(np.uint16)


def trunk(nc, x_d, w_d, const_d, mask_d, small_d, comp_d, wa2_d, out_d, stop=99):
    ctx = ExitStack()
    with ctx:
        def sb(name, shape, dt=F32):
            return ctx.enter_context(nc.sbuf_tensor(name, shape, dt))

        def sem(name):
            return ctx.enter_context(nc.semaphore(name))

        raw = sb("raw", [P, RAW, UB, BLK])
        whi = sb("whi", [P, SPLIT, UB, BLK], F32R)
        wlo = sb("wlo", [P, SPLIT, UB, BLK], F32R)
        x = sb("x", [P, NT, DM])
        hn = sb("hn", [P, NT, DM])
        hT_hi = sb("hT_hi", [P, NK, SEQ], F32R)
        hT_lo = sb("hT_lo", [P, NK, SEQ], F32R)
        swhi = sb("swhi", [P, 192], F32R)
        swlo = sb("swlo", [P, 192], F32R)
        cst = sb("cst", [P, C_END])
        msk_bits = sb("msk_bits", [P, 1024 + P], mybir.dt.uint16)
        msk = msk_bits[:, :].bitcast(BF16)
        sml = sb("sml", [P, R_END])
        wa2 = sb("wa2", [16, 512])
        ss = sb("ss", [P, NT])
        rstd = sb("rstd", [P, NT])
        mhalf = sb("mhalf", [P, 32])
        esc = sb("esc", [P, 2, 512])
        oss = sb("oss", [P, NT * GH])
        ors = sb("ors", [P, NT * GH])
        mxi = sb("mxi", [P, 2, 8], U32)
        ovi = sb("ovi", [1, 4], I32)
        arena_ctx = ExitStack()
        arena = arena_ctx.enter_context(nc.sbuf_tensor("arena", [P, ARENA], F32))

        class Carve:
            def __init__(self):
                self.at = 0

            def __call__(self, n, dt=F32):
                a = arena[:, self.at:self.at + n]
                self.at += n
                assert self.at <= ARENA, self.at
                return a

        ident = cst[:, C_ID:C_ID + P]
        tri = cst[:, C_TRI:C_TRI + P]
        ones = cst[:, C_ONES:C_ONES + P]
        iota = cst[:, C_IOTA:C_IOTA + P]
        mbd = cst[:, C_BD:C_BD + P]
        mident = msk[:, 1024:1024 + P]

        bank = [ctx.enter_context(nc.psum_tensor(f"bank{i}", [P, 512], F32)) for i in range(8)]

        c0 = Carve()
        front = c0(A_IN_CG * NT * BLK)
        proj4 = front.rearrange("p (c t n) -> p c t n", c=A_IN_CG, t=NT)
        proj = [proj4[:, i, :, :] for i in (5, 0, 2, 3, 4, 1)]
        qT = c0(NH * SEQ).rearrange("p (h n) -> p h n", h=NH)
        keyT = c0(4 * SEQ).rearrange("p (h n) -> p h n", h=4)
        fqT = front[:, 2048:4096].rearrange("p (h n) -> p h n", h=NH)
        fkT = front[:, 4096:6144].rearrange("p (h n) -> p h n", h=NH)
        scr0 = c0.at
        cw1 = c0(2 * 16 * HD).rearrange("p (v j d) -> p v j d", v=2, j=16)
        cw2 = c0(2 * HD).rearrange("p (v d) -> p v d", v=2)
        kc2 = esc[:, :, :].rearrange("p b n -> p (b n)").rearrange("p (v g n) -> p v g n", v=2, g=NG)
        blkT = c0(2 * 16 * 30).rearrange("p (v j g n) -> p v j g n", v=2, j=16, g=NG)
        assert c0.at - scr0 >= 2560
        pbuf = arena[:, scr0:scr0 + 1024].rearrange("p (b n) -> p b n", b=2)
        ptb = arena[:, scr0 + 1024:scr0 + 2048].rearrange("p (b n) -> p b n", b=2)
        tmpo = arena[:, scr0 + 2048:scr0 + 2560]
        sq = hn[:, :, :].rearrange("p t n -> p (t n)")
        faug = arena[:, scr0:scr0 + 2 * NT * NH * 66].rearrange("p (w t h n) -> p w t h n", w=2, t=NT, h=NH)
        hss = c0(6 * 32).rearrange("p (w n) -> p w n", w=6)
        hrs = c0(6 * 32).rearrange("p (w n) -> p w n", w=6)
        rA = c0(256)
        rB = c0(256)
        gel = c0(4 * 64).rearrange("p (w n) -> p w n", w=4)
        kcm = c0(4 * 64).rearrange("p (w n) -> p w n", w=4)
        kcmpT = c0(32)
        vcmp = c0(2 * 64).rearrange("p (g d) -> p g d", g=2)
        vbd = c0(512)
        fz = c0(5 * 16).rearrange("p (w n) -> p w n", w=5)
        gat = c0(48)
        sc = c0(2 * 128).rearrange("p (t n) -> p t n", t=2)
        mc = c0(16)
        sumc = c0(16)
        facc = c0(16)
        pcT = c0(256).rearrange("p (t n) -> p t n", t=2)
        negm = c0(6 * 8).rearrange("p (s h) -> p s h", s=6)
        sums = c0(6 * 8).rearrange("p (s h) -> p s h", s=6)
        fac = c0(6 * 8).rearrange("p (s h) -> p s h", s=6)
        oacc = hn

        cg_ = Carve()
        gq = cg_(NT * 512).rearrange("p (t n) -> p t n", t=NT)
        gk = cg_(NT * 512).rearrange("p (t n) -> p t n", t=NT)
        gb = cg_(NT * 512).rearrange("p (t n) -> p t n", t=NT)
        gv = hn
        prod = cg_(GB * 512).rearrange("p (s n) -> p s n", s=GB)
        kt = cg_((NGB - 1) * 512).rearrange("p (i n) -> p i n", i=NGB - 1)
        gr = kt[:, 0:4, :].rearrange("p i n -> p (i n)").rearrange("p (t n) -> p t n", t=NT)
        gqt = cg_(512)
        att = prod[:, 0:2, :]
        kbar, qbar, far = prod[:, 2, :], prod[:, 3, :], prod[:, 4, :]
        a1T = cg_(SEQ)
        gz = prod[:, 0:2, :].rearrange("p s n -> p (s n)")
        ge = prod[:, 2:4, :].rearrange("p s n -> p (s n)")
        rmask = prod[:, 4:6, :].rearrange("p s n -> p (s n)")

        arena_ctx.close()
        sg = sb("sg", [P, 2, CH])
        hact = sb("hact", [P, 2, CH])
        h2_hi = sb("h2_hi", [P, 2, CH], F32R)
        h2_lo = sb("h2_lo", [P, 2, CH], F32R)
        hn_hi = sb("hn_hi", [P, NT, DM], F32R)
        hn_lo = sb("hn_lo", [P, NT, DM], F32R)
        y_hi = sb("y_hi", [P, DM], F32R)
        y_lo = sb("y_lo", [P, DM], F32R)
        disp = sb("disp", [P, NT, P], F32R)
        combT = sb("combT", [P, NT, P], F32R)
        gslot = sb("gslot", [P, 1])
        mtab = sb("mtab", [P, 400])
        tab_at = [0]

        def cf(n):
            a_ = mtab[:, tab_at[0]:tab_at[0] + n]
            tab_at[0] += n
            return a_

        lg = cf(16).rearrange("p (t n) -> p t n", t=2)
        mx = cf(16).rearrange("p (t n) -> p t n", t=2)
        idf = cf(16).rearrange("p (t n) -> p t n", t=2)
        ee = cf(2)
        w12 = cf(4).rearrange("p (t n) -> p t n", t=2)
        oh = cf(2 * 16).rearrange("p (w t n) -> p w t n", w=2, t=2)
        gate = cf(24).rearrange("p (t n) -> p t n", t=2)
        slot = cf(24).rearrange("p (t n) -> p t n", t=2)
        picked = cf(16).rearrange("p (t n) -> p t n", t=2)
        cur = cf(4).rearrange("p (w t) -> p w t", w=2)
        over = cf(8 * 8).rearrange("p (w n) -> p w n", w=8)
        ovt = cf(16).rearrange("p (t n) -> p t n", t=2)
        ovf = cf(4)

        NAMES = """hn_lo w_hi w_lo tmp hT_hi sw_hi sw_lo hn_hi a1T_psum y_hi xg_tmp xg_hi h2_hi m_h2_hi gslot_psum x_in const_in late_in units_used x_ready ss rstd hn hT_psum hT dve_chain act_chain pool_chain
            proj kc_psum kc blk hid hid_in tanh gelu cmp2 cmp2_sb kcmp_ss kcmp_rstd kcmp kcmpT_psum kcmpT
            vrep vbd head_ss head_rstd head_done gate_z gate_e fox_z fox_l fox_lf cum aug
            headT_psum headT foxT_psum foxT cmp_s cmp_d cmp_e cmp_p cmp_pT_psum cmp_pT cmp_o
            scores rowmax probs probsT_psum probsT pv o_done
            gu silu hact h2T_psum h2T
            a1 a1_sb z zb absz soft decay gla_qk gla_vr prod_zero kt_zero diag_arg diag_exp prod diag
            k_arg k_exp kt q_arg q_exp qt cross att far_arg far_exp far_ops far_psum far_sb
            gla_o gla_ss gla_rstd mixed
            logits top gap gap_exp picked rank route disp dispg combT_psum combT xg_psum xg
            cur m_silu m_hact m_h2T_psum m_h2T ysb scat out""".split()
        S = {n: sem(n) for n in NAMES}
        s_loaded = [sem(f"loaded{i}") for i in range(RAW)]

        def loads_before(slot_, u):
            return len(range(slot_, u, RAW))

        att_units = []
        for br in range(3):
            for t in range(NT):
                n = 4 if t == 0 else 2
                att_units += [(br, t, h0, n) for h0 in range(0, NH, n)]
        AU = len(att_units)

        def seq_of(u):
            return att_units[u][0] * NT + att_units[u][1]

        ends_seq = [u for u in range(AU) if u == AU - 1 or seq_of(u + 1) != seq_of(u)]
        steps = [(c, t) for c in range(NCH) for t in range(NT)]
        X_MOE = 12

        def dense_g(c, half):
            return half if c == 0 else 3 * c - 1 + half

        def dense_d(c):
            return 4 + 3 * c if c < NCH - 1 else EXP_UNITS - 1

        def pos_g(c, half, fresh):
            return (2 * c if fresh and c < 2 else 3 * c - 2) + half

        def pos_d(c, drain):
            return EXP_UNITS - NCH + c if drain and c >= NCH - 2 else 3 * c + 6

        def loads_main(e, base, pos):
            return e * (16 * EXP_UNITS // RAW) + 16 * ((base + pos) // RAW + 1)

        def loads_over(e, pos):
            sl = (U_END + pos) % RAW
            per_round = len(range(pos % RAW, EXP_UNITS, RAW))
            return (e - NE) * (16 * per_round) + 16 * (loads_before(sl, U_END) + pos // RAW + 1)

        block = ctx.enter_context(nc.Block())

        @block.sync
        def _(sp):
            def fetch(u):
                hole = sum(u >= at for at in HOLES)
                sp.dma_start(raw[:, u % RAW, :, :], w_d[u + hole, :, :].rearrange("p (b n) -> p b n", b=UB))\
                  .then_inc(s_loaded[u % RAW], 16)

            sp.dma_start(x[:, :, :], x_d.rearrange("(t p) n -> p t n", p=P)).then_inc(S["x_in"], 16)
            for dst, src in ((cst[:, :], const_d[:, :]), (sml[:, :], small_d[:, :])):
                sp.dma_start(dst, src).then_inc(S["const_in"], 16)
            fetch(0)
            fetch(1)
            for dst, src in ((arena[:, scr0:scr0 + 2176], comp_d[:, :]), (msk_bits[:, :], mask_d[:, :]),
                             (wa2[:, :], wa2_d[:, :])):
                sp.dma_start(dst, src).then_inc(S["late_in"], 16)
            for u in range(2, RAW):
                fetch(u)
            def stream(first, last, hole):
                with sp.Fori(first, last) as it:
                    for s_ in range(RAW):
                        sp.wait_ge(S["w_lo"], (it - 1) * RAW + s_ + 1)
                        sp.dma_start(raw[:, s_, :, :], w_d[bass.ds(it * RAW + (s_ + hole), 1), :, :]
                                     .rearrange("a p (b n) -> p (a b) n", b=UB)).then_inc(s_loaded[s_], 16)

            def single(u):
                sp.wait_ge(S["w_lo"], u - RAW + 1)
                fetch(u)

            if stop < 5:
                for u in range(RAW, LIMITS[stop]):
                    single(u)
            else:
                before, behind = (U_MOE + 2) // RAW, -(-(U_MOE + 4) // RAW)
                stream(1, before, 0)
                for u in range(before * RAW, behind * RAW):
                    single(u)
                stream(behind, U_END // RAW, 2)
                for u in range(U_END // RAW * RAW, U_END):
                    single(u)
            if stop < 5:
                sp.wait_ge(S["x_ready"], 4 * (stop - 1))
            else:
                sp.wait_ge(S["route"], 1)
                n_over = sp.value_load(ovi[0:1, 0:1], min_val=0, max_val=OVER_ROUNDS)
                with sp.Fori(0, OVER_ROUNDS) as r:
                    with sp.If(n_over > r):
                        who = sp.value_load(ovi[0:1, bass.ds(r + 1, 1)], min_val=0, max_val=NE - 1)
                        for i, at in enumerate(EXP_ORDER):
                            sp.wait_ge(S["w_lo"], r * EXP_UNITS + (U_END + max(0, i - RAW + 1)))
                            sl = (U_END + i) % RAW
                            sp.dma_start(raw[:, sl, :, :],
                                         w_d[bass.ds(who * EXP_UNITS + (U_MOE + at), 1), :, :]
                                         .rearrange("a p (b n) -> p (a b) n", b=UB)).then_inc(s_loaded[sl], 16)
                sp.wait_ge(S["x_ready"], n_over * 4 + (X_MOE + 4 * NE))
            sp.dma_start(out_d.rearrange("(t p) n -> p t n", p=P), x[:, :, :]).then_inc(S["out"], 16)
            sp.wait_ge(S["out"], 16)

        @block.gpsimd
        def _(pool):
            chain = [0]

            def link(ins):
                chain[0] += 1
                ins.then_inc(S["pool_chain"], 1)
                pool.wait_ge(S["pool_chain"], chain[0])

            def inv_root(out, in_, width, n, done):
                r = in_.shape[0]
                link(nc.gpsimd.tensor_scalar(in_, in_, 1.0 / width, EPS, ALU.mult, ALU.add))
                nc.gpsimd.tensor_tensor(out, in_, mhalf[0:r, 0:n], ALU.pow).then_inc(S[done], 1)

            link(nc.gpsimd.memset(mhalf[:], -0.5))

            def norm(n):
                pool.wait_ge(S["ss"], NT * (n + 1))
                inv_root(rstd[:], ss[:], DM, NT, "rstd")

            norm(0)
            for i, n in enumerate((8, 16, 16, 16)):
                pool.wait_ge(S["head_ss"], i + 1)
                inv_root(hrs[:, i, 0:n], hss[:, i, 0:n], HD, n, "head_rstd")
                if i == 1:
                    pool.wait_ge(S["kcmp_ss"], 1)
                    inv_root(hrs[0:30, 4, 0:1], hss[0:30, 4, 0:1], HD, 1, "kcmp_rstd")
            if stop >= 3:
                norm(1)
            if stop >= 4:
                norm(2)
                pool.wait_ge(S["x_ready"], 8)
                nc.gpsimd.memset(kt, 0.0).then_inc(S["kt_zero"], 1)
                pool.wait_ge(S["decay"], 1)
                nc.gpsimd.memset(prod, 0.0).then_inc(S["prod_zero"], 1)
                pool.wait_ge(S["gla_ss"], NT * GH)
                inv_root(ors[:], oss[:], 256, NT * GH, "gla_rstd")
            if stop >= 5:
                norm(3)

        @block.tensor
        def _(pe):
            mm = nc.tensor.matmul

            def mm3(out_, a_hi, a_lo, b_hi, b_lo, start, stop):
                mm(out_, a_hi, b_hi, start=start, stop=False)
                mm(out_, a_hi, b_lo, start=False, stop=False)
                return mm(out_, a_lo, b_hi, start=False, stop=stop)

            def transposes(g, ready):
                for i in range(4):
                    t, half = i // 2, i % 2
                    ready(t)
                    for j in range(4):
                        k = half * 4 + j
                        last = nc.tensor.transpose(bank[i][:, j * P:(j + 1) * P], hn[:, t, k * P:(k + 1) * P], ident)
                    last.then_inc(S["hT_psum"], 1)

            def normed(n):
                return lambda t: pe.wait_ge(S["hn"], NT * n + t + 1)

            def block_at(u0, b):
                u = u0 + b // UB
                return whi[:, u % SPLIT, b % UB, :], wlo[:, u % SPLIT, b % UB, :]

            def group(u0, cg, banks, width=BLK):
                for k in range(NK):
                    b = cg * NK + k
                    if b % UB == 0:
                        pe.wait_ge(S["w_lo"], u0 + b // UB + 1)
                    w_h, w_l = block_at(u0, b)
                    for t in range(NT):
                        last = mm3(bank[banks[t]][:, 0:width], hT_hi[:, k, t * P:(t + 1) * P],
                                   hT_lo[:, k, t * P:(t + 1) * P], w_h[:, 0:width], w_l[:, 0:width],
                                   k == 0, k == NK - 1)
                    if b % UB == UB - 1:
                        last.then_inc(S["units_used"], 1)

            pe.wait_ge(S["const_in"], CONST_DMAS * 16)
            transposes(0, normed(0))
            pe.wait_ge(S["hT"], 4)

            def in_group(cg):
                if cg >= 2:
                    pe.wait_ge(S["proj"], 2 * (cg - 1))
                b = 4 + 2 * (cg % 2)
                group(U_A_IN, cg, (b, b + 1), FRONT_WIDTH.get(cg, BLK))

            in_group(0)
            in_group(1)
            pe.wait_ge(S["proj"], 2)
            for v in range(2):
                for g in range(NG):
                    for t in range(NT):
                        last = nc.tensor.transpose(bank[v][0:HD, (g * NT + t) * P:(g * NT + t + 1) * P],
                                                   proj[0][:, t, v * P + g * HD:v * P + (g + 1) * HD], ident)
                last.then_inc(S["kc_psum"], 1)
            in_group(2)
            pe.wait_ge(S["late_in"], 48)
            pe.wait_ge(S["blk"], 4)
            for v in range(2):
                for j in range(16):
                    last = mm(bank[2][0:HD, v * 32:v * 32 + 30], cw1[:, v, j, :],
                              blkT[:, v, j, :, :].rearrange("p g n -> p (g n)"), start=(j == 0), stop=(j == 15))
            last.then_inc(S["hid"], 1)
            pe.wait_ge(S["head_done"], 1)
            pe.wait_ge(S["kc"], 4)
            for t in range(NT):
                for kk in range(4):
                    last = nc.tensor.transpose(bank[t][0:HD, kk * P:(kk + 1) * P],
                                               proj[0][:, t, 256 + kk * HD:256 + (kk + 1) * HD], ident)
                last.then_inc(S["headT_psum"], 1)
            in_group(3)
            pe.wait_ge(S["gelu"], 1)
            mm(bank[3][0:30, 0:HD], gel[0:HD, 3, 0:30], cw2[0:HD, 0, :], start=True, stop=True)
            for g in range(NG):
                last = mm(bank[3][0:NCMP, (g + 1) * HD:(g + 2) * HD], gel[0:HD, 3, 30 + NCMP * g:30 + NCMP * (g + 1)],
                          cw2[0:HD, 1, :], start=True, stop=True)
            last.then_inc(S["cmp2"], 1)
            in_group(4)
            pe.wait_ge(S["cmp2_sb"], 1)
            for g in range(NG):
                last = mm(bank[2][:, 0:HD], cst[0:NCMP, C_REP + g * P:C_REP + (g + 1) * P], vcmp[0:NCMP, g, :],
                          start=(g == 0), stop=(g == NG - 1))
            last.then_inc(S["vrep"], 1)
            pe.wait_ge(S["kcmp"], 1)
            nc.tensor.transpose(bank[3][0:HD, 256:286], kcm[0:30, 3, :], ident[0:30, 0:30]).then_inc(S["kcmpT_psum"], 1)
            in_group(5)
            pe.wait_ge(S["head_done"], 2)
            pe.wait_ge(S["vbd"], 1)
            pe.wait_ge(S["kcmpT"], 1)
            for i in range(4):
                t, half = i // 2, i % 2
                if i < 2:
                    pe.wait_ge(S["headT"], i + 1)
                for j in range(4):
                    h = half * 4 + j
                    last = nc.tensor.transpose(bank[i][0:HD, j * P:(j + 1) * P],
                                               proj[2][:, t, h * HD:(h + 1) * HD], ident)
                last.then_inc(S["headT_psum"], 1)
            pe.wait_ge(S["headT"], 3)
            pe.wait_ge(S["fox_lf"], 1)
            mm(bank[0][:, 0:8], tri, fz[:, 4, 0:8], start=True, stop=True)
            mm(bank[0][:, 8:16], ones, fz[:, 4, 0:8], start=True, stop=False)
            mm(bank[0][:, 8:16], tri, fz[:, 4, 8:16], start=False, stop=True).then_inc(S["cum"], 1)
            pe.wait_ge(S["proj"], 12)
            pe.wait_ge(S["headT"], 6)
            for t in range(NT):
                for h in range(NH):
                    g = h // 4
                    last = mm(bank[6][:, t * P + h * 16:t * P + h * 16 + NCMP], qT[0:HD, h, t * P:(t + 1) * P],
                              kcmpT[0:HD, g * NCMP:(g + 1) * NCMP], start=True, stop=True)
            last.then_inc(S["cmp_s"], 1)
            pe.wait_ge(S["aug"], 1)
            for i in range(8):
                w, t, half = i // 4, i // 2 % 2, i % 2
                if i % 4 == 0:
                    pe.wait_ge(S["head_done"], 3 + w)
                if i >= 4:
                    pe.wait_ge(S["foxT"], i - 3)
                for j in range(4):
                    h = half * 4 + j
                    last = nc.tensor.transpose(bank[i % 4][0:66, j * P:(j + 1) * P], faug[:, w, t, h, :], ident)
                last.then_inc(S["foxT_psum"], 1)
            pe.wait_ge(S["cmp_p"], 1)
            for t in range(NT):
                last = nc.tensor.transpose(bank[7][:, t * P:(t + 1) * P], sc[:, t, :], ident)
            last.then_inc(S["cmp_pT_psum"], 1)
            pe.wait_ge(S["cmp_pT"], 1)
            for t in range(NT):
                mm(bank[4 + t][:, :], pcT[:, t, :], vbd, start=True, stop=True).then_inc(S["cmp_o"], 1)

            def qk(u):
                br, t, h0, n = att_units[u]
                kw = (t + 1) * P
                if u >= 2:
                    pe.wait_ge(S["probs"], u - 1)
                mm(bank[u % 2][:, :], mident, msk[:, 512 * t:512 * t + 512], start=True, stop=False)
                for j in range(n):
                    h = h0 + j
                    if br < 2:
                        q, k = qT[0:HD, h, t * P:(t + 1) * P], keyT[0:HD, br * 2 + h // 4, 0:kw]
                    else:
                        q, k = fqT[0:66, h, t * P:(t + 1) * P], fkT[0:66, h, 0:kw]
                    last = mm(bank[u % 2][:, j * kw:(j + 1) * kw], q, k, start=False, stop=(j == n - 1))
                last.then_inc(S["scores"], 1)

            def turn(u):
                pe.wait_ge(S["probs"], u + 1)
                if u >= 2:
                    pe.wait_ge(S["probsT"], u - 1)
                for j in range(4):
                    last = nc.tensor.transpose(bank[2 + u % 2][:, j * P:(j + 1) * P],
                                               pbuf[:, u % 2, j * P:(j + 1) * P], ident)
                last.then_inc(S["probsT_psum"], 1)

            def pv(u):
                br, t, h0, n = att_units[u]
                sq_ = seq_of(u)
                pe.wait_ge(S["probsT"], u + 1)
                if u == 0 or seq_of(u - 1) != sq_:
                    pe.wait_ge(S["o_done"], sq_ + 1)
                for j in range(n):
                    h = h0 + j
                    for kt_ in range(t + 1):
                        if br < 2:
                            v = proj[1][:, kt_, br * P + (h // 4) * HD:br * P + (h // 4 + 1) * HD]
                        else:
                            v = proj[5][:, kt_, h * HD:(h + 1) * HD]
                        m = j * (t + 1) + kt_
                        last = mm(bank[4 + sq_ % 2][:, h * HD:(h + 1) * HD], ptb[:, u % 2, m * P:(m + 1) * P], v,
                                  start=(kt_ == 0), stop=(kt_ == t))
                last.then_inc(S["pv"], 1)

            pe.wait_ge(S["foxT"], 8)
            qk(0)
            for u in range(AU):
                if u + 1 < AU:
                    qk(u + 1)
                turn(u)
                if u >= 1:
                    pv(u - 1)
            pv(AU - 1)
            transposes(1, lambda t: pe.wait_ge(S["o_done"], 8))
            if stop < 2:
                return
            pe.wait_ge(S["hT"], 8)
            group(U_A_OUT, 0, (4, 5))
            group(U_A_OUT, 1, (6, 7))
            if stop < 3:
                return
            transposes(2, normed(1))
            pe.wait_ge(S["hT"], 12)

            def gate_up(i, half):
                c, t = steps[i]
                u = U_FFN + dense_g(c, half)
                if t == 0:
                    pe.wait_ge(S["w_lo"], u + 1)
                if half == 0 and i >= 2:
                    pe.wait_ge(S["hact"], i - 1)
                for k in range(4 * half, 4 * half + 4):
                    last = mm3(bank[i % 2][:, :], hT_hi[:, k, t * P:(t + 1) * P], hT_lo[:, k, t * P:(t + 1) * P],
                               *block_at(u, k % 4), k == 0, k == NK - 1)
                if t == 1:
                    last.then_inc(S["units_used"], 1)
                elif half:
                    last.then_inc(S["gu"], 1)

            def hidden_T(i):
                pe.wait_ge(S["hact"], i + 1)
                if i:
                    pe.wait_ge(S["h2T"], i)
                for j in range(2):
                    last = nc.tensor.transpose(bank[2][:, j * P:(j + 1) * P], hact[:, i % 2, j * P:(j + 1) * P], ident)
                last.then_inc(S["h2T_psum"], 1)

            def down(i):
                c, t = steps[i]
                u = U_FFN + dense_d(c)
                if t == 0:
                    pe.wait_ge(S["w_lo"], u + 1)
                pe.wait_ge(S["h2T"], i + 1)
                for j in range(2):
                    for half in range(2):
                        last = mm3(bank[4 + 2 * t + half][:, :], h2_hi[:, i % 2, j * P:(j + 1) * P],
                                   h2_lo[:, i % 2, j * P:(j + 1) * P], *block_at(u, 2 * j + half),
                                   c == 0 and j == 0, c == NCH - 1 and j == 1)
                if t == 1:
                    last.then_inc(S["units_used"], 1)

            n = len(steps)
            for i in range(n):
                gate_up(i, 0)
                gate_up(i, 1)
                if i >= 1:
                    hidden_T(i - 1)
                if i >= 2:
                    down(i - 2)
            down(n - 2)
            hidden_T(n - 1)
            down(n - 1)
            if stop < 4:
                return

            transposes(3, normed(2))
            pe.wait_ge(S["hT"], 16)
            pe.wait_ge(S["sw_lo"], 1)
            for t in range(NT):
                for k in range(NK):
                    w = slice(64 + 16 * k, 64 + 16 * (k + 1))
                    last = mm3(bank[6][:, 16 * t:16 * (t + 1)], hT_hi[:, k, t * P:(t + 1) * P],
                               hT_lo[:, k, t * P:(t + 1) * P], swhi[:, w], swlo[:, w], k == 0, k == NK - 1)
            last.then_inc(S["a1"], 1)

            def channels(cg, b0):
                for k in range(NK):
                    b = cg * NK + k
                    if b % UB == 0:
                        pe.wait_ge(S["w_lo"], U_C_IN + b // UB + 1)
                    w_h, w_l = block_at(U_C_IN, b)
                    for m in range(GH):
                        c = slice(m * P, (m + 1) * P)
                        last = mm3(bank[b0 + m][:, 0:SEQ], w_h[:, c], w_l[:, c], hT_hi[:, k, :], hT_lo[:, k, :],
                                   k == 0, k == NK - 1)
                    if b % UB == UB - 1:
                        last.then_inc(S["units_used"], 1)

            channels(0, 0)
            pe.wait_ge(S["a1_sb"], 1)
            for t in range(NT):
                last = nc.tensor.transpose(bank[7][0:16, t * P:(t + 1) * P], esc[:, 0, 16 * t:16 * (t + 1)], ident)
            last.then_inc(S["a1T_psum"], 1)
            pe.wait_ge(S["a1_sb"], 2)
            for h in range(GH):
                last = mm(bank[4 + h // 2][:, h % 2 * SEQ:(h % 2 + 1) * SEQ], wa2[:, h * P:(h + 1) * P], a1T[0:16, :],
                          start=True, stop=True)
            last.then_inc(S["z"], 1)
            pe.wait_ge(S["zb"], 1)
            channels(1, 4)
            pe.wait_ge(S["gla_qk"], 4)
            group(U_C_IN, 2, (0, 1))
            group(U_C_IN, 3, (2, 3))
            pe.wait_ge(S["gla_qk"], 8)
            group(U_C_IN, 4, (4, 5))
            group(U_C_IN, 5, (6, 7))

            def diagonal(t):
                pe.wait_ge(S["prod"], GB * (t + 1))
                for s_ in range(GB):
                    last = mm(bank[t][:, :], cst[:, C_SEL + GB - s_:C_SEL + GB - s_ + P], prod[:, s_, :],
                              start=(s_ == 0), stop=(s_ == GB - 1))
                last.then_inc(S["diag"], 1)

            def cross(t):
                pe.wait_ge(S["kt"], t + 1)
                pe.wait_ge(S["qt"], t + 1)
                for h in range(GH):
                    for i in range(1, NGB):
                        at = h * P + i * GB
                        last = mm(bank[2 + t][:, at:at + GB], kt[:, i - 1, h * P:(h + 1) * P], gqt[:, at:at + GB],
                                  start=True, stop=True)
                last.then_inc(S["cross"], 1)

            pe.wait_ge(S["gla_vr"], 4)
            for t in range(NT):
                cross(t)
                diagonal(t)
            pe.wait_ge(S["far_ops"], 1)
            pe.wait_ge(S["gla_vr"], 8)
            for h in range(GH):
                last = mm(bank[4][:, h * P:(h + 1) * P], kbar[:, h * P:(h + 1) * P], qbar[:, h * P:(h + 1) * P],
                          start=True, stop=True)
            last.then_inc(S["far_psum"], 1)
            pe.wait_ge(S["att"], 2)
            pe.wait_ge(S["far_sb"], 1)
            for t in range(NT):
                for h in range(GH):
                    o = bank[GLA_BANKS[2 * t + h // 2]][:, h % 2 * 256:(h % 2 + 1) * 256]
                    last = mm(o, att[:, t, h * P:(h + 1) * P], gv[:, t, h * 256:(h + 1) * 256],
                              start=True, stop=(t == 0))
                    if t == 1:
                        last = mm(o, far[:, h * P:(h + 1) * P], gv[:, 0, h * 256:(h + 1) * 256],
                                  start=False, stop=True)
                    if h % 2:
                        last.then_inc(S["gla_o"], 1)
            transposes(4, lambda t: pe.wait_ge(S["mixed"], NT * GH))
            pe.wait_ge(S["hT"], 20)
            group(U_C_OUT, 0, (4, 5))
            group(U_C_OUT, 1, (6, 7))
            if stop < 5:
                return

            transposes(5, normed(3))
            pe.wait_ge(S["hT"], 24)
            for t in range(NT):
                for k in range(NK):
                    w = slice(8 * k, 8 * (k + 1))
                    last = mm3(bank[0][:, t * 8:t * 8 + 8], hT_hi[:, k, t * P:(t + 1) * P],
                               hT_lo[:, k, t * P:(t + 1) * P], swhi[:, w], swlo[:, w], k == 0, k == NK - 1)
            last.then_inc(S["logits"], 1)
            pe.wait_ge(S["picked"], 1)
            mm(bank[1][:, 0:8], tri, picked[:, 0, :], start=True, stop=True)
            mm(bank[1][:, 8:16], ones, picked[:, 0, :], start=True, stop=False)
            mm(bank[1][:, 8:16], tri, picked[:, 1, :], start=False, stop=True)
            mm(bank[1][:, 16:24], ones, picked[:, 0, :], start=True, stop=False)
            mm(bank[1][:, 16:24], ones, picked[:, 1, :], start=False, stop=True).then_inc(S["rank"], 1)

            def gather(e, half):
                if half == 0:
                    pe.wait_ge(S["disp"], e + 2)
                if half or not isinstance(e, int) or e >= 0:
                    pe.wait_ge(S["xg_tmp"], (e + 1) * 2 + half)
                for j in range(4):
                    c = slice((half * 4 + j) * P, (half * 4 + j + 1) * P)
                    for t in range(NT):
                        mm(bank[3][:, j * P:(j + 1) * P], hn_hi[:, t, c], disp[:, t, :], start=(t == 0), stop=False)
                        last = mm(bank[3][:, j * P:(j + 1) * P], hn_lo[:, t, c], disp[:, t, :],
                                  start=False, stop=(t == NT - 1))
                last.then_inc(S["xg_psum"], 1)

            def scatter(e, halves):
                if 0 in halves:
                    pe.wait_ge(S["ysb"], e * 2 + 2)
                for i in halves:
                    t, half = i // 2, i % 2
                    if i >= 2:
                        pe.wait_ge(S["x_ready"], e * 4 + (X_MOE + i - 1))
                    mm(bank[6 + i % 2][:, :], combT[:, t, :], y_hi[:, half * BLK:(half + 1) * BLK],
                       start=True, stop=False)
                    mm(bank[6 + i % 2][:, :], combT[:, t, :], y_lo[:, half * BLK:(half + 1) * BLK],
                       start=False, stop=True).then_inc(S["scat"], 1)

            def expert(e, base, par, fresh=False, drain=False, second=False):
                def split_unit(pos):
                    pe.wait_ge(S["w_lo"], e * EXP_UNITS + (U_MOE + pos + 1))
                    sl = (base + pos) % SPLIT
                    return lambda b: (whi[:, sl, b, :], wlo[:, sl, b, :])

                def m_gate_up(c, half):
                    w = split_unit(pos_g(c, half, fresh))
                    tokens = slice(par * P, (par + 1) * P)
                    for k in range(4 * half, 4 * half + 4):
                        last = mm3(bank[(par + c) % 2][:, :], hT_hi[:, k, tokens], hT_lo[:, k, tokens], *w(k % 4),
                                   k == 0, k == NK - 1)
                    last.then_inc(S["units_used"], 1)

                def m_hidden_T(c):
                    pe.wait_ge(S["m_hact"], e * NCH + (c + 1))
                    if c or not fresh:
                        pe.wait_ge(S["m_h2T"], e * NCH + c)
                    for j in range(2):
                        last = nc.tensor.transpose(bank[2][:, j * P:(j + 1) * P],
                                                   hact[:, (par + c) % 2, j * P:(j + 1) * P], ident)
                    last.then_inc(S["m_h2T_psum"], 1)

                def m_down(c):
                    w = split_unit(pos_d(c, drain))
                    pe.wait_ge(S["m_h2T"], e * NCH + (c + 1))
                    if c == 0 and not fresh:
                        pe.wait_ge(S["ysb"], e * 2)
                    first, final = c in (0,), c % NCH == NCH - 1
                    for j in range(2):
                        for half in range(2):
                            last = mm3(bank[4 + half][:, :], h2_hi[:, (par + c) % 2, j * P:(j + 1) * P],
                                       h2_lo[:, (par + c) % 2, j * P:(j + 1) * P], *w(2 * j + half),
                                       first and j == 0, final and j == 1)
                    last.then_inc(S["units_used"], 1)

                if second:
                    gather(e - 1, 0)
                    gather(e - 1, 1)
                pe.wait_ge(S["xg"], (e + 1) * 2)
                for c in range(NCH):
                    if c >= 2 or not fresh:
                        pe.wait_ge(S["m_hact"], e * NCH + (c - 1))
                    m_gate_up(c, 0)
                    m_gate_up(c, 1)
                    if c or not fresh:
                        m_hidden_T(c - 1)
                    if not fresh and c in (SCATTER, SCATTER + 1):
                        scatter(e - 1, (0, 1) if c == SCATTER else (2, 3))
                    if c == TURN:
                        pe.wait_ge(S["x_ready"], e * 4 + X_MOE)
                        for t in range(NT):
                            nc.tensor.transpose(bank[6][:, t * P:(t + 1) * P], disp[:, t, :].bitcast(F32), ident)
                        for t in range(NT):
                            last = mm(bank[6][:, 2 * P:2 * P + 1], disp[:, t, :].bitcast(F32), cur[:, 1, t:t + 1],
                                      start=(t == 0), stop=(t == NT - 1))
                        last.then_inc(S["combT_psum"], 1)
                    if not drain and c in (GATHER, GATHER + 1):
                        gather(e, c - GATHER)
                    if c >= 2 or not fresh:
                        m_down(c - 2)
                if drain:
                    m_down(NCH - 2)
                    m_hidden_T(NCH - 1)
                    m_down(NCH - 1)
                    pe.wait_ge(S["combT"], e + 1)
                    scatter(e, range(4))

            pe.wait_ge(S["hn_lo"], 2)
            gather(-1, 0)
            gather(-1, 1)
            expert(0, U_MOE, 0, fresh=True)
            with pe.Fori(1, NE - 1, 2) as e:
                expert(e, U_MOE + EXP_UNITS, 1)
                expert(e + 1, U_MOE + 2 * EXP_UNITS, 0)
            expert(NE - 1, U_MOE + (NE - 1) * EXP_UNITS, 1, drain=True)
            n_over = pe.value_load(ovi[0:1, 0:1], min_val=0, max_val=OVER_ROUNDS)
            with pe.Fori(NE, NE + OVER_ROUNDS) as e:
                with pe.If(n_over > e - NE):
                    expert(e, U_END, 0, fresh=True, drain=True, second=True)

        @block.scalar
        def _(act):
            A = nc.scalar.activation

            def norm(n):
                if n == 0:
                    act.wait_ge(S["x_in"], 16)
                else:
                    act.wait_ge(S["x_ready"], 4 * n)
                junk = esc[:, :, :].rearrange("p k n -> p (k n)")
                for t in range(NT):
                    if t:
                        act.wait_ge(S["ss"], NT * n + 1)
                    A(junk, x[:, t, :], ACT.Square, accum_out=ss[:, t:t + 1]).then_inc(S["ss"], 1)

            def split(u, first=U_MOE + 1):
                act.wait_ge(s_loaded[u % RAW], 16 * (u // RAW + 1))
                if u >= SPLIT:
                    act.wait_ge(S["units_used"], u - SPLIT + 1)
                nc.scalar.copy(whi[:, u % SPLIT, :, :], raw[:, u % RAW, :, :]).then_inc(S["w_hi"], 1)

            def turned(g, gained=True):
                for i in range(4):
                    t, half = i // 2, i % 2
                    if gained:
                        act.wait_ge(S["tmp"], TMP[g] + i + 1)
                        src = esc[:, i % 2, :]
                    else:
                        act.wait_ge(S["hT_psum"], 4 * g + i + 1)
                        src = bank[i][:, :]
                    nc.scalar.copy(hT_hi[:, half * 4:half * 4 + 4, t * P:(t + 1) * P],
                                   src.rearrange("p (k n) -> p k n", k=4)).then_inc(S["hT_hi"], 1)

            norm(0)
            for u in range(3):
                split(u)
            turned(0)
            split(3)
            act.wait_ge(S["const_in"], CONST_DMAS * 16)
            nc.scalar.copy(swhi[:, :], sml[:, R_ROUTER:R_ROUTER + 192]).then_inc(S["sw_hi"], 1)
            for cg in range(A_IN_CG):
                split(2 * cg + 4)
                w = FRONT_WIDTH.get(cg, BLK)
                act.wait_ge(S["units_used"], 2 * (cg + 1))
                for t in range(NT):
                    nc.scalar.copy(proj[cg][:, t, 0:w], bank[4 + 2 * (cg % 2) + t][:, 0:w]).then_inc(S["proj"], 1)
                if cg < A_IN_CG - 1:
                    split(2 * cg + 5)
                if cg == 2:
                    act.wait_ge(S["hid_in"], 1)
                    A(gel[0:HD, 1, 0:60], gel[0:HD, 2, 0:60], ACT.Tanh, scale=0.7978845608028654).then_inc(S["tanh"], 1)
                    act.wait_ge(S["gate_z"], 1)
                    A(gat, gat, ACT.Exp, scale=-1.0).then_inc(S["gate_e"], 1)
                    act.wait_ge(S["fox_z"], 1)
                    A(fz[:, 2, :], fz[:, 1, :], ACT.Exp, scale=-1.0).then_inc(S["act_chain"], 1)
                    act.wait_ge(S["act_chain"], 1)
                    A(fz[:, 3, :], fz[:, 2, :], ACT.Ln, bias=1.0).then_inc(S["fox_l"], 1)
            act.wait_ge(S["cmp_d"], 1)
            A(sc, sc, ACT.Exp, scale=HD ** -0.5).then_inc(S["cmp_e"], 1)
            for i in range(8):
                w, t, half = i // 4, i // 2 % 2, i % 2
                act.wait_ge(S["foxT_psum"], i + 1)
                dst = (fqT, fkT)[w]
                nc.scalar.copy(dst[0:66, half * 4:half * 4 + 4, t * P:(t + 1) * P],
                               bank[i % 4][0:66, :].rearrange("p (h n) -> p h n", h=4)).then_inc(S["foxT"], 1)
            for u in range(AU):
                br, t, h0, n = att_units[u]
                kw = (t + 1) * P
                act.wait_ge(S["rowmax"], u + 1)
                if u >= 2:
                    act.wait_ge(S["probsT_psum"], u - 1)
                for j in range(n):
                    last = A(pbuf[:, u % 2, j * kw:(j + 1) * kw], bank[u % 2][:, j * kw:(j + 1) * kw], ACT.Exp,
                             scale=HD ** -0.5, bias=negm[:, seq_of(u), h0 + j:h0 + j + 1],
                             accum_out=sums[:, seq_of(u), h0 + j:h0 + j + 1])
                last.then_inc(S["probs"], 1)
            turned(1, False)
            if stop < 2:
                return
            for u in range(U_A_OUT + 3, U_FFN + 3):
                split(u)
            if stop < 3:
                return
            norm(1)
            turned(2)
            n_steps = len(steps)
            for i, (c, t) in enumerate(steps):
                freed = U_FFN + dense_g(c, 0) + 1
                if t:
                    split(freed + 2)
                    act.wait_ge(S["units_used"], freed + 1)
                else:
                    act.wait_ge(S["gu"], c + 1)
                A(sg[:, i % 2, :], bank[i % 2][:, 0:CH], ACT.Silu).then_inc(S["silu"], 1)
                if t:
                    split(freed + 3)
                if i >= 1:
                    act.wait_ge(S["h2T_psum"], i)
                    nc.scalar.copy(h2_hi[:, (i - 1) % 2, :], bank[2][:, 0:CH]).then_inc(S["h2_hi"], 1)
                if t and c:
                    split(freed + 4)
            act.wait_ge(S["h2T_psum"], n_steps)
            nc.scalar.copy(h2_hi[:, (n_steps - 1) % 2, :], bank[2][:, 0:CH]).then_inc(S["h2_hi"], 1)
            split(U_C_IN + 2)
            if stop < 4:
                return
            norm(2)
            turned(3)
            split(U_C_IN + 3)
            act.wait_ge(S["a1"], 1)
            nc.scalar.copy(esc[:, 0, 0:32], bank[6][:, 0:32]).then_inc(S["a1_sb"], 1)
            act.wait_ge(S["a1T_psum"], 1)
            nc.scalar.copy(a1T[0:16, :], bank[7][0:16, 0:SEQ]).then_inc(S["a1_sb"], 1)
            act.wait_ge(S["units_used"], U_C_IN + 2)
            for h in range(GH):
                A(gq[:, :, h * P:(h + 1) * P], bank[h][:, 0:SEQ].rearrange("p (t n) -> p t n", t=NT), ACT.Copy,
                  scale=P ** -0.5).then_inc(S["gla_qk"], 1)
            split(U_C_IN + 4)
            act.wait_ge(S["absz"], 1)
            A(ge, ge, ACT.Exp, scale=-1.0).then_inc(S["act_chain"], 1)
            act.wait_ge(S["act_chain"], 2)
            A(ge, ge, ACT.Ln, bias=1.0).then_inc(S["soft"], 1)
            split(U_C_IN + 5)
            act.wait_ge(S["units_used"], U_C_IN + 4)
            for h in range(GH):
                nc.scalar.copy(gk[:, :, h * P:(h + 1) * P], bank[4 + h][:, 0:SEQ].rearrange("p (t n) -> p t n", t=NT))\
                  .then_inc(S["gla_qk"], 1)
            split(U_C_IN + 6)

            def vr(cg):
                act.wait_ge(S["units_used"], U_C_IN + 2 * (cg + 1))
                half = cg % 2
                for t in range(NT):
                    dst = (gv if cg < 4 else gr)[:, t, half * BLK:(half + 1) * BLK]
                    b = bank[(0, 2, 4, 6)[cg - 2] + t]
                    if cg == 4 and t == 0:
                        act.wait_ge(S["cross"], NT)
                    A(dst, b[:, :], ACT.Copy if cg < 4 else ACT.Silu).then_inc(S["gla_vr"], 1)

            split(U_C_IN + 7)
            split(U_C_IN + 8)
            vr(2)
            for t in range(NT):
                act.wait_ge(S["q_arg"], t + 1)
                qv = gqt.rearrange("p (h i r) -> p h i r", h=GH, r=GB)[:, :, 1:NGB, :]
                A(qv, qv, ACT.Exp).then_inc(S["q_exp"], 1)
                for i in range(1, NGB):
                    act.wait_ge(S["k_arg"], (NGB - 1) * t + i)
                    kv = kt[:, i - 1, :].rearrange("p (h n) -> p h n", h=GH)[:, :, 0:i * GB]
                    A(kv, kv, ACT.Exp).then_inc(S["k_exp"], 1)
                    if t == 0 and i in CROSS_SPLITS:
                        split(U_C_IN + CROSS_SPLITS[i])
                    if t == 0 and i == 9:
                        vr(3)
                for s_ in range(GB):
                    d = t * GB + s_
                    act.wait_ge(S["diag_arg"], d + 1)
                    e_ = esc[:, d % 2, 0:(GB - s_) * 64]
                    A(e_, e_, ACT.Exp).then_inc(S["diag_exp"], 1)
                    if d in DIAG_SPLITS:
                        split(U_C_IN + DIAG_SPLITS[d])
            act.wait_ge(S["far_arg"], 1)
            A(kbar, kbar, ACT.Exp).then_inc(S["far_exp"], 1)
            A(qbar, gb[:, 1, :], ACT.Exp).then_inc(S["far_exp"], 1)
            vr(4)
            vr(5)
            act.wait_ge(S["far_psum"], 1)
            nc.scalar.copy(far, bank[4][:, :]).then_inc(S["far_sb"], 1)
            act.wait_ge(S["prod"], NT * GB)
            for i in range(NT * GH):
                act.wait_ge(S["gla_o"], i // 2 + 1)
                if i >= 2:
                    act.wait_ge(S["gla_ss"], i - 1)
                b = bank[GLA_BANKS[i // 2]]
                A(esc[:, i % 2, 0:256], b[:, i % 2 * 256:(i % 2 + 1) * 256], ACT.Square,
                  accum_out=oss[:, i:i + 1]).then_inc(S["gla_ss"], 1)
            turned(4, False)
            for u in range(U_C_OUT + 3, min(U_MOE + 3, LIMITS[stop])):
                split(u)
            if stop < 5:
                return
            norm(3)
            turned(5)
            for t in range(NT):
                act.wait_ge(S["hn"], NT * 3 + t + 1)
                nc.scalar.copy(hn_hi[:, t, :], hn[:, t, :]).then_inc(S["hn_hi"], 1)
            act.wait_ge(S["gap"], 1)
            A(ee, ee, ACT.Exp).then_inc(S["gap_exp"], 1)

            def gathered(e, par, half):
                act.wait_ge(S["xg_tmp"], (e + 1) * 2 + (half + 1))
                nc.scalar.copy(hT_hi[:, half * 4:half * 4 + 4, par * P:(par + 1) * P],
                               esc[:, half, :].rearrange("p (k n) -> p k n", k=4)).then_inc(S["xg_hi"], 1)

            def final_sums(e, used):
                act.wait_ge(S["units_used"], used)
                for half in range(2):
                    A(y_hi[:, half * BLK:(half + 1) * BLK], bank[4 + half][:, :], ACT.Copy, scale=gslot[:, 0:1])\
                      .then_inc(S["y_hi"], 1)

            def expert(e, base, par, loads, fresh=False, drain=False, second=False):
                def split_unit(pos):
                    if pos >= EXP_UNITS and drain:
                        return
                    u = base + pos
                    act.wait_ge(s_loaded[u % RAW], loads(pos))
                    act.wait_ge(S["units_used"],
                                e * EXP_UNITS + (U_MOE + (max(pos - SPLIT + 1, 0) if second else pos - SPLIT + 1)))
                    nc.scalar.copy(whi[:, u % SPLIT, :, :], raw[:, u % RAW, :, :]).then_inc(S["w_hi"], 1)

                def hidden_turned(c):
                    act.wait_ge(S["m_h2T_psum"], e * NCH + (c + 1))
                    nc.scalar.copy(h2_hi[:, (par + c) % 2, :], bank[2][:, 0:CH]).then_inc(S["m_h2_hi"], 1)

                if second:
                    gathered(e - 1, par, 0)
                    gathered(e - 1, par, 1)
                    for pos in range(SPLIT):
                        split_unit(pos)
                for c in range(NCH):
                    if c == 2 and not fresh:
                        final_sums(e - 1, e * EXP_UNITS + (U_MOE + pos_d(-1, drain) + 1))
                    split_unit(pos_g(c, 0, fresh) + SPLIT)
                    act.wait_ge(S["units_used"], e * EXP_UNITS + (U_MOE + pos_g(c, 1, fresh) + 1))
                    A(sg[:, (par + c) % 2, :], bank[(par + c) % 2][:, 0:CH], ACT.Silu).then_inc(S["m_silu"], 1)
                    split_unit(pos_g(c, 1, fresh) + SPLIT)
                    if c or not fresh:
                        hidden_turned(c - 1)
                    if c == TURN:
                        act.wait_ge(S["combT_psum"], e + 1)
                        nc.scalar.copy(gslot[:, :], bank[6][:, 2 * P:2 * P + 1])
                        nc.scalar.copy(combT[:, :, :], bank[6][:, 0:2 * P].rearrange("p (t n) -> p t n", t=NT))\
                          .then_inc(S["combT"], 1)
                    if not drain and c in (GATHER + 1, GATHER + 2):
                        gathered(e, 1 - par, c - GATHER - 1)
                    if c >= 2 or not fresh:
                        split_unit(pos_d(c - 2, drain) + SPLIT)
                if drain:
                    hidden_turned(NCH - 1)
                    final_sums(e, (e + 1) * EXP_UNITS + U_MOE)

            gathered(-1, 0, 0)
            gathered(-1, 0, 1)
            expert(0, U_MOE, 0, lambda pos: loads_main(0, U_MOE, pos), fresh=True)
            with act.Fori(1, NE - 1, 2) as e:
                expert(e, U_MOE + EXP_UNITS, 1, lambda pos: loads_main(e - 1, U_MOE + EXP_UNITS, pos))
                expert(e + 1, U_MOE + 2 * EXP_UNITS, 0, lambda pos: loads_main(e - 1, U_MOE + 2 * EXP_UNITS, pos))
            last = U_MOE + (NE - 1) * EXP_UNITS
            expert(NE - 1, last, 1, lambda pos: loads_main(0, last, pos), drain=True)
            act.wait_ge(S["route"], 1)
            n_over = act.value_load(ovi[0:1, 0:1], min_val=0, max_val=OVER_ROUNDS)
            with act.Fori(NE, NE + OVER_ROUNDS) as e:
                with act.If(n_over > e - NE):
                    expert(e, U_END, 0, lambda pos: loads_over(e, pos), fresh=True, drain=True, second=True)

        @block.vector
        def _(dve):
            V = nc.vector
            chain = [0]

            def link(ins):
                chain[0] += 1
                ins.then_inc(S["dve_chain"], 1)
                dve.wait_ge(S["dve_chain"], chain[0])

            def bc(ap, axis, n):
                a = ap.unsqueeze(axis)
                shape = list(a.shape)
                shape[axis] = n
                return a.to_broadcast(shape)

            def norm(n):
                dve.wait_ge(S["rstd"], n + 1)
                for t in range(NT):
                    V.tensor_scalar(hn[:, t, :], x[:, t, :], rstd[:, t:t + 1], None, ALU.mult).then_inc(S["hn"], 1)

            def split(u):
                dve.wait_ge(S["w_hi"], u + 1)
                V.tensor_tensor(wlo[:, u % SPLIT, :, :], raw[:, u % RAW, :, :], whi[:, u % SPLIT, :, :].bitcast(F32),
                                ALU.subtract).then_inc(S["w_lo"], 1)

            def turned(g, gain=None):
                def lower(i):
                    t, half = i // 2, i % 2
                    at = (slice(None), slice(half * 4, half * 4 + 4), slice(t * P, (t + 1) * P))
                    dve.wait_ge(S["hT_hi"], 4 * g + i + 1)
                    src = bank[i][:, :] if gain is None else esc[:, i % 2, :]
                    V.tensor_tensor(hT_lo[at], src.rearrange("p (k n) -> p k n", k=4), hT_hi[at].bitcast(F32),
                                    ALU.subtract).then_inc(S["hT"], 1)

                for i in range(4):
                    half = i % 2
                    dve.wait_ge(S["hT_psum"], 4 * g + i + 1)
                    if gain is not None:
                        if i >= 2:
                            lower(i - 2)
                        gc = R_NORM + NK * gain + 4 * half
                        if i >= 2:
                            dve.wait_ge(S["hT"], 4 * g + i - 1)
                        V.tensor_tensor(esc[:, half, :].rearrange("p (k n) -> p k n", k=4),
                                        bank[i][:, :].rearrange("p (k n) -> p k n", k=4),
                                        bc(sml[:, gc:gc + 4], 2, P), ALU.mult).then_inc(S["tmp"], 1)
                    else:
                        lower(i)
                if gain is not None:
                    lower(2)
                    lower(3)

            def residual(u0):
                for cg in range(2):
                    for j in (3, 4):
                        if u0 + 2 * cg + j < LIMITS[stop]:
                            split(u0 + 2 * cg + j)
                    dve.wait_ge(S["units_used"], u0 + 2 * (cg + 1))
                    for t in range(NT):
                        xs = x[:, t, cg * BLK:(cg + 1) * BLK]
                        V.tensor_tensor(xs, xs, bank[4 + 2 * cg + t][:, :], ALU.add).then_inc(S["x_ready"], 1)

            def head_norm(src, nh, which, gain, dst, order):
                n = NT * nh
                dve.wait_ge(S["head_done"], order - 1)
                s3 = sq[:, 0:n * HD].rearrange("p (r d) -> p r d", d=HD).rearrange("p (t h) d -> p t h d", t=NT)
                link(V.tensor_tensor(s3, src, src, ALU.mult))
                V.tensor_reduce(hss[:, which, 0:n], sq[:, 0:n * HD].rearrange("p (r d) -> p r d", d=HD), AX.X, ALU.add)\
                 .then_inc(S["head_ss"], 1)
                dve.wait_ge(S["head_rstd"], order)
                r3 = hrs[:, which, 0:n].rearrange("p (t h) -> p t h", t=NT)
                link(V.tensor_tensor(s3, src, bc(r3, 3, HD), ALU.mult))
                g1 = bc(bc(sml[:, gain:gain + HD], 1, nh), 1, NT)
                return V.tensor_tensor(dst, s3, g1, ALU.mult)

            def rope(v, tab, nh, ra, rb):
                link(V.tensor_tensor(ra, v[:, :, :, 0:16], bc(tab[:, :, 0:16], 2, nh), ALU.mult))
                V.tensor_tensor(rb[:, :, :, 0:8], v[:, :, :, 8:16], bc(tab[:, :, 16:24], 2, nh), ALU.mult)
                link(V.tensor_tensor(rb[:, :, :, 8:16], v[:, :, :, 0:8], bc(tab[:, :, 24:32], 2, nh), ALU.mult))
                return V.tensor_tensor(v[:, :, :, 0:16], ra, rb, ALU.add)

            def four(buf, nh):
                return buf[:, 0:NT * nh * 16].rearrange("p (t h d) -> p t h d", t=NT, h=nh)

            dve.wait_ge(S["x_in"], 16)
            norm(0)
            dve.wait_ge(S["const_in"], CONST_DMAS * 16)
            for u in range(3):
                split(u)
            turned(0, 0)
            for u in (3, 4, 5):
                split(u)
            dve.wait_ge(S["sw_hi"], 1)
            V.tensor_tensor(swlo[:, :], sml[:, R_ROUTER:R_ROUTER + 192], swhi[:, :].bitcast(F32), ALU.subtract)\
             .then_inc(S["sw_lo"], 1)
            for v in range(2):
                dve.wait_ge(S["kc_psum"], v + 1)
                src = bank[v][0:HD, :].rearrange("p (g n) -> p g n", g=NG)
                V.tensor_copy(kc2[0:HD, v, :, :], src).then_inc(S["kc"], 1)
                V.tensor_copy(kc2[HD:P, v, :, 0:SEQ - 1], src[:, :, 1:SEQ]).then_inc(S["kc"], 1)
            dve.wait_ge(S["kc"], 4)
            for v in range(2):
                for g in range(NG):
                    first = kc2[:, v, g, :].rearrange("p (m j w) -> p j m w", j=8, w=2)[:, :, :, 0]
                    pe_ = sml[:, R_PE + 16 * v:R_PE + 16 * (v + 1)]
                    V.tensor_tensor(blkT[:, v, 0:8, g, :], first[:, :, 0:NCMP], bc(pe_[:, 0:8], 2, NCMP), ALU.add)
                    V.tensor_tensor(blkT[:, v, 8:16, g, :], first[:, :, 1:NCMP + 1], bc(pe_[:, 8:16], 2, NCMP),
                                    ALU.add).then_inc(S["blk"], 1)
            split(6)
            tab = cst[:, C_ROPE:C_ROPE + 64].rearrange("p (t n) -> p t n", t=NT)
            keys = proj[0][:, :, 256:512].rearrange("p t (h d) -> p t h d", h=4)
            link(head_norm(keys, 4, 0, R_KN, keys, 1))
            split(7)
            rope(keys, tab, 4, four(rA, 4), four(rB, 4)).then_inc(S["head_done"], 1)
            dve.wait_ge(S["proj"], 4)
            V.tensor_tensor(gat.rearrange("p (t n) -> p t n", t=NT), proj[1][:, :, 256:280],
                            bc(sml[:, R_GB:R_GB + 24], 1, NT), ALU.add).then_inc(S["gate_z"], 1)
            link(V.tensor_tensor(fz[:, 0, :].rearrange("p (t n) -> p t n", t=NT), proj[1][:, :, 280:288],
                                 bc(sml[:, R_FB:R_FB + 8], 1, NT), ALU.add))
            link(V.tensor_scalar(fz[:, 1, :], fz[:, 0, :], -1.0, None, ALU.mult))
            V.tensor_tensor(fz[:, 1, :], fz[:, 1, :], fz[:, 0, :], ALU.max).then_inc(S["fox_z"], 1)
            split(8)
            dve.wait_ge(S["hid"], 1)
            xh = gel[0:HD, 0, 0:60]
            uu = gel[0:HD, 2, 0:60]
            link(V.tensor_copy(xh.rearrange("p (v n) -> p v n", v=2),
                               bank[2][0:HD, 0:64].rearrange("p (v n) -> p v n", v=2)[:, :, 0:30]))
            link(V.tensor_tensor(uu, xh, xh, ALU.mult))
            link(V.tensor_scalar(uu, uu, 0.044715, 1.0, ALU.mult, ALU.add))
            V.tensor_tensor(uu, uu, xh, ALU.mult).then_inc(S["hid_in"], 1)
            for t in range(NT):
                dve.wait_ge(S["headT_psum"], t + 1)
                V.tensor_copy(keyT[0:HD, :, t * P:(t + 1) * P], bank[t][0:HD, :].rearrange("p (h n) -> p h n", h=4))\
                 .then_inc(S["headT"], 1)
            split(9)
            dve.wait_ge(S["tanh"], 1)
            link(V.tensor_scalar(gel[0:HD, 1, 0:60], gel[0:HD, 1, 0:60], 0.5, 0.5, ALU.mult, ALU.add))
            V.tensor_tensor(gel[0:HD, 3, 0:60], gel[0:HD, 1, 0:60], xh, ALU.mult).then_inc(S["gelu"], 1)
            dve.wait_ge(S["proj"], 6)
            qa = proj[2][:, :, :].rearrange("p t (h d) -> p t h d", h=NH)
            link(head_norm(qa, NH, 1, R_QN, qa, 2))
            split(10)
            dve.wait_ge(S["cmp2"], 1)
            V.tensor_copy(vcmp[0:NCMP, :, :], bank[3][0:NCMP, HD:3 * HD].rearrange("p (g d) -> p g d", g=NG))\
             .then_inc(S["cmp2_sb"], 1)
            link(V.tensor_copy(kcm[0:30, 0, :], bank[3][0:30, 0:HD]))
            link(V.tensor_tensor(kcm[0:30, 1, :], kcm[0:30, 0, :], kcm[0:30, 0, :], ALU.mult))
            V.tensor_reduce(hss[0:30, 4, 0:1], kcm[0:30, 1, :], AX.X, ALU.add).then_inc(S["kcmp_ss"], 1)
            rope(qa, tab, NH, four(rA, NH), four(rB, NH)).then_inc(S["head_done"], 1)
            split(11)
            dve.wait_ge(S["kcmp_rstd"], 1)
            link(V.scalar_tensor_tensor(kcm[0:30, 3, :], kcm[0:30, 0, :], hrs[0:30, 4, 0:1], sml[0:30, R_KN:R_KN + HD],
                                        ALU.mult, ALU.mult))
            ct = cst[0:30, C_CROPE:C_CROPE + 32]
            kv = kcm[0:30, 3, :]
            dve.wait_ge(S["head_done"], 2)
            link(V.tensor_tensor(rA[0:30, 0:16], kv[:, 0:16], ct[:, 0:16], ALU.mult))
            V.tensor_tensor(rB[0:30, 0:8], kv[:, 8:16], ct[:, 16:24], ALU.mult)
            link(V.tensor_tensor(rB[0:30, 8:16], kv[:, 0:8], ct[:, 24:32], ALU.mult))
            V.tensor_tensor(kv[:, 0:16], rA[0:30, 0:16], rB[0:30, 0:16], ALU.add).then_inc(S["kcmp"], 1)
            split(12)
            dve.wait_ge(S["vrep"], 1)
            V.tensor_tensor(vbd.rearrange("p (h d) -> p h d", h=NH), bc(bank[2][:, 0:HD], 1, NH),
                            bc(cst[:, C_HMASK:C_HMASK + 8], 2, HD), ALU.mult).then_inc(S["vbd"], 1)
            dve.wait_ge(S["kcmpT_psum"], 1)
            V.tensor_copy(kcmpT[0:HD, 0:30], bank[3][0:HD, 256:286]).then_inc(S["kcmpT"], 1)
            split(13)
            split(14)
            for i in range(4):
                t, half = i // 2, i % 2
                dve.wait_ge(S["headT_psum"], 3 + i)
                V.tensor_copy(qT[0:HD, half * 4:half * 4 + 4, t * P:(t + 1) * P],
                              bank[i][0:HD, :].rearrange("p (h n) -> p h n", h=4)).then_inc(S["headT"], 1)
            dve.wait_ge(S["fox_l"], 1)
            V.scalar_tensor_tensor(fz[:, 4, :], fz[:, 0, :], 0.0, fz[:, 3, :], ALU.min, ALU.subtract)\
             .then_inc(S["fox_lf"], 1)
            dve.wait_ge(S["gate_e"], 1)
            link(V.tensor_scalar(gat, gat, 1.0, None, ALU.add))
            link(V.reciprocal(gat, gat))
            for w, gain in ((0, R_FQ), (1, R_FK)):
                dve.wait_ge(S["proj"], 8 + 2 * w)
                src = proj[3 + w][:, :, :].rearrange("p t (h d) -> p t h d", h=NH)
                head_norm(src, NH, 2 + w, gain, faug[:, w, :, :, 0:HD], 3 + w).then_inc(S["head_done"], 1)
                V.memset(faug[:, w, :, :, HD + 1 - w:HD + 2 - w], 1.0)
            dve.wait_ge(S["cum"], 1)
            cum = bank[0][:, 0:16].rearrange("p (t h) -> p t h", t=NT).unsqueeze(3)
            V.tensor_scalar(faug[:, 0, :, :, HD:HD + 1], cum, HD ** 0.5, None, ALU.mult)
            V.tensor_scalar(faug[:, 1, :, :, HD + 1:HD + 2], cum, -HD ** 0.5, None, ALU.mult).then_inc(S["aug"], 1)
            dve.wait_ge(S["cmp_s"], 1)
            s16 = sc.rearrange("p t (h n) -> p t h n", h=NH)
            s15 = s16[:, :, :, 0:NCMP]
            bias = cst[:, C_CBIAS:C_CBIAS + 32].rearrange("p (t n) -> p t n", t=NT)[:, :, 0:NCMP]
            cm01 = cst[:, C_CMASK:C_CMASK + 32].rearrange("p (t n) -> p t n", t=NT)
            V.memset(s16[:, :, :, NCMP:16], 0.0)
            link(V.tensor_tensor(s15, bank[6][:, 0:2 * P].rearrange("p (t h n) -> p t h n", t=NT, h=NH)[:, :, :, 0:NCMP],
                                 bc(bias, 2, NH), ALU.add))
            m3 = mc.rearrange("p (t h) -> p t h", t=NT)
            link(V.tensor_reduce(m3, s15, AX.X, ALU.max))
            V.tensor_tensor(s15, s15, bc(m3, 3, NCMP), ALU.subtract).then_inc(S["cmp_d"], 1)
            dve.wait_ge(S["cmp_e"], 1)
            link(V.tensor_reduce(sumc.rearrange("p (t h) -> p t h", t=NT), s15, AX.X, ALU.add))
            V.tensor_tensor(s16, s16, bc(cm01, 2, NH), ALU.mult).then_inc(S["cmp_p"], 1)
            link(V.reciprocal(sumc, sumc))
            g4 = gat.rearrange("p (t h w) -> p t h w", t=NT, h=NH)
            V.tensor_tensor(facc.rearrange("p (t h) -> p t h", t=NT), sumc.rearrange("p (t h) -> p t h", t=NT),
                            g4[:, :, :, 0], ALU.mult).then_inc(S["dve_chain"], 1)
            chain[0] += 1
            dve.wait_ge(S["cmp_pT_psum"], 1)
            V.tensor_copy(pcT, bank[7][:, 0:2 * P].rearrange("p (t n) -> p t n", t=NT)).then_inc(S["cmp_pT"], 1)
            dve.wait_ge(S["dve_chain"], chain[0])

            def heads(ap):
                return ap.rearrange("p (h d) -> p h d", h=NH)

            for t in range(NT):
                dve.wait_ge(S["cmp_o"], t + 1)
                V.tensor_tensor(heads(oacc[:, t, 0:512]), heads(bank[4 + t][:, :]), bc(facc[:, t * 8:t * 8 + 8], 2, HD),
                                ALU.mult).then_inc(S["o_done"], 1)

            def rowmax(u):
                br, t, h0, n = att_units[u]
                dve.wait_ge(S["scores"], u + 1)
                m = negm[:, seq_of(u), h0:h0 + n]
                link(V.tensor_reduce(m, bank[u % 2][:, :].rearrange("p (h n) -> p h n", h=n), AX.X, ALU.max))
                V.tensor_scalar(m, m, -HD ** -0.5, None, ALU.mult).then_inc(S["rowmax"], 1)

            def take(q):
                br, t = q // NT, q % NT
                dve.wait_ge(S["pv"], ends_seq[q] + 1)
                o = heads(bank[4 + q % 2][:, :])
                link(V.reciprocal(fac[:, q, :], sums[:, q, :]))
                if br == 2:
                    V.tensor_tensor(heads(oacc[:, t, 512:1024]), o, bc(fac[:, q, :], 2, HD), ALU.mult)\
                     .then_inc(S["o_done"], 1)
                    return
                link(V.tensor_tensor(fac[:, q, :], fac[:, q, :], g4[:, t, :, br + 1], ALU.mult))
                link(V.tensor_tensor(heads(tmpo), o, bc(fac[:, q, :], 2, HD), ALU.mult))
                V.tensor_tensor(oacc[:, t, 0:512], oacc[:, t, 0:512], tmpo, ALU.add).then_inc(S["o_done"], 1)

            rowmax(0)
            for u in range(AU):
                if u + 1 < AU:
                    rowmax(u + 1)
                dve.wait_ge(S["probsT_psum"], u + 1)
                if u >= 2:
                    dve.wait_ge(S["pv"], u - 1)
                V.tensor_copy(ptb[:, u % 2, :], bank[2 + u % 2][:, :]).then_inc(S["probsT"], 1)
                if u - 1 in ends_seq:
                    take(ends_seq.index(u - 1))
            take(2 * 3 - 1)
            turned(1)
            if stop < 2:
                return
            residual(U_A_OUT)
            if stop < 3:
                return
            norm(1)
            turned(2, 1)
            def h2_lower(i):
                dve.wait_ge(S["h2_hi"], i + 1)
                V.tensor_tensor(h2_lo[:, i % 2, :], bank[2][:, 0:CH], h2_hi[:, i % 2, :].bitcast(F32), ALU.subtract)\
                 .then_inc(S["h2T"], 1)

            for i, (c, t) in enumerate(steps):
                freed = U_FFN + dense_g(c, 0) + 1
                if t:
                    split(freed + 2)
                dve.wait_ge(S["silu"], i + 1)
                V.tensor_tensor(hact[:, i % 2, :], sg[:, i % 2, :], bank[i % 2][:, CH:2 * CH], ALU.mult)\
                 .then_inc(S["hact"], 1)
                if t:
                    split(freed + 3)
                if i >= 1:
                    h2_lower(i - 1)
                if t and c:
                    split(freed + 4)
            h2_lower(len(steps) - 1)
            split(U_C_IN + 2)
            dve.wait_ge(S["units_used"], U_C_IN)
            for t in range(NT):
                for half in range(2):
                    xs = x[:, t, half * BLK:(half + 1) * BLK]
                    V.tensor_tensor(xs, xs, bank[4 + 2 * t + half][:, :], ALU.add).then_inc(S["x_ready"], 1)
            if stop < 4:
                return

            norm(2)
            turned(3, 2)
            split(U_C_IN + 3)
            V.memset(rmask, 1.0).then_inc(S["dve_chain"], 1)
            chain[0] += 1
            dve.wait_ge(S["dve_chain"], chain[0])
            link(V.memset(rmask.rearrange("p (s n) -> p s n", n=P)[:, :, 0:1], 0.0))
            dve.wait_ge(S["z"], 1)
            for h in range(GH):
                last = V.tensor_scalar(gz.rearrange("p (t h n) -> p t h n", t=NT, h=GH)[:, :, h, :],
                                       bank[4 + h // 2][:, h % 2 * SEQ:(h % 2 + 1) * SEQ].rearrange("p (t n) -> p t n", t=NT),
                                       sml[:, R_BA + h:R_BA + h + 1], None, ALU.add)
            last.then_inc(S["zb"], 1)
            split(U_C_IN + 4)
            dve.wait_ge(S["zb"], 1)
            link(V.tensor_scalar(ge, gz, -1.0, None, ALU.mult))
            V.tensor_tensor(ge, ge, gz, ALU.max).then_inc(S["absz"], 1)
            dve.wait_ge(S["soft"], 1)
            split(U_C_IN + 5)
            link(V.scalar_tensor_tensor(gz, gz, 0.0, ge, ALU.min, ALU.subtract))
            gbf = gb.rearrange("p t n -> p (t n)")
            link(V.tensor_scalar(gz, gz, 1.0 / 16.0, None, ALU.mult))
            V.tensor_tensor_scan(gbf, rmask, gz, 0.0, ALU.mult, ALU.add).then_inc(S["decay"], 1)
            dve.wait_ge(S["decay"], 1)
            dve.wait_ge(S["kt_zero"], 1)
            dve.wait_ge(S["gla_qk"], 8)
            for j in (6, 7, 8):
                split(U_C_IN + j)

            def q_arg(t):
                b4 = gb[:, t, :].rearrange("p (h i r) -> p h i r", h=GH, r=GB)
                q4 = gqt.rearrange("p (h i r) -> p h i r", h=GH, r=GB)
                prev = b4[:, :, 0:NGB - 1, GB - 1:GB].to_broadcast([P, GH, NGB - 1, GB])
                V.tensor_tensor(q4[:, :, 1:NGB, :], b4[:, :, 1:NGB, :], prev, ALU.subtract).then_inc(S["q_arg"], 1)

            def k_view(t, i):
                kv_ = kt[:, i - 1, :].rearrange("p (h n) -> p h n", h=GH)[:, :, 0:i * GB]
                return kv_, gb[:, t, :].rearrange("p (h n) -> p h n", h=GH), gk[:, t, :].rearrange("p (h n) -> p h n", h=GH)

            def k_arg(t, i):
                kv_, b3, _ = k_view(t, i)
                edge = b3[:, :, i * GB - 1:i * GB].to_broadcast([P, GH, i * GB])
                V.tensor_tensor(kv_, edge, b3[:, :, 0:i * GB], ALU.subtract).then_inc(S["k_arg"], 1)

            def k_mul(t, i):
                kv_, _, k3 = k_view(t, i)
                dve.wait_ge(S["k_exp"], (NGB - 1) * t + i)
                last = V.tensor_tensor(kv_, kv_, k3[:, :, 0:i * GB], ALU.mult)
                if i == NGB - 1:
                    last.then_inc(S["kt"], 1)

            def diag_arg(d):
                t, s_ = d // GB, d % GB
                b3 = gb[:, t, :].rearrange("p (m r) -> p m r", r=GB)
                q3 = gq[:, t, :].rearrange("p (m r) -> p m r", r=GB)
                k3 = gk[:, t, :].rearrange("p (m r) -> p m r", r=GB)
                w = GB - s_
                e3 = esc[:, d % 2, 0:64 * w].rearrange("p (m r) -> p m r", r=w)
                if d >= 2:
                    dve.wait_ge(S["prod"], d - 1)
                V.tensor_tensor(e3, b3[:, :, s_:GB], b3[:, :, s_:s_ + 1].to_broadcast([P, 64, w]), ALU.subtract)\
                 .then_inc(S["diag_arg"], 1)
                p3 = prod[:, s_, :].rearrange("p (m r) -> p m r", r=GB)
                chain[0] += 1
                V.tensor_tensor(p3[:, :, s_:GB], q3[:, :, s_:GB], k3[:, :, s_:s_ + 1].to_broadcast([P, 64, w]), ALU.mult)\
                 .then_inc(S["dve_chain"], 1)
                return chain[0]

            def diag_mul(d, tag):
                s_ = d % GB
                w = GB - s_
                e3 = esc[:, d % 2, 0:64 * w].rearrange("p (m r) -> p m r", r=w)
                p3 = prod[:, s_, :].rearrange("p (m r) -> p m r", r=GB)
                dve.wait_ge(S["diag_exp"], d + 1)
                dve.wait_ge(S["dve_chain"], tag)
                V.tensor_tensor(p3[:, :, s_:GB], p3[:, :, s_:GB], e3, ALU.mult).then_inc(S["prod"], 1)

            for t in range(NT):
                if t:
                    dve.wait_ge(S["cross"], t)
                q_arg(t)
                k_arg(t, 1)
                k_arg(t, 2)
                for i in range(1, NGB):
                    if i + 2 < NGB:
                        k_arg(t, i + 2)
                    k_mul(t, i)
                    if t == 0 and i in CROSS_SPLITS:
                        split(U_C_IN + CROSS_SPLITS[i])
                q4 = gqt.rearrange("p (h i r) -> p h i r", h=GH, r=GB)[:, :, 1:NGB, :]
                dve.wait_ge(S["q_exp"], t + 1)
                V.tensor_tensor(q4, q4, gq[:, t, :].rearrange("p (h i r) -> p h i r", h=GH, r=GB)[:, :, 1:NGB, :],
                                ALU.mult).then_inc(S["qt"], 1)
                if t == 0:
                    dve.wait_ge(S["prod_zero"], 1)
                else:
                    dve.wait_ge(S["diag"], t)
                tag = diag_arg(GB * t)
                for d in range(GB * t, GB * (t + 1)):
                    nxt = diag_arg(d + 1) if d + 1 < GB * (t + 1) else None
                    diag_mul(d, tag)
                    if d in DIAG_SPLITS:
                        split(U_C_IN + DIAG_SPLITS[d])
                    tag = nxt
            dve.wait_ge(S["diag"], NT)
            V.tensor_tensor(kbar.rearrange("p (h n) -> p h n", h=GH),
                            gb[:, 0, :].rearrange("p (h n) -> p h n", h=GH)[:, :, P - 1:P].to_broadcast([P, GH, P]),
                            gb[:, 0, :].rearrange("p (h n) -> p h n", h=GH), ALU.subtract).then_inc(S["far_arg"], 1)
            for t in range(NT):
                dve.wait_ge(S["diag"], t + 1)
                a3 = att[:, t, :].rearrange("p (h n) -> p h n", h=GH)
                link(V.tensor_tensor(a3, bank[t][:, :].rearrange("p (h n) -> p h n", h=GH), bc(mbd, 1, GH), ALU.mult))
                dve.wait_ge(S["cross"], t + 1)
                V.tensor_tensor(a3[:, :, GB:P], a3[:, :, GB:P],
                                bank[2 + t][:, :].rearrange("p (h n) -> p h n", h=GH)[:, :, GB:P], ALU.add)\
                 .then_inc(S["att"], 1)
            dve.wait_ge(S["far_exp"], 2)
            V.tensor_tensor(kbar, kbar, gk[:, 0, :], ALU.mult)
            V.tensor_tensor(qbar, qbar, gq[:, 1, :], ALU.mult).then_inc(S["far_ops"], 1)
            dve.wait_ge(S["gla_vr"], 8)
            r4 = gr.rearrange("p t (h d) -> p t h d", h=GH)
            link(V.tensor_tensor(r4, r4, bc(bc(sml[:, R_ON:R_ON + 256], 1, GH), 1, NT), ALU.mult))
            dve.wait_ge(S["gla_rstd"], 1)
            for i in range(NT * GH):
                t, h = i // GH, i % GH
                b = bank[GLA_BANKS[i // 2]]
                V.scalar_tensor_tensor(hn[:, t, h * 256:(h + 1) * 256], b[:, i % 2 * 256:(i % 2 + 1) * 256],
                                       ors[:, i:i + 1], gr[:, t, h * 256:(h + 1) * 256], ALU.mult, ALU.mult)\
                 .then_inc(S["mixed"], 1)
            turned(4)
            residual(U_C_OUT)
            if stop < 5:
                return

            norm(3)
            turned(5, 3)
            for t in range(NT):
                dve.wait_ge(S["hn_hi"], t + 1)
                V.tensor_tensor(hn_lo[:, t, :], hn[:, t, :], hn_hi[:, t, :].bitcast(F32), ALU.subtract)\
                 .then_inc(S["hn_lo"], 1)
            dve.wait_ge(S["logits"], 1)
            link(V.tensor_copy(lg, bank[0][:, 0:16].rearrange("p (t n) -> p t n", t=NT)))
            for t in range(NT):
                link(V.max(mx[:, t, :], lg[:, t, :]))
                link(V.max_index(mxi[:, t, :], mx[:, t, :], lg[:, t, :]))
            link(V.tensor_copy(idf, mxi[:, :, :]))
            V.tensor_tensor(ee, mx[:, :, 1], mx[:, :, 0], ALU.subtract).then_inc(S["gap"], 1)
            for t in range(NT):
                for w in range(2):
                    V.tensor_scalar(oh[:, w, t, :], iota[:, 0:8], idf[:, t, w:w + 1], None, ALU.is_equal)
            link(V.memset(slot[:, :, :], -1.0))
            V.tensor_tensor(picked, oh[:, 0, :, :], oh[:, 1, :, :], ALU.add).then_inc(S["picked"], 1)
            dve.wait_ge(S["gap_exp"], 1)
            link(V.tensor_scalar(w12[:, :, 0], ee, 1.0, None, ALU.add))
            link(V.reciprocal(w12[:, :, 0], w12[:, :, 0]))
            link(V.tensor_tensor(w12[:, :, 1], w12[:, :, 0], ee, ALU.mult))
            link(V.memset(gate[:, :, :], 0.0))
            for t in range(NT):
                link(V.tensor_scalar(gate[:, t, 0:8], oh[:, 0, t, :], w12[:, t, 0:1], None, ALU.mult))
                link(V.scalar_tensor_tensor(gate[:, t, 0:8], oh[:, 1, t, :], w12[:, t, 1:2], gate[:, t, 0:8],
                                            ALU.mult, ALU.add))
            dve.wait_ge(S["rank"], 1)
            dve.wait_ge(S["picked"], 1)
            link(V.tensor_tensor(slot[:, :, 0:8], bank[1][:, 0:16].rearrange("p (t n) -> p t n", t=NT), picked, ALU.mult))
            link(V.tensor_scalar(slot[:, :, 0:8], slot[:, :, 0:8], -1.0, None, ALU.add))
            link(V.tensor_scalar(over[:, 0, :], bank[1][:, 16:24], float(CAP), None, ALU.is_gt))
            link(V.tensor_tensor_scan(over[:, 1, :], ones[:, 0:8], over[:, 0, :], 0.0, ALU.mult, ALU.add))
            V.tensor_copy(ovf[:, 0:1], over[:, 1, 7:8])
            for r in range(OVER_ROUNDS):
                sel = over[:, 2 + r, :]
                link(V.scalar_tensor_tensor(sel, over[:, 1, :], float(r + 1), over[:, 0, :], ALU.is_equal, ALU.mult))
                for col, shift in ((slot, -float(CAP)), (gate, 0.0)):
                    link(V.tensor_tensor(ovt, col[:, :, 0:8], bc(sel, 1, NT), ALU.mult))
                    link(V.tensor_reduce(col[:, :, NE + r], ovt, AX.X, ALU.add))
                    link(V.tensor_scalar(col[:, :, NE + r], col[:, :, NE + r], shift, None, ALU.add))
                link(V.tensor_tensor(ovt[:, 0, :], iota[:, 0:8], sel, ALU.mult))
                link(V.tensor_reduce(ovf[:, 1 + r:2 + r], ovt[:, 0, :], AX.X, ALU.add))
            V.tensor_copy(ovi[:, :], ovf[0:1, :]).then_inc(S["route"], 1)

            def prepare(e):
                V.tensor_copy(cur[:, 0, :].unsqueeze(2), slot[:, :, bass.ds(e + 1, 1)]).then_inc(S["cur"], 1)
                V.tensor_copy(cur[:, 1, :].unsqueeze(2), gate[:, :, bass.ds(e + 1, 1)]).then_inc(S["cur"], 1)
                dve.wait_ge(S["cur"], (e + 1) * 2 + 2)
                V.tensor_scalar(disp[:, 0, :], iota, cur[:, 0, 0:1], None, ALU.is_equal)
                V.tensor_scalar(disp[:, 1, :], iota, cur[:, 0, 1:2], None, ALU.is_equal).then_inc(S["disp"], 1)

            def gathered(e, half):
                dve.wait_ge(S["xg_psum"], (e + 1) * 2 + (half + 1))
                gc = R_NORM + NK * 3 + 4 * half
                V.tensor_tensor(esc[:, half, :].rearrange("p (k n) -> p k n", k=4),
                                bank[3][:, :].rearrange("p (k n) -> p k n", k=4),
                                bc(sml[:, gc:gc + 4], 2, P), ALU.mult).then_inc(S["xg_tmp"], 1)

            def gathered_lower(e, par, half):
                at = (slice(None), slice(half * 4, half * 4 + 4), slice(par * P, (par + 1) * P))
                dve.wait_ge(S["xg_hi"], (e + 1) * 2 + (half + 1))
                V.tensor_tensor(hT_lo[at], esc[:, half, :].rearrange("p (k n) -> p k n", k=4),
                                hT_hi[at].bitcast(F32), ALU.subtract).then_inc(S["xg"], 1)

            def sums_lower(e):
                for half in range(2):
                    dve.wait_ge(S["y_hi"], e * 2 + (half + 1))
                    ys = slice(half * BLK, (half + 1) * BLK)
                    V.scalar_tensor_tensor(y_lo[:, ys], bank[4 + half][:, :], gslot[:, 0:1], y_hi[:, ys].bitcast(F32),
                                           ALU.mult, ALU.subtract).then_inc(S["ysb"], 1)

            def scattered(e, halves):
                for i in halves:
                    t, half = i // 2, i % 2
                    dve.wait_ge(S["scat"], e * 4 + (i + 1))
                    xs = x[:, t, half * BLK:(half + 1) * BLK]
                    V.tensor_tensor(xs, xs, bank[6 + i % 2][:, :], ALU.add).then_inc(S["x_ready"], 1)

            def expert(e, base, par, fresh=False, drain=False, second=False):
                def split_unit(pos):
                    if pos >= EXP_UNITS and drain:
                        return
                    u = base + pos
                    dve.wait_ge(S["w_hi"], e * EXP_UNITS + (U_MOE + pos + 1))
                    V.tensor_tensor(wlo[:, u % SPLIT, :, :], raw[:, u % RAW, :, :],
                                    whi[:, u % SPLIT, :, :].bitcast(F32), ALU.subtract).then_inc(S["w_lo"], 1)

                def hidden_lower(c):
                    dve.wait_ge(S["m_h2_hi"], e * NCH + (c + 1))
                    V.tensor_tensor(h2_lo[:, (par + c) % 2, :], bank[2][:, 0:CH],
                                    h2_hi[:, (par + c) % 2, :].bitcast(F32), ALU.subtract).then_inc(S["m_h2T"], 1)

                if second:
                    prepare(e - 1)
                    for half in range(2):
                        gathered(e - 1, half)
                        gathered_lower(e - 1, par, half)
                    for pos in range(SPLIT):
                        split_unit(pos)
                for c in range(NCH):
                    split_unit(pos_g(c, 0, fresh) + SPLIT)
                    if c == 2 and not fresh:
                        sums_lower(e - 1)
                    dve.wait_ge(S["m_silu"], e * NCH + (c + 1))
                    V.tensor_tensor(hact[:, (par + c) % 2, :], sg[:, (par + c) % 2, :],
                                    bank[(par + c) % 2][:, CH:2 * CH], ALU.mult).then_inc(S["m_hact"], 1)
                    split_unit(pos_g(c, 1, fresh) + SPLIT)
                    if c or not fresh:
                        hidden_lower(c - 1)
                    if not drain and c == TURN + 1:
                        dve.wait_ge(S["combT"], e + 1)
                        prepare(e)
                    if not drain and c in (GATHER + 1, GATHER + 2):
                        gathered_lower(e, 1 - par, c - GATHER - 1)
                    if c >= 2 or not fresh:
                        split_unit(pos_d(c - 2, drain) + SPLIT)
                    if not fresh and c in (SCATTER, SCATTER + 1):
                        scattered(e - 1, (0, 1) if c == SCATTER else (2, 3))
                    if not drain and c in (GATHER, GATHER + 1):
                        gathered(e, c - GATHER)
                if drain:
                    hidden_lower(NCH - 1)
                    sums_lower(e)
                    scattered(e, range(4))

            prepare(-1)
            gathered(-1, 0)
            gathered_lower(-1, 0, 0)
            gathered(-1, 1)
            gathered_lower(-1, 0, 1)
            expert(0, U_MOE, 0, fresh=True)
            with dve.Fori(1, NE - 1, 2) as e:
                expert(e, U_MOE + EXP_UNITS, 1)
                expert(e + 1, U_MOE + 2 * EXP_UNITS, 0)
            expert(NE - 1, U_MOE + (NE - 1) * EXP_UNITS, 1, drain=True)
            dve.wait_ge(S["route"], 1)
            n_over = dve.value_load(ovi[0:1, 0:1], min_val=0, max_val=OVER_ROUNDS)
            with dve.Fori(NE, NE + OVER_ROUNDS) as e:
                with dve.If(n_over > e - NE):
                    expert(e, U_END, 0, fresh=True, drain=True, second=True)


def pack_blocks(w, order=None):
    rows, cols = w.shape
    n = -(-cols // BLK)
    out = np.zeros((n, rows // P, P, BLK), np.float32)
    for c in range(n):
        part = w[:, c * BLK:(c + 1) * BLK]
        out[c, :, :, :part.shape[1]] = part.reshape(rows // P, P, -1)
    return out.reshape(-1, P, BLK)


def pack_ffn(wg, wu, wd):
    g = wg.reshape(NK, P, NCH, CH).transpose(2, 0, 1, 3)
    u = wu.reshape(NK, P, NCH, CH).transpose(2, 0, 1, 3)
    d = wd.reshape(NCH, 2, P, 2, BLK).transpose(0, 1, 3, 2, 4).reshape(NCH, 4, P, BLK)
    return np.concatenate([np.concatenate([g, u], axis=3), d], axis=1)


def consumed():
    order = [(0, b) for b in range(8)]
    for c in range(1, NCH):
        order += [(c, b) for b in range(8)] + [(c - 1, b) for b in range(8, 12)]
    order += [(NCH - 1, b) for b in range(8, 12)]
    return np.array([o[0] for o in order]), np.array([o[1] for o in order])


def layout(inp):
    a = np.asarray
    w = a(inp["a_w_in"])[0]
    cut = np.cumsum([512, 128, 128, 128, 128, 128, 128, 24, 512, 512, 512])
    qa, kc, vc, ksl, vsl, kwn, vwn, ga, qb, kb, vb, fb = np.split(w, cut, axis=1)
    first = pack_blocks(np.concatenate([kc, vc, ksl, kwn], axis=1))
    second = pack_blocks(np.concatenate([vsl, vwn, ga, fb], axis=1))
    a_in = np.concatenate([first, second] + [pack_blocks(m) for m in (qa, qb, kb, vb)])
    cw = a(inp["c_w_in"])[0]
    fc, fb_ = consumed()
    parts = [a_in, pack_blocks(a(inp["a_w_out"])[0]),
             pack_ffn(a(inp["f_w_gate"])[0], a(inp["f_w_up"])[0], a(inp["f_w_down"])[0])[fc, fb_],
             pack_blocks(cw[:, 0:3072]), pack_blocks(a(inp["c_w_out"])[0])]
    stream = np.zeros((W_END, P, UB * BLK), np.float32)
    front = np.concatenate(parts)
    stream[0:U_MOE] = front.reshape(U_MOE, UB, P, BLK).transpose(0, 2, 1, 3).reshape(U_MOE, P, UB * BLK)
    for e in range(NE):
        blocks = pack_ffn(a(inp["m_w_gate"])[0, e], a(inp["m_w_up"])[0, e], a(inp["m_w_down"])[0, e])
        units = blocks.reshape(NCH, CHUNK_UNITS, UB, P, BLK).transpose(0, 1, 3, 2, 4).reshape(NCH, CHUNK_UNITS, P, -1)
        at = U_MOE + e * EXP_UNITS
        for i, first in enumerate((at, at + 1, at + 8)):
            stream[first:first + EXP_UNITS:CHUNK_UNITS] = units[:, i]
    small = np.zeros((P, R_END), np.float32)
    for at, name in ((R_QN, "a_q_norm"), (R_KN, "a_k_norm"), (R_FQ, "a_fox_q_norm"), (R_FK, "a_fox_k_norm"),
                     (R_ON, "c_o_norm"), (R_GB, "a_gate_bias"), (R_FB, "a_fox_f_bias")):
        v = a(inp[name])[0]
        small[:, at:at + v.shape[0]] = v[None, :]
    for i, name in enumerate(("a_norm", "f_norm", "c_norm", "m_norm")):
        small[:, R_NORM + NK * i:R_NORM + NK * (i + 1)] = a(inp[name])[0].reshape(NK, P).T
    small[:, R_BA:R_BA + GH] = a(inp["c_b_a"])[0].reshape(GH, P).T
    small[:, R_ROUTER:R_ROUTER + NK * NE] = a(inp["m_router"])[0].reshape(NK, P, NE).transpose(1, 0, 2).reshape(P, -1)
    small[:, R_A1:R_A1 + NK * 16] = cw[:, 3072:3088].reshape(NK, P, 16).transpose(1, 0, 2).reshape(P, -1)
    for v, name in enumerate(("a_pe_k", "a_pe_v")):
        small[:, R_PE + 16 * v:R_PE + 16 * (v + 1)] = a(inp[name])[0].reshape(16, P).T
    comp = np.zeros((P, 2176), np.float32)
    for v, c in enumerate("kv"):
        comp[:, 1024 * v:1024 * (v + 1)] = a(inp[f"a_cmp_{c}_w1"])[0].reshape(16, P, HD).transpose(1, 0, 2).reshape(P, -1)
        comp[0:HD, 2048 + HD * v:2048 + HD * (v + 1)] = a(inp[f"a_cmp_{c}_w2"])[0]
    return {"x": a(inp["x"])[0], "weights": stream, "constants": constants(), "masks": masks(), "small": small,
            "compress": comp, "w_a2": a(inp["c_w_a2"])[0]}


ARENA = 15616
TMP = {0: 0, 2: 4, 3: 8, 5: 12}
CROSS_SPLITS = {4: 9, 7: 10, 11: 11, 14: 12}
DIAG_SPLITS = {2: 13, 5: 14}
CONST_DMAS = 2
GLA_BANKS = (5, 6, 7, 0)
LIMITS = {1: U_A_OUT + 4, 2: U_FFN + 3, 3: U_C_IN + 3, 4: U_MOE, 5: U_END}


def kernel(**inputs):
    import concourse.bacc as bacc
    from concourse.bass_utils import run_bass_kernel_spmd

    nc = bacc.Bacc("TRN2", target_bir_lowering=False, num_devices=1)
    arrays = {k: np.ascontiguousarray(v) for k, v in layout(inputs).items()}
    d = {k: nc.dram_tensor("in_" + k, v.shape, mybir.dt.from_np(v.dtype), kind="ExternalInput").ap()
         for k, v in arrays.items()}
    out = nc.dram_tensor("out", (SEQ, DM), F32, kind="ExternalOutput").ap()
    trunk(nc, d["x"], d["weights"], d["constants"], d["masks"], d["small"], d["compress"], d["w_a2"], out, STOP)
    r = run_bass_kernel_spmd(nc, [{"in_" + k: v for k, v in arrays.items()}], core_ids=[0])
    return r.results[0]["out"].reshape(1, SEQ, DM)


STOP = 5
```

```python
from contextlib import ExitStack

import concourse.bass as bass
import numpy as np
from concourse import mybir

F32 = mybir.dt.float32
F32R = mybir.dt.float32r
BF16 = mybir.dt.bfloat16
I32 = mybir.dt.int32
U32 = mybir.dt.uint32
ALU = mybir.AluOpType
ACT = mybir.ActivationFunctionType
AX = mybir.AxisListType

P = 128
SEQ, DM = 256, 1024
NT = SEQ // P
NK = DM // P
HD = 64
NH = 8
NG = 2
NCMP = 15
EPS = 1e-6
NEG = -1e30
DFF = 2816
CH = 256
NCH = DFF // CH
BLK = 512
UB = 4
RAW = 6
SPLIT = 3
NE = 8
CAP = 128
SCATTER, TURN, GATHER = 2, 4, 6
OVER_ROUNDS = 3
GH = 4
GB = 8
GE = 32
NGE = P // GE
NED = NGE - 1 + GE // GB - 1

A_IN_CG, C_IN_CG = 6, 6
U_A_IN = 0
U_A_OUT = U_A_IN + A_IN_CG * NK // UB
U_FFN = U_A_OUT + 2 * NK // UB
CHUNK_UNITS = (NK + 4) // UB
U_C_IN = U_FFN + NCH * CHUNK_UNITS
U_C_OUT = U_C_IN + C_IN_CG * NK // UB
U_MOE = U_C_OUT + 2 * NK // UB
EXP_UNITS = NCH * CHUNK_UNITS
U_END = U_MOE + NE * EXP_UNITS
W_END = U_END + 6
EXP_ORDER = [0, 1, 3, 4] + [3 * c + i for c in range(2, NCH) for i in (0, 1, 2)] + [3 * NCH + 2, 3 * NCH + 5]
HOLES = (U_MOE + 2, U_MOE + 4, U_END - 2, U_END - 2, U_END - 1, U_END - 1)
FRONT_WIDTH = {1: 288}

C_ID, C_TRI, C_ONES, C_IOTA, C_BD = 0, 128, 256, 384, 512
C_BE = 640
C_SEL = 768
C_ROPE = C_SEL + GB + P
C_CROPE = C_ROPE + NT * 32
C_CBIAS = C_CROPE + 32
C_CMASK = C_CBIAS + NT * 16
C_HMASK = C_CMASK + NT * 16
C_REP = C_HMASK + 8
C_FOLD = C_REP + 2 * P
C_END = C_FOLD + NE
R_QN, R_KN, R_FQ, R_FK, R_ON, R_GB, R_FB = 0, 64, 128, 192, 256, 512, 536
R_NORM = 544
R_BA = R_NORM + 4 * NK
R_ROUTER = R_BA + GH
R_A1 = R_ROUTER + NK * NE
R_PE = R_A1 + NK * 16
R_END = R_PE + 2 * 16


def constants():
    c = np.zeros((P, C_END), np.float32)
    i = np.arange(P)
    c[:, C_ID:C_ID + P] = np.eye(P)
    c[:, C_TRI:C_TRI + P] = i[:, None] <= i[None, :]
    c[:, C_ONES:C_ONES + P] = 1.0
    c[:, C_IOTA:C_IOTA + P] = i[None, :]
    c[:, C_BD:C_BD + P] = (i[:, None] <= i[None, :]) & (i[:, None] // GB == i[None, :] // GB)
    c[:, C_BE:C_BE + P] = i[:, None] // GE == i[None, :] // GE
    c[:, C_SEL:C_SEL + GB + P] = np.arange(GB + P)[None, :] % GB == 0
    inv = np.float32(500000.0) ** (-np.arange(0, 16, 2, dtype=np.float32) / np.float32(16))

    def rope(pos):
        ang = pos.astype(np.float32)[:, None] * inv[None, :].astype(np.float32)
        co, si = np.cos(ang), np.sin(ang)
        return np.concatenate([co, co, -si, si], axis=1).astype(np.float32)

    for t in range(NT):
        c[:, C_ROPE + 32 * t:C_ROPE + 32 * (t + 1)] = rope(t * P + i)
    ends = np.arange(NCMP) * 16 + 31
    c[0:NCMP, C_CROPE:C_CROPE + 32] = rope(ends)
    c[NCMP:2 * NCMP, C_CROPE:C_CROPE + 32] = rope(ends)
    for t in range(NT):
        seen = (ends[None, :] <= (t * P + i)[:, None])
        c[:, C_CBIAS + 16 * t:C_CBIAS + 16 * t + NCMP] = np.where(seen, 0.0, NEG)
        c[:, C_CMASK + 16 * t:C_CMASK + 16 * t + NCMP] = seen
    c[:, C_HMASK:C_HMASK + 8] = i[:, None] // 16 == np.arange(8)[None, :]
    c[:, C_FOLD:C_FOLD + NE] = i[:, None] % NE == np.arange(NE)[None, :]
    for g in range(NG):
        rep = (i[:, None] == i[None, :] % 16) & (i[None, :] // 64 == g) & (i[:, None] < NCMP)
        c[:, C_REP + g * P:C_REP + (g + 1) * P] = rep
    return c


def masks():
    i = np.arange(P)
    m = np.zeros((P, 1024 + P), np.float32)
    late = np.where(i[:, None] >= i[None, :], 0.0, NEG)
    for h in range(4):
        m[:, h * P:(h + 1) * P] = late
    m[:, 512 + 128:512 + 256] = late
    m[:, 512 + 384:512 + 512] = late
    m[:, 1024:1024 + P] = np.eye(P)
    return (m.view(np.uint32) >> 16).astype(np.uint16)


def trunk(nc, x_d, w_d, const_d, mask_d, small_d, comp_d, wa2_d, out_d):
    ctx = ExitStack()
    with ctx:
        def sb(name, shape, dt=F32):
            return ctx.enter_context(nc.sbuf_tensor(name, shape, dt))

        def sem(name):
            return ctx.enter_context(nc.semaphore(name))

        raw = sb("raw", [P, RAW, UB, BLK])
        whi = sb("whi", [P, SPLIT, UB, BLK], F32R)
        wlo = sb("wlo", [P, SPLIT, UB, BLK], F32R)
        x = sb("x", [P, NT, DM])
        hn = sb("hn", [P, NT, DM])
        hT_hi = sb("hT_hi", [P, NK, SEQ], F32R)
        hT_lo = sb("hT_lo", [P, NK, SEQ], F32R)
        sw = sb("sw", [P, 384], F32R)
        cst = sb("cst", [P, C_END])
        msk_bits = sb("msk_bits", [P, 1024 + P], mybir.dt.uint16)
        msk = msk_bits[:, :].bitcast(BF16)
        sml = sb("sml", [P, R_END])
        wa2 = sb("wa2", [32, 512])
        ss = sb("ss", [P, NT])
        rstd = sb("rstd", [P, NT])
        mhalf = sb("mhalf", [P, 32])
        esc = sb("esc", [P, 2, 512])
        oss = sb("oss", [P, NT * GH])
        ors = sb("ors", [P, NT * GH])
        mxi = sb("mxi", [P, 2, 8], U32)
        ovi = sb("ovi", [1, 4], I32)
        arena_ctx = ExitStack()
        arena = arena_ctx.enter_context(nc.sbuf_tensor("arena", [P, ARENA], F32))

        class Carve:
            def __init__(self):
                self.at = 0

            def __call__(self, n, dt=F32):
                a = arena[:, self.at:self.at + n]
                self.at += n
                assert self.at <= ARENA, self.at
                return a

        sw_router = sw[:, 0:128].rearrange("p (k w n) -> p k w n", k=NK, w=2)
        sw_a1 = sw[:, 128:384].rearrange("p (k w n) -> p k w n", k=NK, w=2)
        small_weights = [(sw_router, sml[:, R_ROUTER:R_ROUTER + NK * NE].rearrange("p (k n) -> p k n", k=NK)),
                         (sw_a1, sml[:, R_A1:R_A1 + NK * 16].rearrange("p (k n) -> p k n", k=NK))]
        ident = cst[:, C_ID:C_ID + P]
        tri = cst[:, C_TRI:C_TRI + P]
        ones = cst[:, C_ONES:C_ONES + P]
        iota = cst[:, C_IOTA:C_IOTA + P]
        mbd = cst[:, C_BD:C_BD + P]
        mbe = cst[:, C_BE:C_BE + P]
        mident = msk[:, 1024:1024 + P]

        bank = [ctx.enter_context(nc.psum_tensor(f"bank{i}", [P, 512], F32)) for i in range(8)]

        c0 = Carve()
        front = c0(A_IN_CG * NT * BLK)
        proj4 = front.rearrange("p (c t n) -> p c t n", c=A_IN_CG, t=NT)
        proj = [proj4[:, i, :, :] for i in (5, 0, 2, 3, 4, 1)]
        qT = c0(NH * SEQ).rearrange("p (h n) -> p h n", h=NH)
        keyT = c0(4 * SEQ).rearrange("p (h n) -> p h n", h=4)
        fqT = front[:, 2048:4096].rearrange("p (h n) -> p h n", h=NH)
        fkT = front[:, 4096:6144].rearrange("p (h n) -> p h n", h=NH)
        scr0 = c0.at
        cw1 = c0(2 * 16 * HD).rearrange("p (v j d) -> p v j d", v=2, j=16)
        cw2 = c0(2 * HD).rearrange("p (v d) -> p v d", v=2)
        kc2 = esc[:, :, :].rearrange("p b n -> p (b n)").rearrange("p (v g n) -> p v g n", v=2, g=NG)
        blkT = c0(2 * 16 * 30).rearrange("p (v j g n) -> p v j g n", v=2, j=16, g=NG)
        assert c0.at - scr0 >= 2560
        pbuf = arena[:, scr0:scr0 + 1024].rearrange("p (b n) -> p b n", b=2)
        ptb = arena[:, scr0 + 1024:scr0 + 2048].rearrange("p (b n) -> p b n", b=2)
        tmpo = arena[:, scr0 + 2048:scr0 + 2560]
        sq = hn[:, :, :].rearrange("p t n -> p (t n)")
        faug = arena[:, scr0:scr0 + 2 * NT * NH * 66].rearrange("p (w t h n) -> p w t h n", w=2, t=NT, h=NH)
        hss = c0(6 * 32).rearrange("p (w n) -> p w n", w=6)
        hrs = c0(6 * 32).rearrange("p (w n) -> p w n", w=6)
        rA = c0(256)
        rB = c0(256)
        gel = c0(4 * 64).rearrange("p (w n) -> p w n", w=4)
        kcm = c0(4 * 64).rearrange("p (w n) -> p w n", w=4)
        kcmpT = c0(32)
        vcmp = c0(2 * 64).rearrange("p (g d) -> p g d", g=2)
        vbd = c0(512)
        fz = c0(5 * 16).rearrange("p (w n) -> p w n", w=5)
        gat = c0(48)
        sc = c0(2 * 128).rearrange("p (t n) -> p t n", t=2)
        mc = c0(16)
        sumc = c0(16)
        facc = c0(16)
        pcT = c0(256).rearrange("p (t n) -> p t n", t=2)
        negm = c0(6 * 8).rearrange("p (s h) -> p s h", s=6)
        sums = c0(6 * 8).rearrange("p (s h) -> p s h", s=6)
        fac = c0(6 * 8).rearrange("p (s h) -> p s h", s=6)
        oacc = hn

        cg_ = Carve()
        gq = cg_(NT * 512).rearrange("p (t n) -> p t n", t=NT)
        gk = cg_(NT * 512).rearrange("p (t n) -> p t n", t=NT)
        gb = cg_(NT * 512).rearrange("p (t n) -> p t n", t=NT)
        gv = hn
        prod = cg_(GB * 512).rearrange("p (s n) -> p s n", s=GB)
        kt = cg_(NED * NT * 512).rearrange("p (i t n) -> p i t n", i=NED, t=NT)
        qt = cg_(2 * NT * 512).rearrange("p (i t n) -> p i t n", i=2, t=NT)
        a1T = cg_(SEQ)
        roots, root_diag = esc[:, 0, 0:SEQ], esc[:, 1, 0:SEQ]
        att, atmp = kt[:, 0, :, :], kt[:, 1, :, :]
        gr = kt[:, 2:4, :, :].rearrange("p i t n -> p (i t n)").rearrange("p (t n) -> p t n", t=NT)
        kbar, qbar, far = kt[:, 4, 0, :], kt[:, 5, 0, :], kt[:, 5, 1, :]

        def q_view(i):
            return qt[:, i, :, :].rearrange("p t n -> p (t n)")\
                .rearrange("p (g b r) -> p g b r", b=4, r=(GE, GB)[i])[:, :, 1:4, :]

        def before_edge(a_, i):
            block_, width = (P, (i + 1) * GE) if i < NGE - 1 else (GE, (i - NGE + 2) * GB)
            return a_.rearrange("p (g n) -> p g n", n=block_)[:, :, 0:width]

        def k_view(i):
            return before_edge(kt[:, i, :, :].rearrange("p t n -> p (t n)"), i)

        gz = prod[:, 0:2, :].rearrange("p s n -> p (s n)")
        ge = prod[:, 2:4, :].rearrange("p s n -> p (s n)")
        rmask = prod[:, 4:6, :].rearrange("p s n -> p (s n)")

        arena_ctx.close()
        sg = sb("sg", [P, 2, CH])
        hact = sb("hact", [P, 2, CH])
        h2_hi = sb("h2_hi", [P, 2, CH], F32R)
        h2_lo = sb("h2_lo", [P, 2, CH], F32R)
        hn_hi = sb("hn_hi", [P, NT, DM], F32R)
        hn_lo = sb("hn_lo", [P, NT, DM], F32R)
        y_hi = sb("y_hi", [P, DM], F32R)
        y_lo = sb("y_lo", [P, DM], F32R)
        disp = sb("disp", [P, NT, P], F32R)
        combT = sb("combT", [P, NT, P], F32R)
        gslot = sb("gslot", [P, 1])
        mtab = sb("mtab", [P, 400])
        tab_at = [0]

        def cf(n):
            a_ = mtab[:, tab_at[0]:tab_at[0] + n]
            tab_at[0] += n
            return a_

        lg = cf(16).rearrange("p (t n) -> p t n", t=2)
        mx = cf(16).rearrange("p (t n) -> p t n", t=2)
        idf = cf(16).rearrange("p (t n) -> p t n", t=2)
        ee = cf(2)
        w12 = cf(4).rearrange("p (t n) -> p t n", t=2)
        oh = cf(2 * 16).rearrange("p (w t n) -> p w t n", w=2, t=2)
        gate = cf(24).rearrange("p (t n) -> p t n", t=2)
        slot = cf(24).rearrange("p (t n) -> p t n", t=2)
        picked = cf(16).rearrange("p (t n) -> p t n", t=2)
        cur = cf(4).rearrange("p (w t) -> p w t", w=2)
        over = cf(2 * NE).rearrange("p (w n) -> p w n", w=2)
        osel = cf(OVER_ROUNDS * NE).rearrange("p (r n) -> p r n", r=OVER_ROUNDS)
        ovt = cf(NT * OVER_ROUNDS * NE).rearrange("p (t r n) -> p t r n", t=NT, r=OVER_ROUNDS)
        ovf = cf(4)

        NAMES = """x_in const_in late_in w_hi w_lo units_used x_ready ss rstd root_diag roots_psum roots
            tmp hT_psum hT_hi hT sw_hi sw_lo
            dve_chain act_chain pool_chain
            hn_lo hn_hi y_hi xg_tmp xg_hi h2_hi m_h2_hi proj kc_psum kc blk hid hid_in tanh gelu cmp2
            cmp2_sb kcmp_ss kcmp_rstd kcmp kcmpT_psum kcmpT vrep vbd head_ss head_rstd head_done gate_z
            gate_e fox_z fox_l fox_lf cum aug headT_psum headT foxT_psum foxT cmp_s cmp_d cmp_e cmp_p
            cmp_pT_psum cmp_pT cmp_o scores rowmax probs probsT_psum probsT pv o_done gu silu hact h2T_psum
            h2T a1 a1_sb z zb absz soft decay gla_qk gla_vr prod_zero kt_zero diag_arg diag_exp prod diag
            k_arg k_exp kt q_arg q_exp qt cross att far_arg far_exp far_ops far_psum far_sb gla_o gla_ss
            gla_rstd mixed first_rows logitsT_psum logitsT logits gap gap_exp picked rank route disp
            combT_psum combT rows_psum rows xg_psum xg cur m_silu m_hact m_h2T_psum m_h2T ysb scat out""".split()
        S = {n: sem(n) for n in NAMES}
        s_loaded = [sem(f"loaded{i}") for i in range(RAW)]

        def loads_before(slot_, u):
            return len(range(slot_, u, RAW))

        att_units = []
        for br in range(3):
            for t in range(NT):
                n = 4 if t == 0 else 2
                att_units += [(br, t, h0, n) for h0 in range(0, NH, n)]
        AU = len(att_units)

        def seq_of(u):
            return att_units[u][0] * NT + att_units[u][1]

        ends_seq = [u for u in range(AU) if u == AU - 1 or seq_of(u + 1) != seq_of(u)]
        steps = [(c, t) for c in range(NCH) for t in range(NT)]
        X_MOE = 12

        def dense_g(c, half):
            return half if c == 0 else 3 * c - 1 + half

        def dense_d(c):
            return 4 + 3 * c if c < NCH - 1 else EXP_UNITS - 1

        def pos_g(c, half, fresh):
            return (2 * c if fresh and c < 2 else 3 * c - 2) + half

        def pos_d(c, drain):
            return EXP_UNITS - NCH + c if drain and c >= NCH - 2 else 3 * c + 6

        def loads_main(e, base, pos):
            return e * (16 * EXP_UNITS // RAW) + 16 * ((base + pos) // RAW + 1)

        def loads_over(e, pos):
            sl = (U_END + pos) % RAW
            per_round = len(range(pos % RAW, EXP_UNITS, RAW))
            return (e - NE) * (16 * per_round) + 16 * (loads_before(sl, U_END) + pos // RAW + 1)

        block = ctx.enter_context(nc.Block())

        @block.sync
        def _(sp):
            def fetch(u):
                hole = sum(u >= at for at in HOLES)
                sp.dma_start(raw[:, u % RAW, :, :], w_d[u + hole, :, :].rearrange("p (b n) -> p b n", b=UB))\
                  .then_inc(s_loaded[u % RAW], 16)

            sp.dma_start(x[:, :, :], x_d.rearrange("(t p) n -> p t n", p=P)).then_inc(S["x_in"], 16)
            for dst, src in ((cst[:, :], const_d[:, :]), (sml[:, :], small_d[:, :])):
                sp.dma_start(dst, src).then_inc(S["const_in"], 16)
            for u in range(3):
                fetch(u)
            for dst, src in ((arena[:, scr0:scr0 + 2176], comp_d[:, :]), (msk_bits[:, :], mask_d[:, :]),
                             (wa2[:, :], wa2_d[:, :])):
                sp.dma_start(dst, src).then_inc(S["late_in"], 16)
            for u in range(3, RAW):
                fetch(u)
            def stream(first, last, hole):
                with sp.Fori(first, last) as it:
                    for s_ in range(RAW):
                        sp.wait_ge(S["w_lo"], (it - 1) * RAW + s_ + 1)
                        sp.dma_start(raw[:, s_, :, :], w_d[bass.ds(it * RAW + (s_ + hole), 1), :, :]
                                     .rearrange("a p (b n) -> p (a b) n", b=UB)).then_inc(s_loaded[s_], 16)

            def single(u):
                sp.wait_ge(S["w_lo"], u - RAW + 1)
                fetch(u)

            before, behind = (U_MOE + 2) // RAW, -(-(U_MOE + 4) // RAW)
            stream(1, before, 0)
            for u in range(before * RAW, behind * RAW):
                single(u)
            stream(behind, U_END // RAW, 2)
            for u in range(U_END // RAW * RAW, U_END):
                single(u)
            sp.wait_ge(S["route"], 1)
            n_over = sp.value_load(ovi[0:1, 0:1], min_val=0, max_val=OVER_ROUNDS)
            with sp.Fori(0, OVER_ROUNDS) as r:
                with sp.If(n_over > r):
                    who = sp.value_load(ovi[0:1, bass.ds(r + 1, 1)], min_val=0, max_val=NE - 1)
                    for i, at in enumerate(EXP_ORDER):
                        sp.wait_ge(S["w_lo"], r * EXP_UNITS + (U_END + max(0, i - RAW + 1)))
                        sl = (U_END + i) % RAW
                        sp.dma_start(raw[:, sl, :, :],
                                     w_d[bass.ds(who * EXP_UNITS + (U_MOE + at), 1), :, :]
                                     .rearrange("a p (b n) -> p (a b) n", b=UB)).then_inc(s_loaded[sl], 16)
            for t in range(NT):
                sp.wait_ge(S["x_ready"], n_over * 4 + (X_MOE + 4 * NE - 2 * (NT - 1 - t)))
                sp.dma_start(out_d[t * P:(t + 1) * P, :], x[:, t, :]).then_inc(S["out"], 16)
            sp.wait_ge(S["out"], NT * 16)

        @block.gpsimd
        def _(pool):
            chain = [0]

            def link(ins):
                chain[0] += 1
                ins.then_inc(S["pool_chain"], 1)
                pool.wait_ge(S["pool_chain"], chain[0])

            def inv_root(out, in_, width, n, done):
                r = in_.shape[0]
                link(nc.gpsimd.tensor_scalar(in_, in_, 1.0 / width, EPS, ALU.mult, ALU.add))
                nc.gpsimd.tensor_tensor(out, in_, mhalf[0:r, 0:n], ALU.pow).then_inc(S[done], 1)

            link(nc.gpsimd.memset(mhalf[:], -0.5))

            def norm(n):
                pool.wait_ge(S["ss"], NT * (n + 1))
                inv_root(rstd[:], ss[:], DM, NT, "rstd")

            norm(0)
            for i, n in enumerate((8, 16, 16, 16)):
                pool.wait_ge(S["head_ss"], i + 1)
                inv_root(hrs[:, i, 0:n], hss[:, i, 0:n], HD, n, "head_rstd")
                if i == 1:
                    pool.wait_ge(S["kcmp_ss"], 1)
                    inv_root(hrs[0:30, 4, 0:1], hss[0:30, 4, 0:1], HD, 1, "kcmp_rstd")
            norm(1)
            norm(2)
            pool.wait_ge(S["x_ready"], 8)
            nc.gpsimd.memset(kt, 0.0).then_inc(S["kt_zero"], 1)
            pool.wait_ge(S["decay"], 1)
            nc.gpsimd.memset(prod, 0.0).then_inc(S["prod_zero"], 1)
            for t in range(NT):
                pool.wait_ge(S["gla_ss"], GH * (t + 1))
                inv_root(ors[:, t * GH:(t + 1) * GH], oss[:, t * GH:(t + 1) * GH], 256, GH, "gla_rstd")
            norm(3)

        @block.tensor
        def _(pe):
            mm = nc.tensor.matmul

            def mm3(out_, a_hi, a_lo, b_hi, b_lo, start, stop):
                mm(out_, a_hi, b_hi, start=start, stop=False)
                mm(out_, a_hi, b_lo, start=False, stop=False)
                return mm(out_, a_lo, b_hi, start=False, stop=stop)

            def transposes(src, ready):
                for i in range(4):
                    half, t = i // 2, i % 2
                    ready(i)
                    for j in range(4):
                        k = half * 4 + j
                        last = nc.tensor.transpose(bank[i][:, j * P:(j + 1) * P], src[:, t, k * P:(k + 1) * P], ident)
                    last.then_inc(S["hT_psum"], 1)

            def turned_k(g, k):
                if k % 4 == 0:
                    pe.wait_ge(S["hT"], 4 * g + 2 + k // 2)

            def small_products(g, parts, dst):
                for k in range(NK):
                    turned_k(g, k)
                    w = parts[:, k, :, :].rearrange("p w n -> p (w n)")
                    mm(dst, w, hT_hi[:, k, :], start=(k == 0), stop=False)
                    last = mm(dst, w, hT_lo[:, k, :], start=False, stop=(k == NK - 1))
                return last

            def block_at(u0, b):
                u = u0 + b // UB
                return whi[:, u % SPLIT, b % UB, :], wlo[:, u % SPLIT, b % UB, :]

            def group(u0, cg, banks, width=BLK, turn=None):
                for k in range(NK):
                    b = cg * NK + k
                    if turn is not None:
                        turned_k(turn, k)
                    if b % UB == 0:
                        pe.wait_ge(S["w_lo"], u0 + b // UB + 1)
                    w_h, w_l = block_at(u0, b)
                    for t in range(NT):
                        last = mm3(bank[banks[t]][:, 0:width], hT_hi[:, k, t * P:(t + 1) * P],
                                   hT_lo[:, k, t * P:(t + 1) * P], w_h[:, 0:width], w_l[:, 0:width],
                                   k == 0, k == NK - 1)
                    if b % UB == UB - 1:
                        last.then_inc(S["units_used"], 1)

            pe.wait_ge(S["const_in"], CONST_DMAS * 16)
            transposes(x, lambda i: pe.wait_ge(S["x_in"], 16))

            def in_group(cg):
                if cg >= 2:
                    pe.wait_ge(S["proj"], 2 * (cg - 1))
                b = 4 + 2 * (cg % 2)
                group(U_A_IN, cg, (b, b + 1), FRONT_WIDTH.get(cg, BLK), 0 if cg == 0 else None)

            in_group(0)
            in_group(1)
            pe.wait_ge(S["proj"], 2)
            for v in range(2):
                for g in range(NG):
                    for t in range(NT):
                        last = nc.tensor.transpose(bank[v][0:HD, (g * NT + t) * P:(g * NT + t + 1) * P],
                                                   proj[0][:, t, v * P + g * HD:v * P + (g + 1) * HD], ident)
                last.then_inc(S["kc_psum"], 1)
            in_group(2)
            pe.wait_ge(S["late_in"], 48)
            pe.wait_ge(S["blk"], 4)
            for v in range(2):
                for j in range(16):
                    last = mm(bank[2][0:HD, v * 32:v * 32 + 30], cw1[:, v, j, :],
                              blkT[:, v, j, :, :].rearrange("p g n -> p (g n)"), start=(j == 0), stop=(j == 15))
            last.then_inc(S["hid"], 1)
            pe.wait_ge(S["head_done"], 1)
            pe.wait_ge(S["kc"], 4)
            for t in range(NT):
                for kk in range(4):
                    last = nc.tensor.transpose(bank[t][0:HD, kk * P:(kk + 1) * P],
                                               proj[0][:, t, 256 + kk * HD:256 + (kk + 1) * HD], ident)
                last.then_inc(S["headT_psum"], 1)
            in_group(3)
            pe.wait_ge(S["gelu"], 1)
            mm(bank[3][0:30, 0:HD], gel[0:HD, 3, 0:30], cw2[0:HD, 0, :], start=True, stop=True)
            for g in range(NG):
                last = mm(bank[3][0:NCMP, (g + 1) * HD:(g + 2) * HD], gel[0:HD, 3, 30 + NCMP * g:30 + NCMP * (g + 1)],
                          cw2[0:HD, 1, :], start=True, stop=True)
            last.then_inc(S["cmp2"], 1)
            in_group(4)
            pe.wait_ge(S["cmp2_sb"], 1)
            for g in range(NG):
                last = mm(bank[2][:, 0:HD], cst[0:NCMP, C_REP + g * P:C_REP + (g + 1) * P], vcmp[0:NCMP, g, :],
                          start=(g == 0), stop=(g == NG - 1))
            last.then_inc(S["vrep"], 1)
            pe.wait_ge(S["kcmp"], 1)
            nc.tensor.transpose(bank[3][0:HD, 256:286], kcm[0:30, 3, :], ident[0:30, 0:30]).then_inc(S["kcmpT_psum"], 1)
            in_group(5)
            pe.wait_ge(S["head_done"], 2)
            pe.wait_ge(S["vbd"], 1)
            pe.wait_ge(S["kcmpT"], 1)
            for i in range(4):
                t, half = i // 2, i % 2
                if i < 2:
                    pe.wait_ge(S["headT"], i + 1)
                for j in range(4):
                    h = half * 4 + j
                    last = nc.tensor.transpose(bank[i][0:HD, j * P:(j + 1) * P],
                                               proj[2][:, t, h * HD:(h + 1) * HD], ident)
                last.then_inc(S["headT_psum"], 1)
            pe.wait_ge(S["headT"], 3)
            pe.wait_ge(S["fox_lf"], 1)
            mm(bank[0][:, 0:8], tri, fz[:, 4, 0:8], start=True, stop=True)
            mm(bank[0][:, 8:16], ones, fz[:, 4, 0:8], start=True, stop=False)
            mm(bank[0][:, 8:16], tri, fz[:, 4, 8:16], start=False, stop=True).then_inc(S["cum"], 1)
            pe.wait_ge(S["proj"], 12)
            pe.wait_ge(S["headT"], 6)
            for t in range(NT):
                for h in range(NH):
                    g = h // 4
                    last = mm(bank[6][:, t * P + h * 16:t * P + h * 16 + NCMP], qT[0:HD, h, t * P:(t + 1) * P],
                              kcmpT[0:HD, g * NCMP:(g + 1) * NCMP], start=True, stop=True)
            last.then_inc(S["cmp_s"], 1)
            pe.wait_ge(S["aug"], 1)
            for i in range(8):
                w, t, half = i // 4, i // 2 % 2, i % 2
                if i % 4 == 0:
                    pe.wait_ge(S["head_done"], 3 + w)
                if i >= 4:
                    pe.wait_ge(S["foxT"], i - 3)
                for j in range(4):
                    h = half * 4 + j
                    last = nc.tensor.transpose(bank[i % 4][0:66, j * P:(j + 1) * P], faug[:, w, t, h, :], ident)
                last.then_inc(S["foxT_psum"], 1)
            pe.wait_ge(S["cmp_p"], 1)
            for t in range(NT):
                last = nc.tensor.transpose(bank[7][:, t * P:(t + 1) * P], sc[:, t, :], ident)
            last.then_inc(S["cmp_pT_psum"], 1)
            pe.wait_ge(S["cmp_pT"], 1)
            for t in range(NT):
                mm(bank[4 + t][:, :], pcT[:, t, :], vbd, start=True, stop=True).then_inc(S["cmp_o"], 1)

            def qk(u):
                br, t, h0, n = att_units[u]
                kw = (t + 1) * P
                b = bank[SCORE_BANKS[u % 3]]
                if u >= 3:
                    pe.wait_ge(S["probs"], u - 2)
                mm(b[:, :], mident, msk[:, 512 * t:512 * t + 512], start=True, stop=False)
                for j in range(n):
                    h = h0 + j
                    if br < 2:
                        q, k = qT[0:HD, h, t * P:(t + 1) * P], keyT[0:HD, br * 2 + h // 4, 0:kw]
                    else:
                        q, k = fqT[0:66, h, t * P:(t + 1) * P], fkT[0:66, h, 0:kw]
                    last = mm(b[:, j * kw:(j + 1) * kw], q, k, start=False, stop=(j == n - 1))
                last.then_inc(S["scores"], 1)

            def turn(u):
                pe.wait_ge(S["probs"], u + 1)
                if u >= 2:
                    pe.wait_ge(S["probsT"], u - 1)
                for j in range(4):
                    last = nc.tensor.transpose(bank[2 + u % 2][:, j * P:(j + 1) * P],
                                               pbuf[:, u % 2, j * P:(j + 1) * P], ident)
                last.then_inc(S["probsT_psum"], 1)

            def pv(u):
                br, t, h0, n = att_units[u]
                sq_ = seq_of(u)
                pe.wait_ge(S["probsT"], u + 1)
                if u == 0 or seq_of(u - 1) != sq_:
                    pe.wait_ge(S["o_done"], sq_ + 1)
                for j in range(n):
                    h = h0 + j
                    for kt_ in range(t + 1):
                        if br < 2:
                            v = proj[1][:, kt_, br * P + (h // 4) * HD:br * P + (h // 4 + 1) * HD]
                        else:
                            v = proj[5][:, kt_, h * HD:(h + 1) * HD]
                        m = j * (t + 1) + kt_
                        last = mm(bank[4 + sq_ % 2][:, h * HD:(h + 1) * HD], ptb[:, u % 2, m * P:(m + 1) * P], v,
                                  start=(kt_ == 0), stop=(kt_ == t))
                last.then_inc(S["pv"], 1)

            pe.wait_ge(S["foxT"], 8)
            qk(0)
            qk(1)
            for u in range(AU):
                if u + 2 < AU:
                    qk(u + 2)
                turn(u)
                if u >= 1:
                    pv(u - 1)
            pv(AU - 1)
            transposes(hn, lambda i: pe.wait_ge(S["o_done"], 8))
            group(U_A_OUT, 0, (4, 5), turn=1)
            group(U_A_OUT, 1, (6, 7))
            transposes(x, lambda i: pe.wait_ge(S["x_ready"], i + 1))

            def gate_up(i, half):
                c, t = steps[i]
                u = U_FFN + dense_g(c, half)
                if t == 0:
                    pe.wait_ge(S["w_lo"], u + 1)
                if half == 0 and i >= 2:
                    pe.wait_ge(S["hact"], i - 1)
                if i < 2:
                    pe.wait_ge(S["hT"], 8 + 2 * half + t + 1)
                for k in range(4 * half, 4 * half + 4):
                    last = mm3(bank[i % 2][:, :], hT_hi[:, k, t * P:(t + 1) * P], hT_lo[:, k, t * P:(t + 1) * P],
                               *block_at(u, k % 4), k == 0, k == NK - 1)
                if t == 1:
                    last.then_inc(S["units_used"], 1)
                elif half:
                    last.then_inc(S["gu"], 1)

            def hidden_T(i):
                pe.wait_ge(S["hact"], i + 1)
                if i:
                    pe.wait_ge(S["h2T"], i)
                for j in range(2):
                    last = nc.tensor.transpose(bank[2][:, j * P:(j + 1) * P], hact[:, i % 2, j * P:(j + 1) * P], ident)
                last.then_inc(S["h2T_psum"], 1)

            def down(i):
                c, t = steps[i]
                u = U_FFN + dense_d(c)
                if t == 0:
                    pe.wait_ge(S["w_lo"], u + 1)
                pe.wait_ge(S["h2T"], i + 1)
                for j in range(2):
                    for half in range(2):
                        last = mm3(bank[4 + 2 * t + half][:, :], h2_hi[:, i % 2, j * P:(j + 1) * P],
                                   h2_lo[:, i % 2, j * P:(j + 1) * P], *block_at(u, 2 * j + half),
                                   c == 0 and j == 0, c == NCH - 1 and j == 1)
                if t == 1:
                    last.then_inc(S["units_used"], 1)
                elif c == NCH - 1:
                    last.then_inc(S["first_rows"], 1)

            n = len(steps)
            for i in range(n):
                gate_up(i, 0)
                gate_up(i, 1)
                if i >= 1:
                    hidden_T(i - 1)
                if i >= 2:
                    down(i - 2)
            down(n - 2)
            hidden_T(n - 1)
            down(n - 1)

            transposes(x, lambda i: pe.wait_ge(S["x_ready"], 4 + 2 * (i % 2) + i // 2 + 1))
            pe.wait_ge(S["sw_lo"], 2)
            small_products(3, sw_a1, bank[6][0:32, 0:SEQ]).then_inc(S["a1"], 1)

            def spread_roots():
                pe.wait_ge(S["root_diag"], 1)
                for t in range(NT):
                    last = mm(bank[7][:, t * P:(t + 1) * P], ones, root_diag[:, t * P:(t + 1) * P], start=True, stop=True)
                last.then_inc(S["roots_psum"], 1)

            def channels(cg, b0):
                for k in range(NK):
                    b = cg * NK + k
                    if b == UB:
                        spread_roots()
                    if b % UB == 0:
                        pe.wait_ge(S["w_lo"], U_C_IN + b // UB + 1)
                    w_h, w_l = block_at(U_C_IN, b)
                    for m in range(GH):
                        c = slice(m * P, (m + 1) * P)
                        last = mm3(bank[b0 + m][:, 0:SEQ], w_h[:, c], w_l[:, c], hT_hi[:, k, :], hT_lo[:, k, :],
                                   k == 0, k == NK - 1)
                    if b % UB == UB - 1:
                        last.then_inc(S["units_used"], 1)

            channels(0, 0)
            pe.wait_ge(S["a1_sb"], 1)
            for h in range(GH):
                last = mm(bank[4 + h // 2][:, h % 2 * SEQ:(h % 2 + 1) * SEQ], wa2[:, h * P:(h + 1) * P], a1T[0:32, :],
                          start=True, stop=True)
            last.then_inc(S["z"], 1)
            pe.wait_ge(S["zb"], 1)
            channels(1, 4)
            pe.wait_ge(S["gla_qk"], 4)
            group(U_C_IN, 2, (0, 1))
            group(U_C_IN, 3, (2, 3))
            pe.wait_ge(S["gla_qk"], 8)
            group(U_C_IN, 4, (4, 5))

            def diagonal(t):
                pe.wait_ge(S["prod"], GB * (t + 1))
                for s_ in range(GB):
                    last = mm(bank[t][:, :], cst[:, C_SEL + GB - s_:C_SEL + GB - s_ + P], prod[:, s_, :],
                              start=(s_ == 0), stop=(s_ == GB - 1))
                last.then_inc(S["diag"], 1)

            def cross(t):
                if t:
                    pe.wait_ge(S["att"], t)
                for h in range(GH):
                    hs = slice(h * P, (h + 1) * P)
                    for i in range(1, NGE):
                        at = h * P + i * GE
                        mm(bank[2][:, at:at + GE], kt[:, i - 1, t, hs], qt[:, 0, t, at:at + GE], start=True, stop=True)
                    for j in range(1, GE // GB):
                        inner = slice(j * GB, (j + 1) * GB)
                        last = mm(bank[3][:, hs].rearrange("p (b r) -> p b r", r=GE)[:, :, inner],
                                  kt[:, NGE - 2 + j, t, hs],
                                  qt[:, 1, t, hs].rearrange("p (b r) -> p b r", r=GE)[:, :, inner],
                                  start=True, stop=True)
                last.then_inc(S["cross"], 1)

            pe.wait_ge(S["gla_vr"], 4)
            diagonal(0)
            group(U_C_IN, 5, (6, 7))
            pe.wait_ge(S["kt"], 1)
            pe.wait_ge(S["qt"], 1)
            cross(0)
            cross(1)
            diagonal(1)
            pe.wait_ge(S["far_ops"], 1)
            for h in range(GH):
                last = mm(bank[0][:, h * P:(h + 1) * P], kbar[:, h * P:(h + 1) * P], qbar[:, h * P:(h + 1) * P],
                          start=True, stop=True)
            last.then_inc(S["far_psum"], 1)
            pe.wait_ge(S["gla_vr"], 8)
            for t in range(NT):
                pe.wait_ge(S["att"], t + 1)
                if t:
                    pe.wait_ge(S["far_sb"], 1)
                for h in range(GH):
                    o = bank[GLA_BANKS[2 * t + h // 2]][:, h % 2 * 256:(h % 2 + 1) * 256]
                    last = mm(o, att[:, t, h * P:(h + 1) * P], gv[:, t, h * 256:(h + 1) * 256],
                              start=True, stop=(t == 0))
                    if t == 1:
                        last = mm(o, far[:, h * P:(h + 1) * P], gv[:, 0, h * 256:(h + 1) * 256],
                                  start=False, stop=True)
                    if h % 2:
                        last.then_inc(S["gla_o"], 1)
            transposes(hn, lambda i: pe.wait_ge(S["mixed"], GH * (i % 2 + 1)))
            group(U_C_OUT, 0, (4, 5), turn=4)
            group(U_C_OUT, 1, (6, 7))

            transposes(x, lambda i: pe.wait_ge(S["x_ready"], 8 + i + 1))
            small_products(5, sw_router, bank[4][0:16, 0:SEQ]).then_inc(S["logitsT_psum"], 1)
            pe.wait_ge(S["logitsT"], 1)
            for t in range(NT):
                last = mm(bank[4][:, SEQ + t * 8:SEQ + t * 8 + 8], hact[0:16, 0, t * P:(t + 1) * P],
                          cst[0:16, C_FOLD:C_FOLD + NE], start=True, stop=True)
            last.then_inc(S["logits"], 1)
            pe.wait_ge(S["picked"], 1)
            mm(bank[1][:, 0:8], tri, picked[:, 0, :], start=True, stop=True)
            mm(bank[1][:, 8:16], ones, picked[:, 0, :], start=True, stop=False)
            mm(bank[1][:, 8:16], tri, picked[:, 1, :], start=False, stop=True)
            mm(bank[1][:, 16:24], ones, picked[:, 0, :], start=True, stop=False)
            mm(bank[1][:, 16:24], ones, picked[:, 1, :], start=False, stop=True).then_inc(S["rank"], 1)

            def gather_rows(e):
                pe.wait_ge(S["disp"], e + 2)
                for half in range(2):
                    c = slice(half * BLK, (half + 1) * BLK)
                    for t in range(NT):
                        mm(bank[6 + half][:, :], disp[:, t, :], hn_hi[:, t, c], start=(t == 0), stop=False)
                        last = mm(bank[6 + half][:, :], disp[:, t, :], hn_lo[:, t, c], start=False, stop=(t == NT - 1))
                    last.then_inc(S["rows_psum"], 1)

            def gather(e, half):
                pe.wait_ge(S["rows"], (e + 1) * 2 + (half + 1))
                if half or not isinstance(e, int) or e >= 0:
                    pe.wait_ge(S["xg_tmp"], (e + 1) * 2 + half)
                for j in range(4):
                    c = slice((half * 4 + j) * P, (half * 4 + j + 1) * P)
                    last = nc.tensor.transpose(bank[3][:, j * P:(j + 1) * P], hn[:, 0, c], ident)
                last.then_inc(S["xg_psum"], 1)

            def scatter(e, quarters, banks=SCATTER_BANKS):
                for i in quarters:
                    t, half = i // 2, i % 2
                    if i < 2:
                        pe.wait_ge(S["ysb"], e * 2 + (half + 1))
                    elif banks[i] == banks[i - 2]:
                        pe.wait_ge(S["x_ready"], e * 4 + (X_MOE + i - 1))
                    mm(bank[banks[i]][:, :], combT[:, t, :], y_hi[:, half * BLK:(half + 1) * BLK],
                       start=True, stop=False)
                    mm(bank[banks[i]][:, :], combT[:, t, :], y_lo[:, half * BLK:(half + 1) * BLK],
                       start=False, stop=True).then_inc(S["scat"], 1)

            def expert(e, base, par, fresh=False, drain=False, second=False):
                def split_unit(pos):
                    pe.wait_ge(S["w_lo"], e * EXP_UNITS + (U_MOE + pos + 1))
                    sl = (base + pos) % SPLIT
                    return lambda b: (whi[:, sl, b, :], wlo[:, sl, b, :])

                def m_gate_up(c, half):
                    w = split_unit(pos_g(c, half, fresh))
                    tokens = slice(par * P, (par + 1) * P)
                    for k in range(4 * half, 4 * half + 4):
                        last = mm3(bank[(par + c) % 2][:, :], hT_hi[:, k, tokens], hT_lo[:, k, tokens], *w(k % 4),
                                   k == 0, k == NK - 1)
                    last.then_inc(S["units_used"], 1)

                def m_hidden_T(c):
                    pe.wait_ge(S["m_hact"], e * NCH + (c + 1))
                    if c or not fresh:
                        pe.wait_ge(S["m_h2T"], e * NCH + c)
                    for j in range(2):
                        last = nc.tensor.transpose(bank[2][:, j * P:(j + 1) * P],
                                                   hact[:, (par + c) % 2, j * P:(j + 1) * P], ident)
                    last.then_inc(S["m_h2T_psum"], 1)

                def m_down(c):
                    w = split_unit(pos_d(c, drain))
                    pe.wait_ge(S["m_h2T"], e * NCH + (c + 1))
                    if c == 0 and not fresh:
                        pe.wait_ge(S["ysb"], e * 2)
                    first, final = c in (0,), c % NCH == NCH - 1
                    for j in range(2):
                        for half in range(2):
                            last = mm3(bank[4 + half][:, :], h2_hi[:, (par + c) % 2, j * P:(j + 1) * P],
                                       h2_lo[:, (par + c) % 2, j * P:(j + 1) * P], *w(2 * j + half),
                                       first and j == 0, final and j == 1)
                    last.then_inc(S["units_used"], 1)

                if second:
                    gather_rows(e - 1)
                    gather(e - 1, 0)
                    gather(e - 1, 1)
                pe.wait_ge(S["xg"], (e + 1) * 2)
                for c in range(NCH):
                    if c >= 2 or not fresh:
                        pe.wait_ge(S["m_hact"], e * NCH + (c - 1))
                    m_gate_up(c, 0)
                    m_gate_up(c, 1)
                    if c or not fresh:
                        m_hidden_T(c - 1)
                    if not fresh and c in (SCATTER, SCATTER + 1):
                        scatter(e - 1, (0, 1) if c == SCATTER else (2, 3))
                    if c == TURN:
                        pe.wait_ge(S["x_ready"], e * 4 + X_MOE)
                        pe.wait_ge(S["cur"], e * 2 + 2)
                        for t in range(NT):
                            nc.tensor.transpose(bank[6][:, t * P:(t + 1) * P], disp[:, t, :].bitcast(F32), ident)
                        for t in range(NT):
                            last = mm(bank[6][:, 2 * P:2 * P + 1], disp[:, t, :].bitcast(F32), cur[:, 1, t:t + 1],
                                      start=(t == 0), stop=(t == NT - 1))
                        last.then_inc(S["combT_psum"], 1)
                    if not drain and c == GATHER:
                        gather_rows(e)
                    if not drain and c in (GATHER + 1, GATHER + 2):
                        gather(e, c - GATHER - 1)
                    if c >= 2 or not fresh:
                        m_down(c - 2)
                if drain:
                    m_hidden_T(NCH - 1)
                    m_down(NCH - 2)
                    m_down(NCH - 1)
                    pe.wait_ge(S["combT"], e + 1)
                    scatter(e, range(4), DRAIN_BANKS)

            pe.wait_ge(S["hn_lo"], 2)
            gather_rows(-1)
            gather(-1, 0)
            gather(-1, 1)
            expert(0, U_MOE, 0, fresh=True)
            with pe.Fori(1, NE - 1, 2) as e:
                expert(e, U_MOE + EXP_UNITS, 1)
                expert(e + 1, U_MOE + 2 * EXP_UNITS, 0)
            expert(NE - 1, U_MOE + (NE - 1) * EXP_UNITS, 1, drain=True)
            n_over = pe.value_load(ovi[0:1, 0:1], min_val=0, max_val=OVER_ROUNDS)
            with pe.Fori(NE, NE + OVER_ROUNDS) as e:
                with pe.If(n_over > e - NE):
                    expert(e, U_END, 0, fresh=True, drain=True, second=True)

        @block.scalar
        def _(act):
            A = nc.scalar.activation

            def norm(n):
                for t in range(NT):
                    if n == 0:
                        act.wait_ge(S["x_in"], 16)
                    else:
                        act.wait_ge(S["x_ready"], 4 * n - (2 if n == 2 and t == 0 else 0))
                    A(hn[:, t, :], x[:, t, :], ACT.Square, accum_out=ss[:, t:t + 1]).then_inc(S["ss"], 1)

            def split(u):
                act.wait_ge(s_loaded[u % RAW], 16 * (u // RAW + 1))
                if u >= SPLIT:
                    act.wait_ge(S["units_used"], u - SPLIT + 1)
                nc.scalar.copy(whi[:, u % SPLIT, :, :], raw[:, u % RAW, :, :]).then_inc(S["w_hi"], 1)

            def turned(g, gained=True, between=None):
                for i in range(4):
                    half, t = i // 2, i % 2
                    if i == 2 and between is not None:
                        between()
                    if gained:
                        act.wait_ge(S["tmp"], TMP[g] + i + 1)
                        src = esc[:, i % 2, :]
                    else:
                        act.wait_ge(S["hT_psum"], 4 * g + i + 1)
                        src = bank[i][:, :]
                    nc.scalar.copy(hT_hi[:, half * 4:half * 4 + 4, t * P:(t + 1) * P],
                                   src.rearrange("p (k n) -> p k n", k=4)).then_inc(S["hT_hi"], 1)

            norm(0)
            turned(0, between=lambda: split(0))
            for u in range(1, 4):
                split(u)
            act.wait_ge(S["const_in"], CONST_DMAS * 16)
            for parts, src in small_weights:
                nc.scalar.copy(parts[:, :, 0, :], src).then_inc(S["sw_hi"], 1)
            act.wait_ge(S["rstd"], 1)
            for cg in range(A_IN_CG):
                split(2 * cg + 4)
                w = FRONT_WIDTH.get(cg, BLK)
                act.wait_ge(S["units_used"], 2 * (cg + 1))
                for t in range(NT):
                    A(proj[cg][:, t, 0:w], bank[4 + 2 * (cg % 2) + t][:, 0:w], ACT.Copy, scale=rstd[:, t:t + 1])\
                      .then_inc(S["proj"], 1)
                if cg < A_IN_CG - 1:
                    split(2 * cg + 5)
                if cg == 2:
                    act.wait_ge(S["hid_in"], 1)
                    A(gel[0:HD, 1, 0:60], gel[0:HD, 2, 0:60], ACT.Tanh, scale=0.7978845608028654).then_inc(S["tanh"], 1)
                    act.wait_ge(S["gate_z"], 1)
                    A(gat, gat, ACT.Exp, scale=-1.0).then_inc(S["gate_e"], 1)
                    act.wait_ge(S["fox_z"], 1)
                    A(fz[:, 2, :], fz[:, 1, :], ACT.Exp, scale=-1.0).then_inc(S["act_chain"], 1)
                    act.wait_ge(S["act_chain"], 1)
                    A(fz[:, 3, :], fz[:, 2, :], ACT.Ln, bias=1.0).then_inc(S["fox_l"], 1)
            for i in range(4):
                t, half = i // 2, i % 2
                act.wait_ge(S["headT_psum"], 3 + i)
                nc.scalar.copy(qT[0:HD, half * 4:half * 4 + 4, t * P:(t + 1) * P],
                               bank[i][0:HD, :].rearrange("p (h n) -> p h n", h=4)).then_inc(S["headT"], 1)
            act.wait_ge(S["cmp_d"], 1)
            A(sc, sc, ACT.Exp, scale=HD ** -0.5).then_inc(S["cmp_e"], 1)
            for i in range(8):
                w, t, half = i // 4, i // 2 % 2, i % 2
                act.wait_ge(S["foxT_psum"], i + 1)
                dst = (fqT, fkT)[w]
                nc.scalar.copy(dst[0:66, half * 4:half * 4 + 4, t * P:(t + 1) * P],
                               bank[i % 4][0:66, :].rearrange("p (h n) -> p h n", h=4)).then_inc(S["foxT"], 1)
            for u in range(AU):
                br, t, h0, n = att_units[u]
                kw = (t + 1) * P
                act.wait_ge(S["rowmax"], u + 1)
                if u >= 2:
                    act.wait_ge(S["probsT_psum"], u - 1)
                for j in range(n):
                    last = A(pbuf[:, u % 2, j * kw:(j + 1) * kw], bank[SCORE_BANKS[u % 3]][:, j * kw:(j + 1) * kw], ACT.Exp,
                             scale=HD ** -0.5, bias=negm[:, seq_of(u), h0 + j:h0 + j + 1],
                             accum_out=sums[:, seq_of(u), h0 + j:h0 + j + 1])
                last.then_inc(S["probs"], 1)
            turned(1, False)
            for u in range(U_A_OUT + 3, U_FFN + 2):
                split(u)
            turned(2)
            norm(1)
            split(U_FFN + 2)
            act.wait_ge(S["rstd"], 2)
            n_steps = len(steps)
            for i, (c, t) in enumerate(steps):
                freed = U_FFN + dense_g(c, 0) + 1
                if t:
                    split(freed + 2)
                    act.wait_ge(S["units_used"], freed + 1)
                else:
                    act.wait_ge(S["gu"], c + 1)
                A(sg[:, i % 2, :], bank[i % 2][:, 0:CH], ACT.Silu, scale=rstd[:, t:t + 1]).then_inc(S["silu"], 1)
                if t:
                    split(freed + 3)
                if i >= 1:
                    act.wait_ge(S["h2T_psum"], i)
                    nc.scalar.copy(h2_hi[:, (i - 1) % 2, :], bank[2][:, 0:CH]).then_inc(S["h2_hi"], 1)
                if t and c:
                    split(freed + 4)
            act.wait_ge(S["h2T_psum"], n_steps)
            nc.scalar.copy(h2_hi[:, (n_steps - 1) % 2, :], bank[2][:, 0:CH]).then_inc(S["h2_hi"], 1)
            turned(3)
            norm(2)
            split(U_C_IN + 2)
            act.wait_ge(S["roots_psum"], 1)
            nc.scalar.copy(roots, bank[7][:, 0:SEQ]).then_inc(S["roots"], 1)
            split(U_C_IN + 3)
            split(U_C_IN + 4)
            act.wait_ge(S["absz"], 1)
            A(ge, ge, ACT.Exp, scale=-1.0).then_inc(S["act_chain"], 1)
            act.wait_ge(S["act_chain"], 2)
            A(ge, ge, ACT.Ln, bias=1.0).then_inc(S["soft"], 1)
            split(U_C_IN + 5)
            split(U_C_IN + 6)

            def vr(cg):
                act.wait_ge(S["units_used"], U_C_IN + 2 * (cg + 1))
                half = cg % 2
                for t in range(NT):
                    dst = (gv if cg < 4 else gr)[:, t, half * BLK:(half + 1) * BLK]
                    b = bank[(0, 2, 4, 6)[cg - 2] + t]
                    if cg == 4 and t == 0:
                        act.wait_ge(S["cross"], NT)
                    A(dst, b[:, :], ACT.Copy if cg < 4 else ACT.Silu, scale=rstd[:, t:t + 1]).then_inc(S["gla_vr"], 1)

            split(U_C_IN + 7)
            split(U_C_IN + 8)
            vr(2)
            def diagonals(first, last):
                for d in range(first, last):
                    act.wait_ge(S["diag_arg"], d + 1)
                    e_ = esc[:, d % 2, 0:(GB - d % GB) * 64]
                    A(e_, e_, ACT.Exp).then_inc(S["diag_exp"], 1)
                    if d in DIAG_SPLITS:
                        split(U_C_IN + DIAG_SPLITS[d])

            diagonals(0, GB)
            vr(3)
            for i in range(2):
                act.wait_ge(S["q_arg"], i + 1)
                qv = q_view(i)
                A(qv, qv, ACT.Exp).then_inc(S["q_exp"], 1)
            for i in range(NED):
                act.wait_ge(S["k_arg"], i + 1)
                kv = k_view(i)
                A(kv, kv, ACT.Exp).then_inc(S["k_exp"], 1)
                if i in CROSS_SPLITS:
                    split(U_C_IN + CROSS_SPLITS[i])
            diagonals(GB, GB + FAR_AT)
            act.wait_ge(S["far_arg"], 1)
            A(kbar, kbar, ACT.Exp).then_inc(S["far_exp"], 1)
            A(qbar, gb[:, 1, :], ACT.Exp).then_inc(S["far_exp"], 1)
            diagonals(GB + FAR_AT, 2 * GB)
            vr(4)
            vr(5)
            act.wait_ge(S["far_psum"], 1)
            nc.scalar.copy(far, bank[0][:, :]).then_inc(S["far_sb"], 1)
            act.wait_ge(S["prod"], NT * GB)
            for i in range(NT * GH):
                act.wait_ge(S["gla_o"], i // 2 + 1)
                if i >= 2:
                    act.wait_ge(S["gla_ss"], i - 1)
                b = bank[GLA_BANKS[i // 2]]
                A(esc[:, i % 2, 0:256], b[:, i % 2 * 256:(i % 2 + 1) * 256], ACT.Square,
                  accum_out=oss[:, i:i + 1]).then_inc(S["gla_ss"], 1)
            turned(4, False)
            for u in range(U_C_OUT + 3, U_MOE + 2):
                split(u)
            turned(5)
            norm(3)
            act.wait_ge(S["rstd"], 4)
            for t in range(NT):
                A(hn_hi[:, t, :], x[:, t, :], ACT.Copy, scale=rstd[:, t:t + 1]).then_inc(S["hn_hi"], 1)
            split(U_MOE + 2)
            act.wait_ge(S["gap"], 1)
            A(ee, ee, ACT.Exp).then_inc(S["gap_exp"], 1)

            def gathered_rows(e):
                for half in range(2):
                    act.wait_ge(S["rows_psum"], (e + 1) * 2 + (half + 1))
                    nc.scalar.copy(hn[:, 0, half * BLK:(half + 1) * BLK], bank[6 + half][:, :]).then_inc(S["rows"], 1)

            def gathered(e, par, half):
                act.wait_ge(S["xg_tmp"], (e + 1) * 2 + (half + 1))
                nc.scalar.copy(hT_hi[:, half * 4:half * 4 + 4, par * P:(par + 1) * P],
                               esc[:, half, :].rearrange("p (k n) -> p k n", k=4)).then_inc(S["xg_hi"], 1)

            def final_sums(e, used):
                act.wait_ge(S["units_used"], used)
                for half in range(2):
                    A(y_hi[:, half * BLK:(half + 1) * BLK], bank[4 + half][:, :], ACT.Copy, scale=gslot[:, 0:1])\
                      .then_inc(S["y_hi"], 1)

            def expert(e, base, par, loads, fresh=False, drain=False, second=False):
                def split_unit(pos):
                    if pos >= EXP_UNITS and drain:
                        return
                    u = base + pos
                    act.wait_ge(s_loaded[u % RAW], loads(pos))
                    act.wait_ge(S["units_used"],
                                e * EXP_UNITS + (U_MOE + (max(pos - SPLIT + 1, 0) if second else pos - SPLIT + 1)))
                    nc.scalar.copy(whi[:, u % SPLIT, :, :], raw[:, u % RAW, :, :]).then_inc(S["w_hi"], 1)

                def hidden_turned(c):
                    act.wait_ge(S["m_h2T_psum"], e * NCH + (c + 1))
                    nc.scalar.copy(h2_hi[:, (par + c) % 2, :], bank[2][:, 0:CH]).then_inc(S["m_h2_hi"], 1)

                if second:
                    gathered_rows(e - 1)
                    gathered(e - 1, par, 0)
                    gathered(e - 1, par, 1)
                    for pos in range(SPLIT):
                        split_unit(pos)
                for c in range(NCH):
                    if c == 2 and not fresh:
                        final_sums(e - 1, e * EXP_UNITS + (U_MOE + pos_d(-1, drain) + 1))
                    split_unit(pos_g(c, 0, fresh) + SPLIT)
                    act.wait_ge(S["units_used"], e * EXP_UNITS + (U_MOE + pos_g(c, 1, fresh) + 1))
                    A(sg[:, (par + c) % 2, :], bank[(par + c) % 2][:, 0:CH], ACT.Silu).then_inc(S["m_silu"], 1)
                    split_unit(pos_g(c, 1, fresh) + SPLIT)
                    if c or not fresh:
                        hidden_turned(c - 1)
                    if c == TURN:
                        act.wait_ge(S["combT_psum"], e + 1)
                        nc.scalar.copy(gslot[:, :], bank[6][:, 2 * P:2 * P + 1])
                        nc.scalar.copy(combT[:, :, :], bank[6][:, 0:2 * P].rearrange("p (t n) -> p t n", t=NT))\
                          .then_inc(S["combT"], 1)
                    if not drain and c in (GATHER + 2, GATHER + 3):
                        gathered(e, 1 - par, c - GATHER - 2)
                    if c >= 2 or not fresh:
                        split_unit(pos_d(c - 2, drain) + SPLIT)
                    if not drain and c == GATHER:
                        gathered_rows(e)
                if drain:
                    hidden_turned(NCH - 1)
                    final_sums(e, (e + 1) * EXP_UNITS + U_MOE)

            gathered_rows(-1)
            gathered(-1, 0, 0)
            gathered(-1, 0, 1)
            expert(0, U_MOE, 0, lambda pos: loads_main(0, U_MOE, pos), fresh=True)
            with act.Fori(1, NE - 1, 2) as e:
                expert(e, U_MOE + EXP_UNITS, 1, lambda pos: loads_main(e - 1, U_MOE + EXP_UNITS, pos))
                expert(e + 1, U_MOE + 2 * EXP_UNITS, 0, lambda pos: loads_main(e - 1, U_MOE + 2 * EXP_UNITS, pos))
            last = U_MOE + (NE - 1) * EXP_UNITS
            expert(NE - 1, last, 1, lambda pos: loads_main(0, last, pos), drain=True)
            act.wait_ge(S["route"], 1)
            n_over = act.value_load(ovi[0:1, 0:1], min_val=0, max_val=OVER_ROUNDS)
            with act.Fori(NE, NE + OVER_ROUNDS) as e:
                with act.If(n_over > e - NE):
                    expert(e, U_END, 0, lambda pos: loads_over(e, pos), fresh=True, drain=True, second=True)

        @block.vector
        def _(dve):
            V = nc.vector
            chain = [0]

            def link(ins):
                chain[0] += 1
                ins.then_inc(S["dve_chain"], 1)
                dve.wait_ge(S["dve_chain"], chain[0])

            def bc(ap, axis, n):
                a = ap.unsqueeze(axis)
                shape = list(a.shape)
                shape[axis] = n
                return a.to_broadcast(shape)

            def split(u):
                dve.wait_ge(S["w_hi"], u + 1)
                V.tensor_tensor(wlo[:, u % SPLIT, :, :], raw[:, u % RAW, :, :], whi[:, u % SPLIT, :, :].bitcast(F32),
                                ALU.subtract).then_inc(S["w_lo"], 1)

            def turned(g, gain=None, between=None):
                def lower(i):
                    half, t = i // 2, i % 2
                    at = (slice(None), slice(half * 4, half * 4 + 4), slice(t * P, (t + 1) * P))
                    dve.wait_ge(S["hT_hi"], 4 * g + i + 1)
                    src = bank[i][:, :] if gain is None else esc[:, i % 2, :]
                    V.tensor_tensor(hT_lo[at], src.rearrange("p (k n) -> p k n", k=4), hT_hi[at].bitcast(F32),
                                    ALU.subtract).then_inc(S["hT"], 1)

                for i in range(4):
                    half = i // 2
                    if i == 2 and between is not None:
                        lower(0)
                        lower(1)
                        between()
                    dve.wait_ge(S["hT_psum"], 4 * g + i + 1)
                    if gain is not None:
                        if i >= 2 and between is None:
                            lower(i - 2)
                        gc = R_NORM + NK * gain + 4 * half
                        if i >= 2:
                            dve.wait_ge(S["hT"], 4 * g + i - 1)
                        V.tensor_tensor(esc[:, i % 2, :].rearrange("p (k n) -> p k n", k=4),
                                        bank[i][:, :].rearrange("p (k n) -> p k n", k=4),
                                        bc(sml[:, gc:gc + 4], 2, P), ALU.mult).then_inc(S["tmp"], 1)
                    else:
                        lower(i)
                if gain is not None:
                    lower(2)
                    lower(3)

            def residual(u0):
                for cg in range(2):
                    for j in ((3, 4), (5,))[cg]:
                        split(u0 + j)
                    dve.wait_ge(S["units_used"], u0 + 2 * (cg + 1))
                    for t in range(NT):
                        xs = x[:, t, cg * BLK:(cg + 1) * BLK]
                        V.tensor_tensor(xs, xs, bank[4 + 2 * cg + t][:, :], ALU.add).then_inc(S["x_ready"], 1)

            def head_squares(src, nh, which, order):
                n = NT * nh
                dve.wait_ge(S["head_done"], order - 1)
                s3 = sq[:, 0:n * HD].rearrange("p (r d) -> p r d", d=HD).rearrange("p (t h) d -> p t h d", t=NT)
                link(V.tensor_tensor(s3, src, src, ALU.mult))
                V.tensor_reduce(hss[:, which, 0:n], sq[:, 0:n * HD].rearrange("p (r d) -> p r d", d=HD), AX.X, ALU.add)\
                 .then_inc(S["head_ss"], 1)

            def head_scale(src, nh, which, gain, dst, order):
                n = NT * nh
                s3 = sq[:, 0:n * HD].rearrange("p (r d) -> p r d", d=HD).rearrange("p (t h) d -> p t h d", t=NT)
                dve.wait_ge(S["head_rstd"], order)
                r3 = hrs[:, which, 0:n].rearrange("p (t h) -> p t h", t=NT)
                link(V.tensor_tensor(s3, src, bc(r3, 3, HD), ALU.mult))
                g1 = bc(bc(sml[:, gain:gain + HD], 1, nh), 1, NT)
                return V.tensor_tensor(dst, s3, g1, ALU.mult)

            def rope(v, tab, nh, ra, rb):
                link(V.tensor_tensor(ra, v[:, :, :, 0:16], bc(tab[:, :, 0:16], 2, nh), ALU.mult))
                V.tensor_tensor(rb[:, :, :, 0:8], v[:, :, :, 8:16], bc(tab[:, :, 16:24], 2, nh), ALU.mult)
                link(V.tensor_tensor(rb[:, :, :, 8:16], v[:, :, :, 0:8], bc(tab[:, :, 24:32], 2, nh), ALU.mult))
                return V.tensor_tensor(v[:, :, :, 0:16], ra, rb, ALU.add)

            def four(buf, nh):
                return buf[:, 0:NT * nh * 16].rearrange("p (t h d) -> p t h d", t=NT, h=nh)

            dve.wait_ge(S["const_in"], CONST_DMAS * 16)
            turned(0, 0, lambda: split(0))
            for u in range(1, 6):
                split(u)
            dve.wait_ge(S["sw_hi"], 2)
            for parts, src in small_weights:
                V.tensor_tensor(parts[:, :, 1, :], src, parts[:, :, 0, :].bitcast(F32), ALU.subtract)\
                 .then_inc(S["sw_lo"], 1)
            for v in range(2):
                dve.wait_ge(S["kc_psum"], v + 1)
                src = bank[v][0:HD, :].rearrange("p (g n) -> p g n", g=NG)
                V.tensor_copy(kc2[0:HD, v, :, :], src).then_inc(S["kc"], 1)
                V.tensor_copy(kc2[HD:P, v, :, 0:SEQ - 1], src[:, :, 1:SEQ]).then_inc(S["kc"], 1)
            dve.wait_ge(S["kc"], 4)
            for v in range(2):
                for g in range(NG):
                    first = kc2[:, v, g, :].rearrange("p (m j w) -> p j m w", j=8, w=2)[:, :, :, 0]
                    pe_ = sml[:, R_PE + 16 * v:R_PE + 16 * (v + 1)]
                    V.tensor_tensor(blkT[:, v, 0:8, g, :], first[:, :, 0:NCMP], bc(pe_[:, 0:8], 2, NCMP), ALU.add)
                    V.tensor_tensor(blkT[:, v, 8:16, g, :], first[:, :, 1:NCMP + 1], bc(pe_[:, 8:16], 2, NCMP),
                                    ALU.add).then_inc(S["blk"], 1)
            tab = cst[:, C_ROPE:C_ROPE + 64].rearrange("p (t n) -> p t n", t=NT)
            keys = proj[0][:, :, 256:512].rearrange("p t (h d) -> p t h d", h=4)
            head_squares(keys, 4, 0, 1)
            split(6)
            link(head_scale(keys, 4, 0, R_KN, keys, 1))
            split(7)
            rope(keys, tab, 4, four(rA, 4), four(rB, 4)).then_inc(S["head_done"], 1)
            dve.wait_ge(S["proj"], 4)
            V.tensor_tensor(gat.rearrange("p (t n) -> p t n", t=NT), proj[1][:, :, 256:280],
                            bc(sml[:, R_GB:R_GB + 24], 1, NT), ALU.add).then_inc(S["gate_z"], 1)
            link(V.tensor_tensor(fz[:, 0, :].rearrange("p (t n) -> p t n", t=NT), proj[1][:, :, 280:288],
                                 bc(sml[:, R_FB:R_FB + 8], 1, NT), ALU.add))
            link(V.tensor_scalar(fz[:, 1, :], fz[:, 0, :], -1.0, None, ALU.mult))
            V.tensor_tensor(fz[:, 1, :], fz[:, 1, :], fz[:, 0, :], ALU.max).then_inc(S["fox_z"], 1)
            split(8)
            dve.wait_ge(S["hid"], 1)
            xh = gel[0:HD, 0, 0:60]
            uu = gel[0:HD, 2, 0:60]
            link(V.tensor_copy(xh.rearrange("p (v n) -> p v n", v=2),
                               bank[2][0:HD, 0:64].rearrange("p (v n) -> p v n", v=2)[:, :, 0:30]))
            link(V.tensor_tensor(uu, xh, xh, ALU.mult))
            link(V.tensor_scalar(uu, uu, 0.044715, 1.0, ALU.mult, ALU.add))
            V.tensor_tensor(uu, uu, xh, ALU.mult).then_inc(S["hid_in"], 1)
            for t in range(NT):
                dve.wait_ge(S["headT_psum"], t + 1)
                V.tensor_copy(keyT[0:HD, :, t * P:(t + 1) * P], bank[t][0:HD, :].rearrange("p (h n) -> p h n", h=4))\
                 .then_inc(S["headT"], 1)
            split(9)
            dve.wait_ge(S["tanh"], 1)
            link(V.tensor_scalar(gel[0:HD, 1, 0:60], gel[0:HD, 1, 0:60], 0.5, 0.5, ALU.mult, ALU.add))
            V.tensor_tensor(gel[0:HD, 3, 0:60], gel[0:HD, 1, 0:60], xh, ALU.mult).then_inc(S["gelu"], 1)
            dve.wait_ge(S["proj"], 6)
            qa = proj[2][:, :, :].rearrange("p t (h d) -> p t h d", h=NH)
            head_squares(qa, NH, 1, 2)
            split(10)
            link(head_scale(qa, NH, 1, R_QN, qa, 2))
            dve.wait_ge(S["cmp2"], 1)
            V.tensor_copy(vcmp[0:NCMP, :, :], bank[3][0:NCMP, HD:3 * HD].rearrange("p (g d) -> p g d", g=NG))\
             .then_inc(S["cmp2_sb"], 1)
            link(V.tensor_copy(kcm[0:30, 0, :], bank[3][0:30, 0:HD]))
            link(V.tensor_tensor(kcm[0:30, 1, :], kcm[0:30, 0, :], kcm[0:30, 0, :], ALU.mult))
            V.tensor_reduce(hss[0:30, 4, 0:1], kcm[0:30, 1, :], AX.X, ALU.add).then_inc(S["kcmp_ss"], 1)
            rope(qa, tab, NH, four(rA, NH), four(rB, NH)).then_inc(S["head_done"], 1)
            split(11)
            dve.wait_ge(S["kcmp_rstd"], 1)
            link(V.scalar_tensor_tensor(kcm[0:30, 3, :], kcm[0:30, 0, :], hrs[0:30, 4, 0:1], sml[0:30, R_KN:R_KN + HD],
                                        ALU.mult, ALU.mult))
            ct = cst[0:30, C_CROPE:C_CROPE + 32]
            kv = kcm[0:30, 3, :]
            dve.wait_ge(S["head_done"], 2)
            link(V.tensor_tensor(rA[0:30, 0:16], kv[:, 0:16], ct[:, 0:16], ALU.mult))
            V.tensor_tensor(rB[0:30, 0:8], kv[:, 8:16], ct[:, 16:24], ALU.mult)
            link(V.tensor_tensor(rB[0:30, 8:16], kv[:, 0:8], ct[:, 24:32], ALU.mult))
            V.tensor_tensor(kv[:, 0:16], rA[0:30, 0:16], rB[0:30, 0:16], ALU.add).then_inc(S["kcmp"], 1)

            def fox(w):
                return proj[3 + w][:, :, :].rearrange("p t (h d) -> p t h d", h=NH)

            def fox_scale(w):
                head_scale(fox(w), NH, 2 + w, (R_FQ, R_FK)[w], faug[:, w, :, :, 0:HD], 3 + w).then_inc(S["head_done"], 1)
                V.memset(faug[:, w, :, :, HD + 1 - w:HD + 2 - w], 1.0)

            dve.wait_ge(S["proj"], 8)
            head_squares(fox(0), NH, 2, 3)
            split(12)
            dve.wait_ge(S["vrep"], 1)
            V.tensor_tensor(vbd.rearrange("p (h d) -> p h d", h=NH), bc(bank[2][:, 0:HD], 1, NH),
                            bc(cst[:, C_HMASK:C_HMASK + 8], 2, HD), ALU.mult).then_inc(S["vbd"], 1)
            dve.wait_ge(S["kcmpT_psum"], 1)
            V.tensor_copy(kcmpT[0:HD, 0:30], bank[3][0:HD, 256:286]).then_inc(S["kcmpT"], 1)
            fox_scale(0)
            dve.wait_ge(S["proj"], 10)
            head_squares(fox(1), NH, 3, 4)
            dve.wait_ge(S["fox_l"], 1)
            V.scalar_tensor_tensor(fz[:, 4, :], fz[:, 0, :], 0.0, fz[:, 3, :], ALU.min, ALU.subtract)\
             .then_inc(S["fox_lf"], 1)
            dve.wait_ge(S["gate_e"], 1)
            link(V.tensor_scalar(gat, gat, 1.0, None, ALU.add))
            link(V.reciprocal(gat, gat))
            split(13)
            fox_scale(1)
            split(14)
            dve.wait_ge(S["cum"], 1)
            cum = bank[0][:, 0:16].rearrange("p (t h) -> p t h", t=NT).unsqueeze(3)
            V.tensor_scalar(faug[:, 0, :, :, HD:HD + 1], cum, HD ** 0.5, None, ALU.mult)
            V.tensor_scalar(faug[:, 1, :, :, HD + 1:HD + 2], cum, -HD ** 0.5, None, ALU.mult).then_inc(S["aug"], 1)
            dve.wait_ge(S["cmp_s"], 1)
            s16 = sc.rearrange("p t (h n) -> p t h n", h=NH)
            s15 = s16[:, :, :, 0:NCMP]
            bias = cst[:, C_CBIAS:C_CBIAS + 32].rearrange("p (t n) -> p t n", t=NT)[:, :, 0:NCMP]
            cm01 = cst[:, C_CMASK:C_CMASK + 32].rearrange("p (t n) -> p t n", t=NT)
            V.memset(s16[:, :, :, NCMP:16], 0.0)
            link(V.tensor_tensor(s15, bank[6][:, 0:2 * P].rearrange("p (t h n) -> p t h n", t=NT, h=NH)[:, :, :, 0:NCMP],
                                 bc(bias, 2, NH), ALU.add))
            m3 = mc.rearrange("p (t h) -> p t h", t=NT)
            link(V.tensor_reduce(m3, s15, AX.X, ALU.max))
            V.tensor_tensor(s15, s15, bc(m3, 3, NCMP), ALU.subtract).then_inc(S["cmp_d"], 1)
            dve.wait_ge(S["cmp_e"], 1)
            link(V.tensor_reduce(sumc.rearrange("p (t h) -> p t h", t=NT), s15, AX.X, ALU.add))
            V.tensor_tensor(s16, s16, bc(cm01, 2, NH), ALU.mult).then_inc(S["cmp_p"], 1)
            link(V.reciprocal(sumc, sumc))
            g4 = gat.rearrange("p (t h w) -> p t h w", t=NT, h=NH)
            V.tensor_tensor(facc.rearrange("p (t h) -> p t h", t=NT), sumc.rearrange("p (t h) -> p t h", t=NT),
                            g4[:, :, :, 0], ALU.mult).then_inc(S["dve_chain"], 1)
            chain[0] += 1
            dve.wait_ge(S["cmp_pT_psum"], 1)
            V.tensor_copy(pcT, bank[7][:, 0:2 * P].rearrange("p (t n) -> p t n", t=NT)).then_inc(S["cmp_pT"], 1)
            dve.wait_ge(S["dve_chain"], chain[0])

            def heads(ap):
                return ap.rearrange("p (h d) -> p h d", h=NH)

            for t in range(NT):
                dve.wait_ge(S["cmp_o"], t + 1)
                V.tensor_tensor(heads(oacc[:, t, 0:512]), heads(bank[4 + t][:, :]), bc(facc[:, t * 8:t * 8 + 8], 2, HD),
                                ALU.mult).then_inc(S["o_done"], 1)

            def rowmax(u):
                br, t, h0, n = att_units[u]
                dve.wait_ge(S["scores"], u + 1)
                m = negm[:, seq_of(u), h0:h0 + n]
                link(V.tensor_reduce(m, bank[SCORE_BANKS[u % 3]][:, :].rearrange("p (h n) -> p h n", h=n), AX.X, ALU.max))
                V.tensor_scalar(m, m, -HD ** -0.5, None, ALU.mult).then_inc(S["rowmax"], 1)

            def take(q):
                br, t = q // NT, q % NT
                dve.wait_ge(S["pv"], ends_seq[q] + 1)
                o = heads(bank[4 + q % 2][:, :])
                link(V.reciprocal(fac[:, q, :], sums[:, q, :]))
                if br == 2:
                    V.tensor_tensor(heads(oacc[:, t, 512:1024]), o, bc(fac[:, q, :], 2, HD), ALU.mult)\
                     .then_inc(S["o_done"], 1)
                    return
                link(V.tensor_tensor(fac[:, q, :], fac[:, q, :], g4[:, t, :, br + 1], ALU.mult))
                link(V.tensor_tensor(heads(tmpo), o, bc(fac[:, q, :], 2, HD), ALU.mult))
                V.tensor_tensor(oacc[:, t, 0:512], oacc[:, t, 0:512], tmpo, ALU.add).then_inc(S["o_done"], 1)

            rowmax(0)
            rowmax(1)
            for u in range(AU):
                if u + 2 < AU:
                    rowmax(u + 2)
                dve.wait_ge(S["probsT_psum"], u + 1)
                if u >= 2:
                    dve.wait_ge(S["pv"], u - 1)
                V.tensor_copy(ptb[:, u % 2, :], bank[2 + u % 2][:, :]).then_inc(S["probsT"], 1)
                if u - 1 in ends_seq:
                    take(ends_seq.index(u - 1))
            take(2 * 3 - 1)
            turned(1)
            residual(U_A_OUT)
            turned(2, 1)
            split(U_FFN + 2)
            dve.wait_ge(S["rstd"], 2)

            def h2_lower(i):
                dve.wait_ge(S["h2_hi"], i + 1)
                V.tensor_tensor(h2_lo[:, i % 2, :], bank[2][:, 0:CH], h2_hi[:, i % 2, :].bitcast(F32), ALU.subtract)\
                 .then_inc(S["h2T"], 1)

            for i, (c, t) in enumerate(steps):
                freed = U_FFN + dense_g(c, 0) + 1
                if t:
                    split(freed + 2)
                dve.wait_ge(S["silu"], i + 1)
                V.scalar_tensor_tensor(hact[:, i % 2, :], bank[i % 2][:, CH:2 * CH], rstd[:, t:t + 1], sg[:, i % 2, :],
                                       ALU.mult, ALU.mult).then_inc(S["hact"], 1)
                if t:
                    split(freed + 3)
                if i >= 1:
                    h2_lower(i - 1)
                if t and c:
                    split(freed + 4)
            h2_lower(len(steps) - 1)
            for t in range(NT):
                dve.wait_ge(S["first_rows"] if t == 0 else S["units_used"], 1 if t == 0 else U_C_IN)
                for half in range(2):
                    xs = x[:, t, half * BLK:(half + 1) * BLK]
                    V.tensor_tensor(xs, xs, bank[4 + 2 * t + half][:, :], ALU.add).then_inc(S["x_ready"], 1)

            turned(3, 2)
            dve.wait_ge(S["rstd"], 3)
            dve.wait_ge(S["hT"], 16)
            V.tensor_scalar(root_diag[:, 0:P], ident, rstd[:, 0:1], None, ALU.mult)
            V.tensor_scalar(root_diag[:, P:SEQ], ident, rstd[:, 1:2], None, ALU.mult).then_inc(S["root_diag"], 1)
            split(U_C_IN + 2)
            dve.wait_ge(S["a1"], 1)
            dve.wait_ge(S["roots"], 1)
            V.tensor_tensor(a1T[0:32, :], bank[6][0:32, 0:SEQ], roots[0:32, :], ALU.mult).then_inc(S["a1_sb"], 1)
            split(U_C_IN + 3)

            def channels_scaled(dst, b0, factor):
                for h in range(GH):
                    V.scalar_tensor_tensor(dst[:, :, h * P:(h + 1) * P],
                                           bank[b0 + h][:, 0:SEQ].rearrange("p (t n) -> p t n", t=NT), factor,
                                           roots.rearrange("p (t n) -> p t n", t=NT), ALU.mult, ALU.mult)\
                     .then_inc(S["gla_qk"], 1)

            V.memset(rmask, 1.0).then_inc(S["dve_chain"], 1)
            chain[0] += 1
            dve.wait_ge(S["dve_chain"], chain[0])
            link(V.memset(rmask.rearrange("p (s n) -> p s n", n=P)[:, :, 0:1], 0.0))
            dve.wait_ge(S["units_used"], U_C_IN + 2)
            channels_scaled(gq, 0, P ** -0.5)
            dve.wait_ge(S["z"], 1)
            for h in range(GH):
                last = V.tensor_scalar(gz.rearrange("p (t h n) -> p t h n", t=NT, h=GH)[:, :, h, :],
                                       bank[4 + h // 2][:, h % 2 * SEQ:(h % 2 + 1) * SEQ].rearrange("p (t n) -> p t n", t=NT),
                                       sml[:, R_BA + h:R_BA + h + 1], None, ALU.add)
            last.then_inc(S["zb"], 1)
            split(U_C_IN + 4)
            dve.wait_ge(S["zb"], 1)
            link(V.tensor_scalar(ge, gz, -1.0, None, ALU.mult))
            V.tensor_tensor(ge, ge, gz, ALU.max).then_inc(S["absz"], 1)
            dve.wait_ge(S["soft"], 1)
            split(U_C_IN + 5)
            link(V.scalar_tensor_tensor(gz, gz, 0.0, ge, ALU.min, ALU.subtract))
            gbf = gb.rearrange("p t n -> p (t n)")
            link(V.tensor_scalar(gz, gz, 1.0 / 16.0, None, ALU.mult))
            V.tensor_tensor_scan(gbf, rmask, gz, 0.0, ALU.mult, ALU.add).then_inc(S["decay"], 1)
            dve.wait_ge(S["units_used"], U_C_IN + 4)
            channels_scaled(gk, 4, 1.0)
            dve.wait_ge(S["decay"], 1)
            dve.wait_ge(S["kt_zero"], 1)
            dve.wait_ge(S["gla_qk"], 8)
            for j in (6, 7, 8):
                split(U_C_IN + j)

            flat = {n: a_.rearrange("p t n -> p (t n)") for n, a_ in (("b", gb), ("q", gq), ("k", gk))}

            def q_arg(i):
                if i == 0:
                    b4 = flat["b"].rearrange("p (g b r) -> p g b r", b=NGE, r=GE)
                    prev = b4[:, :, 0:NGE - 1, GE - 1:GE].to_broadcast([P, NT * GH, NGE - 1, GE])
                    own = b4[:, :, 1:NGE, :]
                else:
                    b4 = flat["b"].rearrange("p (g b r) -> p g b r", b=GE // GB, r=GB)
                    prev = b4[:, :, 0:GE // GB - 1, GB - 1:GB].to_broadcast([P, NT * GH * NGE, GE // GB - 1, GB])
                    own = b4[:, :, 1:GE // GB, :]
                V.tensor_tensor(q_view(i), own, prev, ALU.subtract).then_inc(S["q_arg"], 1)

            def k_arg(i):
                own = before_edge(flat["b"], i)
                edge = own[:, :, own.shape[2] - 1:own.shape[2]].to_broadcast(list(own.shape))
                V.tensor_tensor(k_view(i), edge, own, ALU.subtract).then_inc(S["k_arg"], 1)

            def k_mul(i):
                dve.wait_ge(S["k_exp"], i + 1)
                last = V.tensor_tensor(k_view(i), k_view(i), before_edge(flat["k"], i), ALU.mult)
                if i == NED - 1:
                    last.then_inc(S["kt"], 1)

            def diag_arg(d):
                t, s_ = d // GB, d % GB
                b3 = gb[:, t, :].rearrange("p (m r) -> p m r", r=GB)
                q3 = gq[:, t, :].rearrange("p (m r) -> p m r", r=GB)
                k3 = gk[:, t, :].rearrange("p (m r) -> p m r", r=GB)
                w = GB - s_
                e3 = esc[:, d % 2, 0:64 * w].rearrange("p (m r) -> p m r", r=w)
                if d >= 2:
                    dve.wait_ge(S["prod"], d - 1)
                V.tensor_tensor(e3, b3[:, :, s_:GB], b3[:, :, s_:s_ + 1].to_broadcast([P, 64, w]), ALU.subtract)\
                 .then_inc(S["diag_arg"], 1)
                p3 = prod[:, s_, :].rearrange("p (m r) -> p m r", r=GB)
                chain[0] += 1
                V.tensor_tensor(p3[:, :, s_:GB], q3[:, :, s_:GB], k3[:, :, s_:s_ + 1].to_broadcast([P, 64, w]), ALU.mult)\
                 .then_inc(S["dve_chain"], 1)
                return chain[0]

            def diag_mul(d, tag):
                s_ = d % GB
                w = GB - s_
                e3 = esc[:, d % 2, 0:64 * w].rearrange("p (m r) -> p m r", r=w)
                p3 = prod[:, s_, :].rearrange("p (m r) -> p m r", r=GB)
                dve.wait_ge(S["diag_exp"], d + 1)
                dve.wait_ge(S["dve_chain"], tag)
                V.tensor_tensor(p3[:, :, s_:GB], p3[:, :, s_:GB], e3, ALU.mult).then_inc(S["prod"], 1)

            def take_att(t):
                def view(a_, width, lo):
                    return a_.rearrange("p (g n) -> p g n", n=width)[:, :, lo:width]

                dve.wait_ge(S["diag"], t + 1)
                link(V.tensor_tensor(view(att[:, t, :], P, 0), view(bank[t][:, :], P, 0), bc(mbd, 1, GH), ALU.mult))
                m4 = mbe.rearrange("p (b r) -> p b r", r=GE)[:, :, GB:GE].unsqueeze(1).to_broadcast([P, GH, NGE, GE - GB])

                def inner(a_):
                    return a_.rearrange("p (h b r) -> p h b r", h=GH, r=GE)[:, :, :, GB:GE]

                V.tensor_tensor(inner(atmp[:, t, :]), inner(bank[3][:, :]), m4, ALU.mult).then_inc(S["dve_chain"], 1)
                chain[0] += 1
                link(V.tensor_tensor(view(att[:, t, :], P, GE), view(att[:, t, :], P, GE), view(bank[2][:, :], P, GE),
                                     ALU.add))
                V.tensor_tensor(view(att[:, t, :], GE, GB), view(att[:, t, :], GE, GB), view(atmp[:, t, :], GE, GB),
                                ALU.add).then_inc(S["att"], 1)

            def diagonals(first, last):
                tag = diag_arg(first)
                for d in range(first, last):
                    nxt = diag_arg(d + 1) if d + 1 < last else None
                    diag_mul(d, tag)
                    if d in DIAG_SPLITS:
                        split(U_C_IN + DIAG_SPLITS[d])
                    tag = nxt

            dve.wait_ge(S["prod_zero"], 1)
            diagonals(0, GB)
            q_arg(0)
            q_arg(1)
            k_arg(0)
            k_arg(1)
            for i in range(NED):
                if i + 2 < NED:
                    k_arg(i + 2)
                if i < 2:
                    dve.wait_ge(S["q_exp"], i + 1)
                    width = (GE, GB)[i]
                    q4 = flat["q"].rearrange("p (g b r) -> p g b r", b=4, r=width)[:, :, 1:4, :]
                    last = V.tensor_tensor(q_view(i), q_view(i), q4, ALU.mult)
                    if i:
                        last.then_inc(S["qt"], 1)
                k_mul(i)
                if i in CROSS_SPLITS:
                    split(U_C_IN + CROSS_SPLITS[i])
            dve.wait_ge(S["diag"], 1)
            diagonals(GB, GB + FAR_AT)
            dve.wait_ge(S["cross"], 1)
            take_att(0)
            V.tensor_tensor(kbar.rearrange("p (h n) -> p h n", h=GH),
                            gb[:, 0, :].rearrange("p (h n) -> p h n", h=GH)[:, :, P - 1:P].to_broadcast([P, GH, P]),
                            gb[:, 0, :].rearrange("p (h n) -> p h n", h=GH), ALU.subtract).then_inc(S["far_arg"], 1)
            diagonals(GB + FAR_AT, 2 * GB)
            dve.wait_ge(S["far_exp"], 2)
            V.tensor_tensor(kbar, kbar, gk[:, 0, :], ALU.mult)
            V.tensor_tensor(qbar, qbar, gq[:, 1, :], ALU.mult).then_inc(S["far_ops"], 1)
            dve.wait_ge(S["cross"], 2)
            take_att(1)
            dve.wait_ge(S["gla_vr"], 8)
            r4 = gr.rearrange("p t (h d) -> p t h d", h=GH)
            link(V.tensor_tensor(r4, r4, bc(bc(sml[:, R_ON:R_ON + 256], 1, GH), 1, NT), ALU.mult))
            for i in range(NT * GH):
                t, h = i // GH, i % GH
                dve.wait_ge(S["gla_rstd"], t + 1)
                dve.wait_ge(S["gla_o"], 3 + h // 2)
                b = bank[GLA_BANKS[i // 2]]
                V.scalar_tensor_tensor(hn[:, t, h * 256:(h + 1) * 256], b[:, i % 2 * 256:(i % 2 + 1) * 256],
                                       ors[:, i:i + 1], gr[:, t, h * 256:(h + 1) * 256], ALU.mult, ALU.mult)\
                 .then_inc(S["mixed"], 1)
            turned(4)
            residual(U_C_OUT)

            turned(5, 3)
            dve.wait_ge(S["rstd"], 4)

            def tokens_lower(t):
                dve.wait_ge(S["hn_hi"], t + 1)
                V.scalar_tensor_tensor(hn_lo[:, t, :], x[:, t, :], rstd[:, t:t + 1], hn_hi[:, t, :].bitcast(F32),
                                       ALU.mult, ALU.subtract).then_inc(S["hn_lo"], 1)

            dve.wait_ge(S["logitsT_psum"], 1)
            V.tensor_copy(hact[0:16, 0, :], bank[4][0:16, 0:SEQ]).then_inc(S["logitsT"], 1)
            tokens_lower(0)
            dve.wait_ge(S["logits"], 1)
            for t in range(NT):
                link(V.tensor_scalar(lg[:, t, :], bank[4][:, SEQ + 8 * t:SEQ + 8 * t + 8], rstd[:, t:t + 1], None,
                                     ALU.mult))
            for t in range(NT):
                link(V.max(mx[:, t, :], lg[:, t, :]))
                link(V.max_index(mxi[:, t, :], mx[:, t, :], lg[:, t, :]))
            link(V.tensor_copy(idf, mxi[:, :, :]))
            V.tensor_tensor(ee, mx[:, :, 1], mx[:, :, 0], ALU.subtract).then_inc(S["gap"], 1)
            for t in range(NT):
                for w in range(2):
                    V.tensor_scalar(oh[:, w, t, :], iota[:, 0:8], idf[:, t, w:w + 1], None, ALU.is_equal)
            link(V.memset(slot[:, :, :], -1.0))
            V.tensor_tensor(picked, oh[:, 0, :, :], oh[:, 1, :, :], ALU.add).then_inc(S["picked"], 1)

            def gates():
                dve.wait_ge(S["gap_exp"], 1)
                link(V.tensor_scalar(w12[:, :, 0], ee, 1.0, None, ALU.add))
                link(V.reciprocal(w12[:, :, 0], w12[:, :, 0]))
                link(V.tensor_tensor(w12[:, :, 1], w12[:, :, 0], ee, ALU.mult))
                link(V.memset(gate[:, :, :], 0.0))
                for t in range(NT):
                    link(V.tensor_scalar(gate[:, t, 0:8], oh[:, 0, t, :], w12[:, t, 0:1], None, ALU.mult))
                    link(V.scalar_tensor_tensor(gate[:, t, 0:8], oh[:, 1, t, :], w12[:, t, 1:2], gate[:, t, 0:8],
                                                ALU.mult, ALU.add))

            tokens_lower(1)
            dve.wait_ge(S["rank"], 1)
            dve.wait_ge(S["picked"], 1)
            link(V.tensor_tensor(slot[:, :, 0:8], bank[1][:, 0:16].rearrange("p (t n) -> p t n", t=NT), picked, ALU.mult))
            V.tensor_scalar(over[:, 0, :], bank[1][:, 16:24], float(CAP), None, ALU.is_gt)
            link(V.tensor_scalar(slot[:, :, 0:8], slot[:, :, 0:8], -1.0, None, ALU.add))

            def overflow():
                R = OVER_ROUNDS
                link(V.tensor_tensor_scan(over[:, 1, :], ones[:, 0:8], over[:, 0, :], 0.0, ALU.mult, ALU.add))
                V.tensor_copy(ovf[:, 0:1], over[:, 1, 7:8])
                link(V.tensor_tensor(osel, bc(over[:, 1, :], 1, R), bc(iota[:, 1:R + 1], 2, NE), ALU.is_equal))
                link(V.tensor_tensor(osel, osel, bc(over[:, 0, :], 1, R), ALU.mult))
                for col in (slot, gate):
                    link(V.tensor_tensor(ovt, bc(col[:, :, 0:NE], 2, R), bc(osel, 1, NT), ALU.mult))
                    link(V.tensor_reduce(col[:, :, NE:NE + R], ovt, AX.X, ALU.add))
                link(V.tensor_scalar(slot[:, :, NE:NE + R], slot[:, :, NE:NE + R], -float(CAP), None, ALU.add))
                link(V.tensor_tensor(osel, osel, bc(iota[:, 0:NE], 1, R), ALU.mult))
                link(V.tensor_reduce(ovf[:, 1:1 + R], osel, AX.X, ALU.add))
                V.tensor_copy(ovi[:, :], ovf[0:1, :]).then_inc(S["route"], 1)

            def prepare(e, before_gates=None):
                V.tensor_copy(cur[:, 0, :].unsqueeze(2), slot[:, :, bass.ds(e + 1, 1)]).then_inc(S["cur"], 1)
                dve.wait_ge(S["cur"], (e + 1) * 2 + 1)
                V.tensor_scalar(disp[:, 0, :], iota, cur[:, 0, 0:1], None, ALU.is_equal)
                V.tensor_scalar(disp[:, 1, :], iota, cur[:, 0, 1:2], None, ALU.is_equal).then_inc(S["disp"], 1)
                if before_gates is not None:
                    before_gates()
                V.tensor_copy(cur[:, 1, :].unsqueeze(2), gate[:, :, bass.ds(e + 1, 1)]).then_inc(S["cur"], 1)

            def gathered(e, half):
                dve.wait_ge(S["xg_psum"], (e + 1) * 2 + (half + 1))
                gc = R_NORM + NK * 3 + 4 * half
                V.tensor_tensor(esc[:, half, :].rearrange("p (k n) -> p k n", k=4),
                                bank[3][:, :].rearrange("p (k n) -> p k n", k=4),
                                bc(sml[:, gc:gc + 4], 2, P), ALU.mult).then_inc(S["xg_tmp"], 1)

            def gathered_lower(e, par, half):
                at = (slice(None), slice(half * 4, half * 4 + 4), slice(par * P, (par + 1) * P))
                dve.wait_ge(S["xg_hi"], (e + 1) * 2 + (half + 1))
                V.tensor_tensor(hT_lo[at], esc[:, half, :].rearrange("p (k n) -> p k n", k=4),
                                hT_hi[at].bitcast(F32), ALU.subtract).then_inc(S["xg"], 1)

            def sums_lower(e):
                for half in range(2):
                    dve.wait_ge(S["y_hi"], e * 2 + (half + 1))
                    ys = slice(half * BLK, (half + 1) * BLK)
                    V.scalar_tensor_tensor(y_lo[:, ys], bank[4 + half][:, :], gslot[:, 0:1], y_hi[:, ys].bitcast(F32),
                                           ALU.mult, ALU.subtract).then_inc(S["ysb"], 1)

            def scattered(e, quarters, banks=SCATTER_BANKS):
                for i in quarters:
                    t, half = i // 2, i % 2
                    dve.wait_ge(S["scat"], e * 4 + (i + 1))
                    xs = x[:, t, half * BLK:(half + 1) * BLK]
                    V.tensor_tensor(xs, xs, bank[banks[i]][:, :], ALU.add).then_inc(S["x_ready"], 1)

            def expert(e, base, par, fresh=False, drain=False, second=False):
                def split_unit(pos):
                    if pos >= EXP_UNITS and drain:
                        return
                    u = base + pos
                    dve.wait_ge(S["w_hi"], e * EXP_UNITS + (U_MOE + pos + 1))
                    V.tensor_tensor(wlo[:, u % SPLIT, :, :], raw[:, u % RAW, :, :],
                                    whi[:, u % SPLIT, :, :].bitcast(F32), ALU.subtract).then_inc(S["w_lo"], 1)

                def hidden_lower(c):
                    dve.wait_ge(S["m_h2_hi"], e * NCH + (c + 1))
                    V.tensor_tensor(h2_lo[:, (par + c) % 2, :], bank[2][:, 0:CH],
                                    h2_hi[:, (par + c) % 2, :].bitcast(F32), ALU.subtract).then_inc(S["m_h2T"], 1)

                if second:
                    prepare(e - 1)
                    for half in range(2):
                        gathered(e - 1, half)
                        gathered_lower(e - 1, par, half)
                    for pos in range(SPLIT):
                        split_unit(pos)
                for c in range(NCH):
                    if c == 2 and not fresh:
                        sums_lower(e - 1)
                    split_unit(pos_g(c, 0, fresh) + SPLIT)
                    dve.wait_ge(S["m_silu"], e * NCH + (c + 1))
                    V.tensor_tensor(hact[:, (par + c) % 2, :], sg[:, (par + c) % 2, :],
                                    bank[(par + c) % 2][:, CH:2 * CH], ALU.mult).then_inc(S["m_hact"], 1)
                    split_unit(pos_g(c, 1, fresh) + SPLIT)
                    if c or not fresh:
                        hidden_lower(c - 1)
                    if not drain and c == TURN + 1:
                        dve.wait_ge(S["combT"], e + 1)
                        prepare(e)
                    if not drain and c in (GATHER + 2, GATHER + 3):
                        gathered_lower(e, 1 - par, c - GATHER - 2)
                    if c >= 2 or not fresh:
                        split_unit(pos_d(c - 2, drain) + SPLIT)
                    if not fresh and c in (SCATTER, SCATTER + 1):
                        scattered(e - 1, (0, 1) if c == SCATTER else (2, 3))
                    if not drain and c in (GATHER + 1, GATHER + 2):
                        gathered(e, c - GATHER - 1)
                if drain:
                    hidden_lower(NCH - 1)
                    sums_lower(e)
                    scattered(e, range(4), DRAIN_BANKS)

            prepare(-1, gates)
            split(U_MOE + 2)
            gathered(-1, 0)
            gathered_lower(-1, 0, 0)
            gathered(-1, 1)
            gathered_lower(-1, 0, 1)
            overflow()
            expert(0, U_MOE, 0, fresh=True)
            with dve.Fori(1, NE - 1, 2) as e:
                expert(e, U_MOE + EXP_UNITS, 1)
                expert(e + 1, U_MOE + 2 * EXP_UNITS, 0)
            expert(NE - 1, U_MOE + (NE - 1) * EXP_UNITS, 1, drain=True)
            dve.wait_ge(S["route"], 1)
            n_over = dve.value_load(ovi[0:1, 0:1], min_val=0, max_val=OVER_ROUNDS)
            with dve.Fori(NE, NE + OVER_ROUNDS) as e:
                with dve.If(n_over > e - NE):
                    expert(e, U_END, 0, fresh=True, drain=True, second=True)


def pack_blocks(w):
    rows, cols = w.shape
    n = -(-cols // BLK)
    out = np.zeros((n, rows // P, P, BLK), np.float32)
    for c in range(n):
        part = w[:, c * BLK:(c + 1) * BLK]
        out[c, :, :, :part.shape[1]] = part.reshape(rows // P, P, -1)
    return out.reshape(-1, P, BLK)


def pack_ffn(wg, wu, wd):
    g = wg.reshape(NK, P, NCH, CH).transpose(2, 0, 1, 3)
    u = wu.reshape(NK, P, NCH, CH).transpose(2, 0, 1, 3)
    d = wd.reshape(NCH, 2, P, 2, BLK).transpose(0, 1, 3, 2, 4).reshape(NCH, 4, P, BLK)
    return np.concatenate([np.concatenate([g, u], axis=3), d], axis=1)


def consumed():
    order = [(0, b) for b in range(8)]
    for c in range(1, NCH):
        order += [(c, b) for b in range(8)] + [(c - 1, b) for b in range(8, 12)]
    order += [(NCH - 1, b) for b in range(8, 12)]
    return np.array([o[0] for o in order]), np.array([o[1] for o in order])


def layout(inp):
    a = np.asarray
    w = a(inp["a_w_in"])[0]
    cut = np.cumsum([512, 128, 128, 128, 128, 128, 128, 24, 512, 512, 512])
    qa, kc, vc, ksl, vsl, kwn, vwn, ga, qb, kb, vb, fb = np.split(w, cut, axis=1)
    first = pack_blocks(np.concatenate([kc, vc, ksl, kwn], axis=1))
    second = pack_blocks(np.concatenate([vsl, vwn, ga, fb], axis=1))
    a_in = np.concatenate([first, second] + [pack_blocks(m) for m in (qa, qb, kb, vb)])
    cw = a(inp["c_w_in"])[0]
    fc, fb_ = consumed()
    parts = [a_in, pack_blocks(a(inp["a_w_out"])[0]),
             pack_ffn(a(inp["f_w_gate"])[0], a(inp["f_w_up"])[0], a(inp["f_w_down"])[0])[fc, fb_],
             pack_blocks(cw[:, 0:3072]), pack_blocks(a(inp["c_w_out"])[0])]
    stream = np.zeros((W_END, P, UB * BLK), np.float32)
    front = np.concatenate(parts)
    stream[0:U_MOE] = front.reshape(U_MOE, UB, P, BLK).transpose(0, 2, 1, 3).reshape(U_MOE, P, UB * BLK)
    for e in range(NE):
        blocks = pack_ffn(a(inp["m_w_gate"])[0, e], a(inp["m_w_up"])[0, e], a(inp["m_w_down"])[0, e])
        units = blocks.reshape(NCH, CHUNK_UNITS, UB, P, BLK).transpose(0, 1, 3, 2, 4).reshape(NCH, CHUNK_UNITS, P, -1)
        at = U_MOE + e * EXP_UNITS
        for i, first in enumerate((at, at + 1, at + 8)):
            stream[first:first + EXP_UNITS:CHUNK_UNITS] = units[:, i]
    small = np.zeros((P, R_END), np.float32)
    for at, name in ((R_QN, "a_q_norm"), (R_KN, "a_k_norm"), (R_FQ, "a_fox_q_norm"), (R_FK, "a_fox_k_norm"),
                     (R_ON, "c_o_norm"), (R_GB, "a_gate_bias"), (R_FB, "a_fox_f_bias")):
        v = a(inp[name])[0]
        small[:, at:at + v.shape[0]] = v[None, :]
    for i, name in enumerate(("a_norm", "f_norm", "c_norm", "m_norm")):
        small[:, R_NORM + NK * i:R_NORM + NK * (i + 1)] = a(inp[name])[0].reshape(NK, P).T
    small[:, R_BA:R_BA + GH] = a(inp["c_b_a"])[0].reshape(GH, P).T
    small[:, R_ROUTER:R_ROUTER + NK * NE] = a(inp["m_router"])[0].reshape(NK, P, NE).transpose(1, 0, 2).reshape(P, -1)
    small[:, R_A1:R_A1 + NK * 16] = cw[:, 3072:3088].reshape(NK, P, 16).transpose(1, 0, 2).reshape(P, -1)
    for v, name in enumerate(("a_pe_k", "a_pe_v")):
        small[:, R_PE + 16 * v:R_PE + 16 * (v + 1)] = a(inp[name])[0].reshape(16, P).T
    comp = np.zeros((P, 2176), np.float32)
    for v, c in enumerate("kv"):
        comp[:, 1024 * v:1024 * (v + 1)] = a(inp[f"a_cmp_{c}_w1"])[0].reshape(16, P, HD).transpose(1, 0, 2).reshape(P, -1)
        comp[0:HD, 2048 + HD * v:2048 + HD * (v + 1)] = a(inp[f"a_cmp_{c}_w2"])[0]
    return {"x": a(inp["x"])[0], "weights": stream, "constants": constants(), "masks": masks(), "small": small,
            "compress": comp, "w_a2": np.tile(a(inp["c_w_a2"])[0], (2, 1))}


ARENA = 15616
TMP = {0: 0, 2: 4, 3: 8, 5: 12}
CROSS_SPLITS = {0: 11, 3: 12}
DIAG_SPLITS = {1: 9, 4: 10, 9: 13, 13: 14}
CONST_DMAS = 2
FAR_AT = 5
SCATTER_BANKS, DRAIN_BANKS = (6, 7, 6, 7), (6, 7, 0, 1)
GLA_BANKS = (5, 6, 7, 4)
SCORE_BANKS = (0, 1, 6)


def kernel(**inputs):
    import concourse.bacc as bacc
    from concourse.bass_utils import run_bass_kernel_spmd

    nc = bacc.Bacc("TRN2", target_bir_lowering=False, num_devices=1)
    arrays = {k: np.ascontiguousarray(v) for k, v in layout(inputs).items()}
    d = {k: nc.dram_tensor("in_" + k, v.shape, mybir.dt.from_np(v.dtype), kind="ExternalInput").ap()
         for k, v in arrays.items()}
    out = nc.dram_tensor("out", (SEQ, DM), F32, kind="ExternalOutput").ap()
    trunk(nc, d["x"], d["weights"], d["constants"], d["masks"], d["small"], d["compress"], d["w_a2"], out)
    r = run_bass_kernel_spmd(nc, [{"in_" + k: v for k, v in arrays.items()}], core_ids=[0])
    return r.results[0]["out"].reshape(1, SEQ, DM)
```
